# Optimizing a Trainium2 kernel written in Bass

```python
import math
import jax
import jax.numpy as jnp
from jax import lax
import numpy as np

D_MODEL = 1024
BATCH = 1
SEQ = 128
DEPTH = 2
DEC_BATCH = 1
DEC_SEQ = 512
PAST_LEN = 128

GRID_W = 64
ROPE_BASE = 10000.0
EPS = 1e-6
Q_BLOCK = 128
H_M = 4
DK_M = 64
DV_M = 128
MLSTM_CHUNK = 64
F_BIAS = 3.0
H_A = 8
Q_RANK = 384
KV_RANK = 256
NOPE_A = 64
ROPE_A = 32
V_A = 64
H_D = 4
DK_D = 64
DV_D = 128
D_FF = 4 * D_MODEL
IN_SPLITS = (H_M * DK_M, H_M * DK_M, H_M * DV_M, H_M * DV_M, 4 * H_M,
             Q_RANK, KV_RANK, ROPE_A,
             H_D * 2 * DK_D, H_D * 2 * DK_D, H_D * DV_D,
             3 * D_MODEL)
IN_COLS = (2 * H_M * DK_M + 2 * H_M * DV_M + 4 * H_M + Q_RANK + KV_RANK + ROPE_A
           + 4 * H_D * DK_D + H_D * DV_D + 3 * D_MODEL)

kernel_name = "hybrid_mlstm_mla_diffattn_dit_step"

def _rms(x, g):
    xf = x.astype(jnp.float32)
    y = xf * lax.rsqrt(jnp.mean(xf * xf, axis=-1, keepdims=True) + EPS)
    return (y * g.astype(jnp.float32)).astype(x.dtype)

def _rev(a):
    return jnp.flip(a, axis=1)

def _axial_tables(n_tokens, dim):
    rows = n_tokens // GRID_W
    row = jnp.repeat(jnp.arange(rows, dtype=jnp.float32), GRID_W)
    col = jnp.tile(jnp.arange(GRID_W, dtype=jnp.float32), rows)
    quarter = dim // 4
    inv = ROPE_BASE ** (-jnp.arange(quarter, dtype=jnp.float32) / quarter)
    ang = jnp.concatenate([row[:, None] * inv, col[:, None] * inv], axis=-1)
    return jnp.cos(ang), jnp.sin(ang)

def _rope(x, cos, sin):
    half = x.shape[-1] // 2
    shape = (x.shape[1],) + (1,) * (x.ndim - 3) + (half,)
    c = cos.reshape(shape).astype(x.dtype)
    s = sin.reshape(shape).astype(x.dtype)
    x1, x2 = x[..., :half], x[..., half:]
    return jnp.concatenate([x1 * c - x2 * s, x1 * s + x2 * c], axis=-1)

def _attend(q, k, v, q2=None, k2=None, lam=None):
    B, S, H, d = q.shape
    nb = S // Q_BLOCK
    scale = d ** -0.5

    def blocks(a):
        return jnp.swapaxes(a.reshape((B, nb, Q_BLOCK) + a.shape[2:]), 0, 1)

    def probs(qb, kk):
        s = jnp.einsum("bqhd,bkhd->bhqk", qb, kk).astype(jnp.float32) * scale
        return jax.nn.softmax(s, axis=-1)

    def one(qbs):
        p = probs(qbs[0], k)
        if q2 is not None:
            p = p - lam * probs(qbs[1], k2)
        return jnp.einsum("bhqk,bkhe->bqhe", p.astype(v.dtype), v)

    qs = (blocks(q),) if q2 is None else (blocks(q), blocks(q2))
    o = lax.map(one, qs)
    return jnp.swapaxes(o, 0, 1).reshape(B, S, H, v.shape[-1])

def _mlstm_chunk(carry, xs):
    C, n, m = carry
    q, k, v, log_i, log_f = xs
    L = q.shape[1]
    b = jnp.cumsum(log_f, axis=1).transpose(0, 2, 1)
    li = log_i.transpose(0, 2, 1)
    causal = jnp.tril(jnp.ones((L, L), dtype=bool))
    dmat = jnp.where(causal, b[..., :, None] - b[..., None, :] + li[..., None, :], -jnp.inf)
    inter = b + m[..., None]
    m_t = jnp.maximum(inter, jnp.max(dmat, axis=-1))
    w_inter = jnp.exp(inter - m_t)
    a = jnp.exp(dmat - m_t[..., None]) * jnp.einsum("blhd,bshd->bhls", q, k)
    num = w_inter[..., None] * jnp.einsum("blhd,bhde->bhle", q, C) + jnp.einsum("bhls,bshe->bhle", a, v)
    den = w_inter * jnp.einsum("blhd,bhd->bhl", q, n) + jnp.sum(a, axis=-1)
    h = num / jnp.maximum(jnp.abs(den), jnp.exp(-m_t))[..., None]
    m_new = m_t[..., -1]
    w_old = jnp.exp(b[..., -1] + m - m_new)
    w_s = jnp.exp(b[..., -1:] - b + li - m_new[..., None])
    C_new = w_old[..., None, None] * C + jnp.einsum("bhs,bshd,bshe->bhde", w_s, k, v)
    n_new = w_old[..., None] * n + jnp.einsum("bhs,bshd->bhd", w_s, k)
    return (C_new, n_new, m_new), h.transpose(0, 2, 1, 3)

def _mlstm_scan(q, k, v, log_i, log_f, state):
    B, S = q.shape[:2]
    nc = S // MLSTM_CHUNK

    def chunks(a):
        return jnp.swapaxes(a.reshape((B, nc, MLSTM_CHUNK) + a.shape[2:]), 0, 1)

    state, h = lax.scan(_mlstm_chunk, state,
                        (chunks(q), chunks(k), chunks(v), chunks(log_i), chunks(log_f)))
    return jnp.swapaxes(h, 0, 1).reshape(B, S, H_M, DV_M), state

def _layer(x, cond, lp, lam_init, ctx):
    B, N, _ = x.shape
    dt = x.dtype
    f32 = jnp.float32
    latent = ctx is not None
    mod = jax.nn.silu(cond) @ lp["w_mod"] + lp["b_mod"]
    sh1, sc1, g1, sh2, sc2, g2 = jnp.split(mod[:, None, :], 6, axis=-1)
    h = _rms(x, lp["norm1_g"]) * (1.0 + sc1) + sh1
    z = h @ lp["w_in"]
    (mq, mk, mv, mo, mg, acq, ackv, akr, dq, dk, dv, gate_pre) = jnp.split(
        z, np.cumsum(IN_SPLITS)[:-1].tolist(), axis=-1)
    if latent:
        cos_a, sin_a = _axial_tables(N, ROPE_A)
        cos_d, sin_d = _axial_tables(N, DK_D)

    if latent:
        C0, n0, m0 = ctx[4].astype(f32), ctx[5].astype(f32), ctx[6].astype(f32)
    else:
        C0 = jnp.zeros((B, 2, H_M, DK_M, DV_M), f32)
        n0 = jnp.zeros((B, 2, H_M, DK_M), f32)
        m0 = jnp.zeros((B, 2, H_M), f32)
    q_m = mq.reshape(B, N, H_M, DK_M).astype(f32) * DK_M ** -0.5
    k_m = mk.reshape(B, N, H_M, DK_M).astype(f32)
    v_m = mv.reshape(B, N, H_M, DV_M).astype(f32)
    gp = (mg + lp["mlstm_gate_b"]).astype(f32).reshape(B, N, 2, 2, H_M)
    log_i = gp[:, :, 0]
    log_f = jax.nn.log_sigmoid(gp[:, :, 1])
    h_f, (Cf, nf, mf) = _mlstm_scan(q_m, k_m, v_m, log_i[:, :, 0], log_f[:, :, 0],
                                    (C0[:, 0], n0[:, 0], m0[:, 0]))
    h_b, (Cb, nb, mb) = _mlstm_scan(_rev(q_m), _rev(k_m), _rev(v_m), _rev(log_i[:, :, 1]),
                                    _rev(log_f[:, :, 1]), (C0[:, 1], n0[:, 1], m0[:, 1]))
    h_m = (h_f + _rev(h_b)).astype(dt)
    o_m = _rms(h_m, lp["mlstm_norm_g"].reshape(H_M, DV_M)).reshape(B, N, H_M * DV_M) * jax.nn.sigmoid(mo)

    q_a = (_rms(acq, lp["mla_q_norm_g"]) @ lp["mla_w_q_up"]).reshape(B, N, H_A, NOPE_A + ROPE_A)
    q_nope, q_rope = q_a[..., :NOPE_A], q_a[..., NOPE_A:]
    ckv = _rms(ackv, lp["mla_kv_norm_g"])
    if latent:
        q_rope = _rope(q_rope, cos_a, sin_a)
        ckv_all = jnp.concatenate([ctx[0], ckv], axis=1)
        kr_all = jnp.concatenate([ctx[1], _rope(akr[:, :, None, :], cos_a, sin_a)[:, :, 0]], axis=1)
    else:
        ckv_all, kr_all = ckv, akr
    T = ckv_all.shape[1]
    kv = (ckv_all @ lp["mla_w_kv_up"]).reshape(B, T, H_A, NOPE_A + V_A)
    k_a = jnp.concatenate([kv[..., :NOPE_A],
                           jnp.broadcast_to(kr_all[:, :, None, :], (B, T, H_A, ROPE_A))], axis=-1)
    o_a = _attend(jnp.concatenate([q_nope, q_rope], axis=-1), k_a, kv[..., NOPE_A:]).reshape(B, N, H_A * V_A)

    q_d = dq.reshape(B, N, H_D, 2, DK_D)
    k_d = dk.reshape(B, N, H_D, 2, DK_D)
    v_d = dv.reshape(B, N, H_D, DV_D)
    if latent:
        q_d = _rope(q_d, cos_d, sin_d)
        k_all = jnp.concatenate([ctx[2].reshape(B, ctx[2].shape[1], H_D, 2, DK_D),
                                 _rope(k_d, cos_d, sin_d)], axis=1)
        v_all = jnp.concatenate([ctx[3], v_d], axis=1)
    else:
        k_all, v_all = k_d, v_d
    lam_v = lp["diff_lambda"].astype(f32)
    lam = jnp.exp(jnp.sum(lam_v[0] * lam_v[1])) - jnp.exp(jnp.sum(lam_v[2] * lam_v[3])) + lam_init
    o_d = _attend(q_d[..., 0, :], k_all[..., 0, :], v_all, q_d[..., 1, :], k_all[..., 1, :], lam)
    o_d = (_rms(o_d, lp["diff_norm_g"].reshape(H_D, DV_D)) * (1.0 - lam_init)).reshape(B, N, H_D * DV_D)

    g_m, g_a, g_d = jnp.split(jax.nn.sigmoid(gate_pre), 3, axis=-1)
    y = (g_m * (o_m @ lp["w_br_mlstm"]) + g_a * (o_a @ lp["w_br_mla"])
         + g_d * (o_d @ lp["w_br_diff"]))
    x = x + g1 * (y @ lp["w_out"])

    h2 = _rms(x, lp["norm2_g"]) * (1.0 + sc2) + sh2
    x = x + g2 * (jnp.square(jax.nn.relu(h2 @ lp["w_ff1"])) @ lp["w_ff2"])
    if latent:
        return x, None
    new_ctx = (ckv, akr, k_d.reshape(B, N, H_D, 2 * DK_D), v_d,
               jnp.stack([Cf, Cb], axis=1).astype(dt),
               jnp.stack([nf, nb], axis=1).astype(dt),
               jnp.stack([mf, mb], axis=1).astype(dt))
    return x, new_ctx

def setup_inputs(seed: int = 0) -> dict:
    key = jax.random.key(seed)
    ks = iter(jax.random.split(key, 40))

    def nrm(shape, scale=1.0):
        return scale * jax.random.normal(next(ks), shape, jnp.float32)

    def gain(shape):
        return 1.0 + 0.02 * nrm(shape)

    return {
        "x_prompt": nrm((BATCH, SEQ, D_MODEL)),
        "x_sample": nrm((DEC_BATCH, DEC_SEQ, D_MODEL)),
        "c": nrm((DEC_BATCH, D_MODEL)),
        "cache_mla_ckv": nrm((DEC_BATCH, DEPTH, PAST_LEN, KV_RANK)),
        "cache_mla_krope": nrm((DEC_BATCH, DEPTH, PAST_LEN, ROPE_A)),
        "cache_diff_k": nrm((DEC_BATCH, DEPTH, PAST_LEN, H_D, 2 * DK_D)),
        "cache_diff_v": nrm((DEC_BATCH, DEPTH, PAST_LEN, H_D, DV_D)),
        "state_mlstm_C": nrm((DEC_BATCH, DEPTH, 2, H_M, DK_M, DV_M), 0.5),
        "state_mlstm_n": nrm((DEC_BATCH, DEPTH, 2, H_M, DK_M), 0.5),
        "state_mlstm_m": nrm((DEC_BATCH, DEPTH, 2, H_M), 0.5),
        "c_ctx": nrm((D_MODEL,)),
        "w_mod": nrm((DEPTH, D_MODEL, 6 * D_MODEL), 0.5 * D_MODEL ** -0.5),
        "b_mod": nrm((DEPTH, 6 * D_MODEL), 0.02),
        "norm1_g": gain((DEPTH, D_MODEL)),
        "w_in": nrm((DEPTH, D_MODEL, IN_COLS), D_MODEL ** -0.5),
        "mlstm_gate_b": jnp.concatenate([nrm((DEPTH, 2 * H_M), 0.1),
                                         F_BIAS + nrm((DEPTH, 2 * H_M), 0.1)], axis=-1),
        "mlstm_norm_g": gain((DEPTH, H_M * DV_M)),
        "mla_q_norm_g": gain((DEPTH, Q_RANK)),
        "mla_w_q_up": nrm((DEPTH, Q_RANK, H_A * (NOPE_A + ROPE_A)), Q_RANK ** -0.5),
        "mla_kv_norm_g": gain((DEPTH, KV_RANK)),
        "mla_w_kv_up": nrm((DEPTH, KV_RANK, H_A * (NOPE_A + V_A)), KV_RANK ** -0.5),
        "diff_lambda": nrm((DEPTH, 4, DK_D), 0.1),
        "diff_norm_g": gain((DEPTH, H_D * DV_D)),
        "w_br_mlstm": nrm((DEPTH, H_M * DV_M, D_MODEL), (H_M * DV_M) ** -0.5),
        "w_br_mla": nrm((DEPTH, H_A * V_A, D_MODEL), (H_A * V_A) ** -0.5),
        "w_br_diff": nrm((DEPTH, H_D * DV_D, D_MODEL), (H_D * DV_D) ** -0.5),
        "w_out": nrm((DEPTH, D_MODEL, D_MODEL), D_MODEL ** -0.5),
        "norm2_g": gain((DEPTH, D_MODEL)),
        "w_ff1": nrm((DEPTH, D_MODEL, D_FF), D_MODEL ** -0.5),
        "w_ff2": nrm((DEPTH, D_FF, D_MODEL), D_FF ** -0.5),
        "final_norm_g": gain((D_MODEL,)),
    }

def reference(x_prompt, x_sample, c, cache_mla_ckv, cache_mla_krope, cache_diff_k, cache_diff_v,
              state_mlstm_C, state_mlstm_n, state_mlstm_m, c_ctx, w_mod, b_mod, norm1_g, w_in,
              mlstm_gate_b, mlstm_norm_g, mla_q_norm_g, mla_w_q_up, mla_kv_norm_g, mla_w_kv_up,
              diff_lambda, diff_norm_g, w_br_mlstm, w_br_mla, w_br_diff, w_out, norm2_g, w_ff1, w_ff2,
              final_norm_g):
    y_p = x_prompt
    y_s = x_sample
    cond_ctx = c_ctx[None, :]
    st = ([], [], [], [], [], [], [])
    for l in range(DEPTH):
        lp = {
            "w_mod": w_mod[l], "b_mod": b_mod[l], "norm1_g": norm1_g[l], "w_in": w_in[l],
            "mlstm_gate_b": mlstm_gate_b[l], "mlstm_norm_g": mlstm_norm_g[l],
            "mla_q_norm_g": mla_q_norm_g[l], "mla_w_q_up": mla_w_q_up[l],
            "mla_kv_norm_g": mla_kv_norm_g[l], "mla_w_kv_up": mla_w_kv_up[l],
            "diff_lambda": diff_lambda[l], "diff_norm_g": diff_norm_g[l],
            "w_br_mlstm": w_br_mlstm[l], "w_br_mla": w_br_mla[l], "w_br_diff": w_br_diff[l],
            "w_out": w_out[l], "norm2_g": norm2_g[l], "w_ff1": w_ff1[l], "w_ff2": w_ff2[l],
        }
        lam_init = 0.8 - 0.6 * math.exp(-0.3 * l)
        y_p, ctx_new = _layer(y_p, cond_ctx, lp, lam_init, None)
        for lst, a in zip(st, ctx_new):
            lst.append(a)
        ctx_l = (cache_mla_ckv[:, l], cache_mla_krope[:, l], cache_diff_k[:, l], cache_diff_v[:, l],
                 state_mlstm_C[:, l], state_mlstm_n[:, l], state_mlstm_m[:, l])
        y_s, _ = _layer(y_s, c, lp, lam_init, ctx_l)
    y_prompt = _rms(y_p, final_norm_g)
    y_sample = _rms(y_s, final_norm_g)
    new_mla_ckv = jnp.stack(st[0], axis=1)
    new_mla_krope = jnp.stack(st[1], axis=1)
    new_diff_k = jnp.stack(st[2], axis=1)
    new_diff_v = jnp.stack(st[3], axis=1)
    new_mlstm_C = jnp.stack(st[4], axis=1)
    new_mlstm_n = jnp.stack(st[5], axis=1)
    new_mlstm_m = jnp.stack(st[6], axis=1)
    return (y_prompt, y_sample, new_mla_ckv, new_mla_krope, new_diff_k, new_diff_v,
            new_mlstm_C, new_mlstm_n, new_mlstm_m)


_drawn_inputs = setup_inputs


def setup_inputs(seed=0):
    import zlib

    import numpy as np

    out = dict(_drawn_inputs(seed))
    spreads = {}
    factors = {'cache_mla_ckv': 7.736,
     'cache_mla_krope': 8.0,
     'state_mlstm_C': 8.0,
     'state_mlstm_n': 8.0,
     'state_mlstm_m': 8.0,
     'mlstm_norm_g': 36.589,
     'mla_q_norm_g': 8.0,
     'mla_kv_norm_g': 8.344,
     'diff_lambda': 8.0,
     'diff_norm_g': 21.931,
     'norm2_g': 4.26,
     'final_norm_g': 24.562}
    for name, (base, spread) in spreads.items():
        noise = np.random.default_rng([zlib.crc32(name.encode()), seed]).standard_normal(out[name].shape)
        drawn = base * np.exp(spread * noise) if base else spread * noise
        out[name] = jnp.asarray(drawn.astype(out[name].dtype))
    for name, factor in factors.items():
        out[name] = (out[name] * factor).astype(out[name].dtype)
    return out
```

```python
import math
from contextlib import ExitStack

import numpy as np

import concourse.bass as bass
from concourse import mybir

D = 1024
CTX, LAT, PAST = 128, 512, 128
DEPTH = 2
T = CTX + LAT
TK = T + PAST
HALF = T // 2
P = 128
KD = D // P
H_M, DK_M, DV_M = 4, 64, 128
H_A, NOPE, ROPE, V_A = 8, 64, 32, 64
Q_RANK, KV_RANK = 384, 256
KQ, KKV = Q_RANK // P, KV_RANK // P
H_D, DK_D, DV_D = 4, 64, 128
D_FF = 4 * D
EPS = 1e-6
GRID_W = 64
ROPE_BASE = 10000.0
UNITS = 2 * H_M
ROWS = 32 + H_M
BLK = 1024

MOD_BLOCKS = 6 * D * KD // BLK
FF_CHUNKS = 4
STAGES = [("mv", 4), ("mq", 2), ("mk", 2), ("mo", 4), ("mg", 1), ("merge_m", 12),
          ("acq", 3), ("ckv", 2), ("qup", 3), ("kr", 1), ("kvn", 1), ("kvv", 1), ("merge_a", 12),
          ("dv", 4), ("dq", 4), ("dk", 4), ("merge_d", 12), ("wout", 8), ("ff", 64)]
FIRST_BLOCK, DENSE = {}, 0
for _name, _n in STAGES:
    FIRST_BLOCK[_name] = DENSE
    DENSE += _n
BLOCKS = MOD_BLOCKS + DENSE
RAW, SPLIT = 4, 2
assert BLOCKS % RAW == 0 and MOD_BLOCKS % RAW == 0 and DENSE % SPLIT == 0

USE_STAGES = [("norm1", 1), ("mv", 2), ("mq", 2), ("mk", 2), ("mo", 4), ("mg", 1),
              ("ms", UNITS * 5), ("mr", UNITS), ("mn", H_M), ("merge_m", 16),
              ("acq", KQ), ("qn", 1), ("ckv", KKV), ("kn", 1), ("qup", 8), ("kr", 1), ("kvn", 4), ("kvv", 3),
              ("ma", H_A * 5), ("merge_a", 16),
              ("dv", 2), ("dq", 4), ("dk", 4), ("da", H_D * 10), ("dn", H_D), ("merge_d", 16),
              ("wout", 8), ("norm2", 1), ("ff", 64)]
FIRST_USE, USES = {}, 0
for _name, _n in USE_STAGES:
    FIRST_USE[_name] = USES
    USES += _n
assert USES % 2 == 0

SPLIT_STAGES = [("h1", 8), ("om", 4), ("q", KQ), ("kv", KKV), ("oa", 4), ("od", 4), ("y", 8), ("h2", 8), ("ff", 32)]
FIRST_SPLIT, SPLITS = {}, 0
for _name, _n in SPLIT_STAGES:
    FIRST_SPLIT[_name] = SPLITS
    SPLITS += _n
SQ_STAGES = [("norm1", 8), ("mn", 4), ("qn", KQ), ("kn", KKV), ("dn", 4), ("norm2", 8)]
FIRST_SQ, SQUARES = {}, 0
for _name, _n in SQ_STAGES:
    FIRST_SQ[_name] = SQUARES
    SQUARES += _n
FIRST_SQ_USED, SQ_USED = {}, 0
for _name, _n in SQ_STAGES:
    FIRST_SQ_USED[FIRST_SQ[_name]] = SQ_USED
    SQ_USED += (_n - 1) * (_n > 1) if _name not in ("mn", "dn") else 0
NORMS = {"norm1": 0, "mn": 1, "qn": 5, "kn": 6, "dn": 7, "norm2": 11}
N_NORMS = 12
MOD_CHUNKS = 6 * D // 512

def _columns(parts):
    at, out = 0, {}
    for name, n in parts:
        out[name] = (at, at + n)
        at += n
    return out, at


SMALL, SMALL_W = _columns([("bmod", 48), ("n1", 8), ("n2", 8), ("ng_m", 4), ("ng_q", KQ), ("ng_kv", KKV),
                           ("ng_d", 4), ("gb", 2), ("m0row", 1), ("m0", UNITS), ("lam", 256), ("lam_init", 2),
                           ("fin", 8), ("n0", 4 * ROWS), ("C0", 4 * DV_M)])
CONST, CONST_W = _columns([("cos_d", LAT), ("sin_d", LAT), ("cos_a", LAT), ("sin_a", LAT), ("mask_f", P),
                           ("mask_b", P), ("ident", P), ("ones", P), ("den_sel", UNITS * ROWS),
                           ("row_sel", UNITS * P), ("eps", 1)])
PAST_C, PAST_W = _columns([("ckv", KKV * PAST), ("kr", PAST), ("dk", 4 * PAST), ("dv", H_D * DV_D)])
NEG = -1e30


def unit(u):
    d, h = divmod(u, H_M)
    return d, h, 64 * (h % 2), h // 2, 32 * d + h


def trunk(nc, xT, condT, consts, small_d, past_d, w_d, yT, o_ckv, o_kr, o_dk, o_dv, o_C, o_n, o_m):
    f32, f32r = mybir.dt.float32, mybir.dt.float32r
    ALU, ACT, AX = mybir.AluOpType, mybir.ActivationFunctionType, mybir.AxisListType
    ctx = ExitStack()
    with ctx:
        base = [(nc.sbuf_base + 63) // 64 * 64]

        def at(name, shape, offset, dt=f32):
            return nc.alloc_sbuf_tensor_at(name, shape, dt, offset=offset)

        def sb(name, shape, dt=f32):
            off = base[0]
            base[0] += (int(np.prod(shape[1:])) * 4 + 63) // 64 * 64
            return at(name, shape, off, dt)

        def sem(name):
            return ctx.enter_context(nc.semaphore(name))

        x = sb("x", [P, KD, T])
        act_hi, act_lo = sb("act_hi", [P, KD, T], f32r), sb("act_lo", [P, KD, T], f32r)
        raw = sb("raw", [P, RAW, BLK])
        w_hi, w_lo = sb("w_hi", [P, SPLIT, BLK], f32r), sb("w_lo", [P, SPLIT, BLK], f32r)
        y_at = base[0]
        y = sb("y", [P, KD, T])
        num_sb = at("num_sb", [P, UNITS, T], y_at)
        cst = sb("cst", [P, CONST_W])
        small = sb("small", [P, SMALL_W])
        cond = sb("cond", [P, KD, 2])
        mod = sb("mod", [P, 48, 2])
        scale1, scale2 = sb("scale1", [P, KD, 2]), sb("scale2", [P, KD, 2])
        cols = sb("cols", [P, 32])
        mod_row = sb("mod_row", [2, 2, 512])
        rs = sb("rs", [P, T])
        sq = sb("sq", [P, 2, T])
        t1, t2 = sb("t1", [P, T]), sq[:, 1, :]
        stage = sb("stage", [P, 2, T])
        A0 = base[0]
        qm, km = at("qm", [P, 2, T], A0), at("km", [P, 2, T], A0 + 5120)
        vm = at("vm", [P, 5, 512], A0 + 10240)
        om_hi, om_lo = at("om_hi", [P, 4, T], A0, f32r), at("om_lo", [P, 4, T], A0 + 10240, f32r)
        mo_th = at("mo_th", [P, 4, T], A0 + 20480)
        ebuf, abuf = at("ebuf", [P, 2, 512], A0 + 30720), at("abuf", [P, 2, 512], A0 + 34816)
        nMbc, qw = at("nMbc", [P, T], A0 + 38912), at("qw", [P, 512], A0 + 41472)
        rows = [at(f"row{i}", [ROWS, T], A0 + 43520 + 2560 * i) for i in range(6)]
        acol = at("acol", [P, 5, ROWS], A0 + 58880)
        ktok, kw = at("ktok", [P, 256], A0 + 59648), at("kw", [P, UNITS, DK_M], A0 + 60672)
        c_new, n_new = at("c_new", [DK_M, UNITS, DV_M], A0 + 62720), at("n_new", [DK_M, UNITS], A0 + 66816)
        q_a, o_a = at("q_a", [96, H_A, T], A0), at("o_a", [P, 4, T], A0)
        k_a = at("k_a", [96, H_A, TK], A0 + 20480)
        qn_hi, qn_lo = at("qn_hi", [P, KQ, T], A0 + 20480, f32r), at("qn_lo", [P, KQ, T], A0 + 28160, f32r)
        acq = at("acq", [P, KQ, T], A0 + 35840)
        oa_hi, oa_lo = at("oa_hi", [P, 4, T], A0 + 20480, f32r), at("oa_lo", [P, 4, T], A0 + 30720, f32r)
        v_a, ckv = at("v_a", [P, 6, 512], A0 + 45056), at("ckv", [P, KKV, TK], A0 + 45056)
        ckv_hi, ckv_lo = at("ckv_hi", [P, KKV, TK], A0 + 57344, f32r), at("ckv_lo", [P, KKV, TK], A0 + 63488, f32r)
        prob_a = at("prob_a", [P, 2, T], A0 + 57344)
        probT_a = at("probT_a", [P, 2, 5, P], A0 + 62464)
        q_d, k_d = at("q_d", [P, 4, T], A0), at("k_d", [P, 4, TK], A0 + 10240)
        v_d = at("v_d", [P, 6, 512], A0 + 22528)
        prob_d = at("prob_d", [P, 4, T], A0 + 34816)
        probT_d = at("probT_d", [P, 2, 5, P], A0 + 45056)
        od_hi, od_lo = at("od_hi", [P, 4, T], A0 + 10240, f32r), at("od_lo", [P, 4, T], A0 + 20480, f32r)
        ff_hi, ff_lo = at("ff_hi", [P, 8, T], A0, f32r), at("ff_lo", [P, 8, T], A0 + 20480, f32r)

        big = [ctx.enter_context(nc.psum_tensor(f"big{b}", [P, 2, 512], f32)) for b in range(2)]
        two = ctx.enter_context(nc.psum_tensor("two", [P, 2, 512], f32))
        one = [ctx.enter_context(nc.psum_tensor(f"one{b}", [P, 512], f32)) for b in range(2)]

        def c_(name, rows_=slice(0, P)):
            return cst[rows_, CONST[name][0]:CONST[name][1]]

        def s_(name, rows_=slice(0, P)):
            return small[rows_, SMALL[name][0]:SMALL[name][1]]

        ones, ident = c_("ones"), c_("ident")
        eps = c_("eps")
        den_sel = c_("den_sel").rearrange("p (u r) -> p u r", r=ROWS)
        row_sel = c_("row_sel", slice(0, ROWS)).rearrange("p (u c) -> p u c", c=P)
        n0 = s_("n0").rearrange("p (a r) -> p a r", r=ROWS)
        C0 = s_("C0").rearrange("p (a e) -> p a e", e=DV_M)
        g_half, g_diff, neg_lam = cols[:, 0:4], cols[:, 4:8], cols[:, 8:9]
        lam_tmp = cols[:, 9:12]
        neg_max, row_sum = cols[:, 12:16], cols[:, 16:20]

        raw_loaded = [sem(f"raw_loaded{i}") for i in range(RAW)]
        mod_block_used = sem("mod_block_used")
        split_ready, block_used = sem("split_ready"), sem("block_used")
        ready, free = [sem("ready_a"), sem("ready_b")], [sem("free_a"), sem("free_b")]
        x_loaded, cst_loaded, small_loaded = sem("x_loaded"), sem("cst_loaded"), sem("small_loaded")
        layer_open, started = sem("layer_open"), sem("started")
        cond_done = sem("cond_done")
        row_ready, row_copied, row_free = sem("row_ready"), sem("row_copied"), sem("row_free")
        mod_done = sem("mod_done")
        sq_ready, sq_used = sem("sq_ready"), sem("sq_used")
        rs_ready, rs_used = sem("rs_ready"), sem("rs_used")
        whole, hi_done, lo_done = sem("whole"), sem("hi_done"), sem("lo_done")
        src_ready = sem("src_ready")
        vm_ready, qk_ready, mo_ready = sem("vm_ready"), sem("qk_ready"), sem("mo_ready")
        gate_rows, soft_rows, rows_ready, expm_ready = sem("gate_rows"), sem("soft_rows"), sem("rows_ready"), sem("expm_ready")
        colsT_ready, colsT_copied = sem("colsT_ready"), sem("colsT_copied")
        bc_ready, bc_copied, w_inter_ready, qw_ready = sem("bc_ready"), sem("bc_copied"), sem("w_inter_ready"), sem("qw_ready")
        arg_ready, e_ready, a_ready, a_used = sem("arg_ready"), sem("e_ready"), sem("a_ready"), sem("a_used")
        num_ready, num_copied = sem("num_ready"), sem("num_copied")
        kw_ready, state_ready, state_copied = sem("kw_ready"), sem("state_ready"), sem("state_copied")
        rden_ready = sem("rden_ready")
        gate_ready, y_done = sem("gate_ready"), sem("y_done")
        past_loaded = sem("past_loaded")
        raw_kept, roped = sem("raw_kept"), sem("roped")
        kv_norm_done, k_rope_done, kn_copied = sem("kv_norm_done"), sem("k_rope_done"), sem("kn_copied")
        qnope_copied, v_copied = sem("qnope_copied"), sem("v_copied")
        maxed, exped, p_ready = sem("maxed"), sem("exped"), sem("p_ready")
        pT_ready, pT_copied, o_ready, o_copied = sem("pT_ready"), sem("pT_copied"), sem("o_ready"), sem("o_copied")
        relu_ready, relu_used = sem("relu_ready"), sem("relu_used")
        x_updated, y_final = sem("x_updated"), sem("y_final")
        stored, state_stored, ckv_stored = sem("stored"), sem("state_stored"), sem("ckv_stored")
        kr_stored, diff_stored = sem("kr_stored"), sem("diff_stored")
        lam_sums, lam_exps = sem("lam_sums"), sem("lam_exps")

        def buf(i):
            return big[i % 2], i % 2, i // 2

        def wait_free(pe, l, i, more=0):
            pe.wait_ge(free[i % 2], l * (USES // 2) + more + i // 2 + 1)

        def wait_ready(e, l, i, more=0):
            e.wait_ge(ready[i % 2], l * (USES // 2) + more + i // 2 + 1)

        def halves(t, n=HALF):
            return t[:, :, 0:n]

        def two_parts(ap, n=HALF):
            return ap.rearrange("p (a t) -> p a t", t=n)

        PARTS = [(0, 0, 0, CTX), (1, 0, CTX, HALF), (1, 1, 0, HALF)]
        GROUPS = [(0, 0, CTX), (1, CTX, T)]
        ATT = [(h, t) for h in range(H_A) for t in range(5)]
        LATE = 4

        def keys(t):
            return (0, CTX) if t == LATE else (CTX, TK)

        def queries(t):
            return (0, CTX) if t == LATE else (CTX + P * t, CTX + P * t + P)

        block = ctx.enter_context(nc.Block())

        @block.sync
        def _(sp):
            sp.dma_start(x[:, :, :], xT).then_inc(x_loaded, 16)
            sp.wait_ge(started, 1)
            with sp.Fori(0, DEPTH) as l:
                for j in range(RAW):
                    sp.wait_ge(split_ready, l * DENSE + j + 1)
                    sp.dma_start(raw[:, j, :], w_d[l, j]).then_inc(raw_loaded[j], 16)
                with sp.Fori(1, MOD_BLOCKS // RAW) as i:
                    for j in range(RAW):
                        sp.wait_ge(mod_block_used, l * MOD_BLOCKS + i * RAW + (j - RAW + 1))
                        sp.dma_start(raw[:, j, :], w_d[l, i * RAW + j]).then_inc(raw_loaded[j], 16)
                for j in range(RAW):
                    sp.wait_ge(mod_block_used, l * MOD_BLOCKS + MOD_BLOCKS - RAW + j + 1)
                    sp.dma_start(raw[:, j, :], w_d[l, MOD_BLOCKS + j]).then_inc(raw_loaded[j], 16)
                with sp.Fori(1, DENSE // RAW) as i:
                    for j in range(RAW):
                        sp.wait_ge(split_ready, l * DENSE + i * RAW + (j + 1))
                        sp.dma_start(raw[:, j, :], w_d[l, MOD_BLOCKS + i * RAW + j]).then_inc(raw_loaded[j], 16)
            sp.wait_ge(y_final, KD)
            sp.dma_start(yT, x[:, :, :]).then_inc(stored, 16)
            sp.wait_ge(stored, 16)

        @block.gpsimd
        def _(pool):
            pool.wait_ge(cst_loaded, 32)
            with pool.Fori(0, DEPTH) as l:
                with pool.Fori(0, DENSE // RAW) as i:
                    for j in range(RAW):
                        s = j % SPLIT
                        pool.wait_ge(raw_loaded[j], l * (16 * BLOCKS // RAW) + i * 16 + 16 * (MOD_BLOCKS // RAW + 1))
                        pool.wait_ge(block_used, l * DENSE + i * RAW + (j + 1))
                        nc.gpsimd.tensor_tensor(w_hi[:, s, :], raw[:, j, :], ones[:, 0:1].to_broadcast([P, BLK]),
                                                ALU.mult)
                        pool.drain()
                        nc.gpsimd.tensor_tensor(w_lo[:, s, :], raw[:, j, :], w_hi[:, s, :].bitcast(f32),
                                                ALU.subtract).then_inc(split_ready, 1)

        @block.tensor
        def _(pe):
            mm = nc.tensor.matmul

            def block_start(l, b, more=0):
                pe.wait_ge(split_ready, l * DENSE + more + (b + 1 + RAW))

            def project(l, first_use, first_block, tiles, nk, hi, lo, n=HALF, arrived=None, more_b=0, more_u=0):
                for p in range(tiles * nk):
                    m, k = divmod(p, nk)
                    b, q = divmod(p, 8)
                    slot, col = (first_block + b) % SPLIT, P * q
                    if q == 0:
                        block_start(l, first_block + b, more_b)
                    t, _, _ = buf(first_use + m)
                    if k == 0:
                        wait_free(pe, l, first_use + m, more_u)
                    if arrived is not None and m == 0:
                        pe.wait_ge(lo_done, arrived(k))
                    for h in range(2):
                        ps = t[:, h, 0:n]
                        wh, wl = w_hi[:, slot, col:col + P], w_lo[:, slot, col:col + P]
                        ah, al = hi[:, k, h * n:h * n + n], lo[:, k, h * n:h * n + n]
                        first = mm(ps, wh, ah, start=k == 0, stop=False)
                        if q == 0 and h == 0:
                            first.then_inc(block_used, 1)
                        mm(ps, wh, al, start=False, stop=False)
                        last = mm(ps, wl, ah, start=False, stop=k == nk - 1)
                    if k == nk - 1:
                        last.then_inc(ready[(first_use + m) % 2], 1)

            def project_tokens(l, first_use, first_block, arrived=None):
                wait_free(pe, l, first_use)
                wait_free(pe, l, first_use + 1)
                outs = [big[0][:, 0, :], big[0][:, 1, :], big[1][:, 0, :], big[1][:, 1, :], two[:, 0, :]]
                for b in range(4):
                    block_start(l, first_block + b)
                    slot = (first_block + b) % SPLIT
                    if arrived is not None:
                        pe.wait_ge(lo_done, arrived(2 * b + 1))
                    for t in range(5):
                        for kk in range(2):
                            k = 2 * b + kk
                            wh, wl = w_hi[:, slot, 512 * kk:512 * kk + 512], w_lo[:, slot, 512 * kk:512 * kk + 512]
                            ah, al = act_hi[:, k, P * t:P * t + P], act_lo[:, k, P * t:P * t + P]
                            first = mm(outs[t], ah, wh, start=k == 0, stop=False)
                            if t == 0 and kk == 0:
                                first.then_inc(block_used, 1)
                            mm(outs[t], al, wh, start=False, stop=False)
                            last = mm(outs[t], ah, wl, start=False, stop=k == KD - 1)
                        if b == 3 and t in (1, 4):
                            last.then_inc(ready[t // 4], 1)

            def sums(l, use, first_sq, n, per_layer=SQUARES, off=0):
                wait_free(pe, l, use, off)
                t, b, _ = buf(use)
                for k in range(n):
                    pe.wait_ge(sq_ready, l * SQUARES + first_sq + k + 1)
                    for h in range(2):
                        last = mm(t[:, h, 0:HALF], ones, sq[:, k % 2, h * HALF:(h + 1) * HALF],
                                  start=k == 0, stop=k == n - 1)
                    last.then_inc(ready[b] if k == n - 1 else sq_used, 1)

            def merge(l, name, o_hi, o_lo, split_name):
                for p in range(4):
                    u, b = FIRST_USE[name] + 4 * p, FIRST_BLOCK[name] + 3 * p
                    project(l, u, b, 2, KD, act_hi, act_lo)
                    project(l, u + 2, b + 2, 2, 4, o_hi, o_lo,
                            arrived=(lambda k: l * SPLITS + FIRST_SPLIT[split_name] + k + 1) if p == 0 else None)

            def attend(l, name, maps, unit0, head0, q_of, k_of, v_of, heads, prob, probT):
                units = [(h, t) for h in range(heads) for t in range(5)]

                def scores(i):
                    h, t = units[i]
                    q0, q1 = queries(t)
                    k0, k1 = keys(t)
                    for m in range(maps):
                        use = FIRST_USE[name] + maps * i + m
                        wait_free(pe, l, use)
                        ps, b, _ = buf(use)
                        n = (k1 - k0) // (1 if t == LATE else 2)
                        for c in range((k1 - k0) // n):
                            last = mm(ps[:, c, 0:n], q_of(h, m)[:, q0:q1], k_of(h, m)[:, k0 + c * n:k0 + c * n + n],
                                      start=True, stop=True)
                        last.then_inc(ready[b], 1)

                def turn(i):
                    h, t = units[i]
                    pe.wait_ge(p_ready, l * 60 + unit0 + i + 1)
                    if i:
                        pe.wait_ge(pT_copied, l * 60 + unit0 + i)
                    src = prob[:, maps * (i % 2), :]
                    for c in range(1 if t == LATE else 5):
                        out = two[:, 0, P * c:P * c + P] if c < 4 else two[:, 1, 0:P]
                        last = nc.tensor.transpose(out, src[:, P * c:P * c + P], ident)
                    last.then_inc(pT_ready, 1)

                def values(i):
                    h, t = units[i]
                    pe.wait_ge(pT_copied, l * 60 + unit0 + i + 1)
                    if h and t in (0, LATE):
                        pe.wait_ge(o_copied, l * 24 + 2 * (head0 + h) - (t == 0))
                    m = v_of(h, 0).shape[-1]
                    if t == LATE:
                        last = mm(one[1][0:m, 0:CTX], v_of(h, 0), probT[:, i % 2, 0, :], start=True, stop=True)
                    else:
                        for c in range(5):
                            last = mm(one[0][0:m, P * t:P * t + P], v_of(h, c + 1), probT[:, i % 2, c, :],
                                      start=c == 0, stop=c == 4)
                    last.then_inc(o_ready, 1)

                n = len(units)
                for i in range(-1, n + 2):
                    if i + 1 < n:
                        scores(i + 1)
                    if 0 <= i - 1 < n:
                        turn(i - 1)
                    if 0 <= i - 2:
                        values(i - 2)

            pe.wait_ge(cst_loaded, 32)
            pe.wait_ge(started, 1)
            with pe.Fori(0, DEPTH) as l:
                with pe.Fori(0, MOD_CHUNKS // 2) as i:
                    pe.wait_ge(layer_open, l + 1)
                    pe.wait_ge(mod_done, 1)
                    for c in range(2):
                        for q in range(4):
                            pe.wait_ge(raw_loaded[q], l * (16 * BLOCKS // RAW) + i * 32 + 16 * (c + 1))
                            for kk in range(2):
                                last = mm(two[0:2, c, :], cond[:, 2 * q + kk, :], raw[:, q, 512 * kk:512 * kk + 512],
                                          start=q + kk == 0, stop=q == 3 and kk == 1)
                                if kk == 0 and c + q:
                                    last.then_inc(mod_block_used, 1)
                        last.then_inc(row_ready, 1)
                    for c in range(2):
                        pe.wait_ge(row_copied, l * MOD_CHUNKS + i * 2 + (c + 1))
                        for q in range(4):
                            last = mm(one[0][:, bass.ds(i * 16 + (8 * c + 2 * q), 2)], mod_row[0:2, c, P * q:P * q + P],
                                      ident[0:2, 0:2], start=True, stop=True)
                            if c + q == 0:
                                last.then_inc(mod_block_used, 1)
                        last.then_inc(row_free, 1)
                sums(l, FIRST_USE["norm1"], FIRST_SQ["norm1"], KD)

                def h_arrived(k):
                    return l * SPLITS + FIRST_SPLIT["h1"] + k + 1
                project_tokens(l, FIRST_USE["mv"], FIRST_BLOCK["mv"], h_arrived)
                for name, n in (("mq", 2), ("mk", 2), ("mo", 4), ("mg", 1)):
                    project(l, FIRST_USE[name], FIRST_BLOCK[name], n, KD, act_hi, act_lo)
                pe.wait_ge(vm_ready, l + 1)
                pe.wait_ge(qk_ready, l + 1)
                pe.wait_ge(rows_ready, l + 1)
                for t in range(5):
                    mm(two[:, 1, ROWS * t:ROWS * t + ROWS], rows[0][:, P * t:P * t + P], ident[0:ROWS, 0:ROWS],
                       start=True, stop=True)
                for j in range(2):
                    last = mm(two[:, 0, P * j:P * j + P], km[:, j, 0:CTX], ident, start=True, stop=True)
                last.then_inc(colsT_ready, 1)

                def broadcast(u):
                    if u == 0:
                        pe.wait_ge(colsT_copied, l + 1)
                    else:
                        pe.wait_ge(bc_copied, l * UNITS + u)
                    mm(two[:, 0, :], row_sel[:, u, :], rows[4][:, CTX:T], start=True, stop=True)
                    mm(two[:, 1, 0:CTX], row_sel[:, u, :], rows[4][:, 0:CTX], start=True, stop=True)\
                        .then_inc(bc_ready, 1)

                def span(u, j):
                    if j == LATE:
                        return 0, CTX
                    return (CTX + P * j, T) if u < H_M else (CTX, CTX + P * (j + 1))

                def m_scores(i):
                    u, j = divmod(i, 5)
                    _, h, par, pair, _ = unit(u)
                    s0, _ = queries(j)
                    q0, q1 = span(u, j)
                    use = FIRST_USE["ms"] + i
                    wait_free(pe, l, use)
                    t, b, _ = buf(use)
                    mm(t[:, 0, 0:q1 - q0], km[par:par + 64, pair, s0:s0 + P], qm[par:par + 64, pair, q0:q1],
                       start=True, stop=True).then_inc(ready[b], 1)

                def m_values(i):
                    u, j = divmod(i, 5)
                    d, h, par, pair, row = unit(u)
                    if j == 0:
                        pe.wait_ge(qw_ready, l * UNITS + u + 1)
                        if u:
                            pe.wait_ge(num_copied, l * UNITS + u)
                        mm(one[0][:, :], C0[par:par + 64, 2 * d + pair, :], qw[par:par + 64, :], start=True, stop=False)
                        mm(big[0][0:ROWS, 1, :], n0[par:par + 64, 2 * d + pair, :], qw[par:par + 64, :],
                           start=u == 0, stop=False)
                    q0, q1 = span(u, j)
                    pe.wait_ge(a_ready, l * 40 + i + 1)
                    A = abuf[:, i % 2, 0:q1 - q0]
                    v = vm[:, 0 if j == LATE else j + 1, P * h:P * h + P]
                    if j == LATE:
                        mm(one[1][:, 0:CTX], v, A, start=True, stop=True)
                        mm(big[1][0:ROWS, 1, 0:CTX], den_sel[:, u, :], A, start=u == 0, stop=u == UNITS - 1)\
                            .then_inc(num_ready, 1)
                    else:
                        mm(one[0][:, q0 - CTX:q1 - CTX], v, A, start=False, stop=j == 3)
                        mm(big[0][0:ROWS, 1, q0 - CTX:q1 - CTX], den_sel[:, u, :], A, start=False,
                           stop=u == UNITS - 1 and j == 3).then_inc(a_used, 1)

                broadcast(0)
                m_scores(0)
                for i in range(40):
                    if i + 1 < 40:
                        m_scores(i + 1)
                    if i % 5 == 1 and i // 5 + 1 < UNITS:
                        broadcast(i // 5 + 1)
                    m_values(i)
                pe.wait_ge(kw_ready, l * UNITS + UNITS)
                pe.wait_ge(num_copied, l * UNITS + UNITS)
                for u in range(UNITS):
                    _, h, _, _, _ = unit(u)
                    mm(two[0:DK_M, u // 4, P * (u % 4):P * (u % 4) + P], kw[:, u, :], vm[:, 0, P * h:P * h + P],
                       start=True, stop=True)
                    last = mm(one[1][0:DK_M, u:u + 1], kw[:, u, :], ones[:, 0:1], start=True, stop=True)
                last.then_inc(state_ready, 1)
                pe.wait_ge(rden_ready, l + 1)
                for j in range(UNITS):
                    u = j // 2 + H_M * (j % 2)
                    use = FIRST_USE["mr"] + j
                    wait_free(pe, l, use)
                    t, b, _ = buf(use)
                    for h in range(2):
                        last = mm(t[:, h, 0:HALF], row_sel[:, u, :], rows[2][:, h * HALF:(h + 1) * HALF],
                                  start=True, stop=True)
                    last.then_inc(ready[b], 1)
                for h in range(H_M):
                    sums(l, FIRST_USE["mn"] + h, FIRST_SQ["mn"] + h, 1)
                merge(l, "merge_m", om_hi, om_lo, "om")

                project(l, FIRST_USE["acq"], FIRST_BLOCK["acq"], KQ, KD, act_hi, act_lo)
                sums(l, FIRST_USE["qn"], FIRST_SQ["qn"], KQ)
                project(l, FIRST_USE["ckv"], FIRST_BLOCK["ckv"], KKV, KD, act_hi, act_lo)
                sums(l, FIRST_USE["kn"], FIRST_SQ["kn"], KKV)
                project(l, FIRST_USE["qup"], FIRST_BLOCK["qup"], 8, KQ, qn_hi, qn_lo,
                        arrived=lambda k: l * SPLITS + FIRST_SPLIT["q"] + k + 1)
                project(l, FIRST_USE["kr"], FIRST_BLOCK["kr"], 1, KD, act_hi, act_lo)
                project(l, FIRST_USE["kvn"], FIRST_BLOCK["kvn"], 4, KKV, ckv_hi, ckv_lo, n=TK // 2,
                        arrived=lambda k: l * SPLITS + FIRST_SPLIT["kv"] + k + 1)
                block_start(l, FIRST_BLOCK["kvv"])
                slot = FIRST_BLOCK["kvv"] % SPLIT
                for i in range(3):
                    use = FIRST_USE["kvv"] + i
                    wait_free(pe, l, use)
                    ps, b, _ = buf(use)
                    for tt in range(2):
                        t = 2 * i + tt
                        for kk in range(KKV):
                            wh, wl = w_hi[:, slot, 512 * kk:512 * kk + 512], w_lo[:, slot, 512 * kk:512 * kk + 512]
                            ah, al = ckv_hi[:, kk, P * t:P * t + P], ckv_lo[:, kk, P * t:P * t + P]
                            first = mm(ps[:, tt, :], ah, wh, start=kk == 0, stop=False)
                            if t + kk == 0:
                                first.then_inc(block_used, 1)
                            mm(ps[:, tt, :], al, wh, start=False, stop=False)
                            last = mm(ps[:, tt, :], ah, wl, start=False, stop=kk == KKV - 1)
                    last.then_inc(ready[b], 1)
                pe.wait_ge(roped, l * 11 + 3)
                pe.wait_ge(kn_copied, l + 1)
                pe.wait_ge(v_copied, l * 2 + 1)
                attend(l, "ma", 1, 0, 0, lambda h, m: q_a[:, h, :], lambda h, m: k_a[:, h, :],
                       lambda h, c: v_a[:, c, V_A * h:V_A * h + V_A], H_A, prob_a, probT_a)
                merge(l, "merge_a", oa_hi, oa_lo, "oa")

                project_tokens(l, FIRST_USE["dv"], FIRST_BLOCK["dv"])
                project(l, FIRST_USE["dq"], FIRST_BLOCK["dq"], 4, KD, act_hi, act_lo)
                project(l, FIRST_USE["dk"], FIRST_BLOCK["dk"], 4, KD, act_hi, act_lo)
                pe.wait_ge(roped, l * 11 + 11)
                pe.wait_ge(v_copied, l * 2 + 2)
                pe.wait_ge(past_loaded, l * 64 + 64)
                attend(l, "da", 2, 40, 8, lambda h, m: q_d[64 * m:64 * m + 64, h, :],
                       lambda h, m: k_d[64 * m:64 * m + 64, h, :],
                       lambda h, c: v_d[:, c, P * h:P * h + P], H_D, prob_d, probT_d)
                for h in range(H_D):
                    sums(l, FIRST_USE["dn"] + h, FIRST_SQ["dn"] + h, 1)
                merge(l, "merge_d", od_hi, od_lo, "od")

                project(l, FIRST_USE["wout"], FIRST_BLOCK["wout"], 8, KD, act_hi, act_lo,
                        arrived=lambda k: l * SPLITS + FIRST_SPLIT["y"] + k + 1)
                sums(l, FIRST_USE["norm2"], FIRST_SQ["norm2"], KD)
                with pe.Fori(0, FF_CHUNKS) as c:
                    pe.wait_ge(lo_done, l * SPLITS + FIRST_SPLIT["ff"])
                    project(l, FIRST_USE["ff"], FIRST_BLOCK["ff"], 8, KD, act_hi, act_lo, more_b=c * 16, more_u=c * 8)
                    project(l, FIRST_USE["ff"] + 8, FIRST_BLOCK["ff"] + 8, 8, KD, ff_hi, ff_lo,
                            arrived=lambda k: l * SPLITS + c * 8 + (FIRST_SPLIT["ff"] + k + 1),
                            more_b=c * 16, more_u=c * 8)
            pe.wait_ge(layer_open, DEPTH + 1)
            sums(DEPTH, 0, 0, KD)

        @block.scalar
        def _(act):
            f = nc.scalar.activation

            def squares(l, first_sq, first_src, tiles, sources_wait=True):
                for k, ap in enumerate(tiles):
                    if sources_wait is not None:
                        act.wait_ge(src_ready, sources_wait(k))
                    if k >= 2:
                        act.wait_ge(sq_used, l * SQ_USED + FIRST_SQ_USED[first_sq] + k - 1)
                    f(sq[:, k % 2, :], ap, ACT.Square).then_inc(sq_ready, 1)

            def inverse_root(l, use, norm, n):
                t, b, _ = buf(use)
                act.wait_ge(rs_used, l * N_NORMS + norm + 1)
                wait_ready(act, l, use)
                f(two_parts(rs[:, :]), halves(t), ACT.Ln, bias=eps, scale=1.0 / n).then_inc(free[b], 1)
                act.drain()
                f(rs[:, :], rs[:, :], ACT.Exp, scale=-0.5).then_inc(rs_ready, 1)

            def round_tiles(l, name, pairs, scale=None):
                for k, (hi, src) in enumerate(pairs):
                    act.wait_ge(whole, l * SPLITS + FIRST_SPLIT[name] + k + 1)
                    f(hi, src, ACT.Copy, scale=1.0 if scale is None else scale).then_inc(hi_done, 1)

            def merge(l, name, first_gate):
                for m in range(8):
                    use = FIRST_USE[name] + 4 * (m // 2) + m % 2
                    wait_ready(act, l, use)
                    act.wait_ge(y_done, l * 24 + first_gate + m + 1)
                    t, b, _ = buf(use)
                    f(two_parts(stage[:, m % 2, :]), halves(t), ACT.Tanh, scale=0.5).then_inc(free[b], 1)
                    act.drain().then_inc(gate_ready, 1)

            def attend(l, name, maps, unit0, heads, prob, probT, exp0):
                units = [(h, t) for h in range(heads) for t in range(5)]

                def exps(i):
                    h, t = units[i]
                    if i >= 2:
                        act.wait_ge(pT_ready, l * 60 + unit0 + i - 1)
                    for m in range(maps):
                        use = FIRST_USE[name] + maps * i + m
                        ps, b, _ = buf(use)
                        col = 2 * (i % 2) + m
                        act.wait_ge(maxed, l * 80 + exp0 + maps * i + m + 1)
                        dst = prob[:, maps * (i % 2) + m, :]
                        if t == LATE:
                            out, src = dst[:, 0:CTX], ps[:, 0, 0:CTX]
                        else:
                            out, src = two_parts(dst), halves(ps)
                        f(out, src, ACT.Exp, bias=neg_max[:, col:col + 1],
                          accum_out=row_sum[:, col:col + 1]).then_inc(free[b], 1)
                        act.drain().then_inc(exped, 1)

                def copyT(i):
                    h, t = units[i]
                    act.wait_ge(pT_ready, l * 60 + unit0 + i + 1)
                    if i >= 2:
                        act.wait_ge(o_ready, l * 60 + unit0 + i - 1)
                    n = CTX if t == LATE else T
                    f(probT[:, i % 2, :, :].rearrange("p c q -> p (c q)")[:, 0:n],
                      two[:, :, :].rearrange("p a c -> p (a c)")[:, 0:n], ACT.Copy).then_inc(pT_copied, 1)

                n = len(units)
                for i in range(-1, n + 1):
                    if i + 1 < n:
                        exps(i + 1)
                    if i >= 1:
                        copyT(i - 1)

            act.dma_start(cst[:, :], consts).then_inc(cst_loaded, 16)
            act.dma_start(cond[:, :, :], condT).then_inc(cst_loaded, 16)
            act.wait_ge(cst_loaded, 32)
            f(mod[:, 0:KD, :], cond[:, :, :], ACT.Tanh, scale=0.5).then_inc(cond_done, 1)
            act.wait_ge(x_loaded, 16)
            act.wait_ge(started, 1)
            with act.Fori(0, DEPTH) as l:
                act.wait_ge(layer_open, l + 1)
                act.dma_start(small[:, :], small_d[l]).then_inc(small_loaded, 16)
                act.wait_ge(lam_sums, l + 1)
                f(lam_tmp[:, 0:2], lam_tmp[:, 0:2], ACT.Exp).then_inc(lam_exps, 1)
                with act.Fori(0, MOD_CHUNKS // 2) as i:
                    for c in range(2):
                        act.wait_ge(row_ready, l * MOD_CHUNKS + i * 2 + (c + 1))
                        act.wait_ge(row_free, l * MOD_CHUNKS + i * 2 + (c + 1))
                        f(mod_row[0:2, c, :], two[0:2, c, :], ACT.Copy).then_inc(row_copied, 1)
                squares(l, FIRST_SQ["norm1"], 0, [x[:, k, :] for k in range(KD)], None)
                inverse_root(l, FIRST_USE["norm1"], NORMS["norm1"], D)
                round_tiles(l, "h1", [(act_hi[:, k, :], stage[:, k % 2, :]) for k in range(KD)])

                wait_ready(act, l, FIRST_USE["mv"])
                wait_ready(act, l, FIRST_USE["mv"] + 1)
                f(vm[:, 0:2, :], big[0][:, :, :], ACT.Copy).then_inc(free[0], 1)
                f(vm[:, 2:4, :], big[1][:, :, :], ACT.Copy).then_inc(free[1], 1)
                f(vm[:, 4, :], two[:, 0, :], ACT.Copy).then_inc(vm_ready, 1)
                for name, n, dst, s in (("mq", 2, qm, DK_M ** -0.5), ("mk", 2, km, 1.0)):
                    for m in range(n):
                        wait_ready(act, l, FIRST_USE[name] + m)
                        t, b, _ = buf(FIRST_USE[name] + m)
                        f(two_parts(dst[:, m, :]), halves(t), ACT.Copy, scale=s).then_inc(free[b], 1)
                act.drain().then_inc(qk_ready, 1)
                for m in range(4):
                    wait_ready(act, l, FIRST_USE["mo"] + m)
                    t, b, _ = buf(FIRST_USE["mo"] + m)
                    f(two_parts(mo_th[:, m, :]), halves(t), ACT.Tanh, scale=0.5).then_inc(free[b], 1)
                act.wait_ge(gate_rows, l + 1)
                f(rows[5][:, :], rows[1][:, :], ACT.Abs)
                act.drain()
                f(rows[5][:, :], rows[5][:, :], ACT.Exp, scale=-1.0)
                act.drain()
                f(rows[5][:, :], rows[5][:, :], ACT.Ln, bias=ones[0:ROWS, 0:1]).then_inc(soft_rows, 1)
                act.wait_ge(rows_ready, l + 1)
                f(rows[5][:, :], rows[1][:, :], ACT.Exp, scale=-1.0).then_inc(expm_ready, 1)
                act.dma_start(o_m[l, 0:H_M, :], rows[1][0:H_M, CTX - 1:CTX]).then_inc(state_stored, 16)
                act.dma_start(o_m[l, H_M:UNITS, :], rows[1][32:32 + H_M, 0:1]).then_inc(state_stored, 16)
                act.wait_ge(colsT_ready, l + 1)
                f(acol[:, :, :], two[:, 1, 0:5 * ROWS].rearrange("p (t r) -> p t r", r=ROWS), ACT.Copy)
                f(ktok[:, :], two[:, 0, 0:256], ACT.Copy)
                act.drain().then_inc(colsT_copied, 1)

                def unit_start(u):
                    _, h, par, pair, _ = unit(u)
                    act.wait_ge(bc_ready, l * UNITS + u + 1)
                    if u:
                        act.wait_ge(arg_ready, l * 40 + 5 * u)
                    f(nMbc[:, CTX:T], two[:, 0, :], ACT.Copy)
                    f(nMbc[:, 0:CTX], two[:, 1, 0:CTX], ACT.Copy)
                    act.drain().then_inc(bc_copied, 1)
                    if u:
                        act.wait_ge(num_ready, l * UNITS + u)
                    f(qw[par:par + 64, :], nMbc[par:par + 64, CTX:T], ACT.Exp, bias=s_("m0")[par:par + 64, u:u + 1])\
                        .then_inc(w_inter_ready, 1)

                def unit_end(u):
                    act.wait_ge(num_ready, l * UNITS + u + 1)
                    f(num_sb[:, u, CTX:T], one[0][:, :], ACT.Copy)
                    f(num_sb[:, u, 0:CTX], one[1][:, 0:CTX], ACT.Copy).then_inc(num_copied, 1)

                for i in range(40):
                    u, j = divmod(i, 5)
                    if j == 0:
                        if u:
                            unit_end(u - 1)
                        unit_start(u)
                    act.wait_ge(arg_ready, l * 40 + i + 1)
                    n = CTX if j == LATE else (LAT - P * j if u < H_M else P * (j + 1))
                    f(ebuf[:, i % 2, 0:n], ebuf[:, i % 2, 0:n], ACT.Exp).then_inc(e_ready, 1)
                unit_end(UNITS - 1)
                act.wait_ge(state_ready, l + 1)
                f(c_new[:, 0:4, :], two[0:DK_M, 0, :].rearrange("p (u e) -> p u e", e=DV_M), ACT.Copy)
                f(c_new[:, 4:8, :], two[0:DK_M, 1, :].rearrange("p (u e) -> p u e", e=DV_M), ACT.Copy)
                f(n_new[:, :], one[1][0:DK_M, 0:UNITS], ACT.Copy).then_inc(state_copied, 1)
                act.wait_ge(state_copied, l + 1)
                act.dma_start(o_C[l], c_new[:, :, :]).then_inc(state_stored, 16)
                act.dma_start(o_n[l], n_new[:, :]).then_inc(state_stored, 16)
                for h in range(H_M):
                    squares(l, FIRST_SQ["mn"] + h, 0, [num_sb[:, h, :]],
                            lambda k: l * 16 + h + 1)
                    inverse_root(l, FIRST_USE["mn"] + h, NORMS["mn"] + h, DV_M)
                    act.wait_ge(whole, l * SPLITS + FIRST_SPLIT["om"] + h + 1)
                    f(om_hi[:, h, :], stage[:, h % 2, :], ACT.Copy).then_inc(hi_done, 1)
                act.wait_ge(lo_done, l * SPLITS + FIRST_SPLIT["om"] + 4)
                merge(l, "merge_m", 0)

                act.wait_ge(y_done, l * 24 + 8 + 2)
                act.wait_ge(state_stored, l * 64 + 64)
                act.dma_start(ckv[:, :, T:TK], past_d[l, :, PAST_C["ckv"][0]:PAST_C["ckv"][1]]
                              .rearrange("p (k t) -> p k t", t=PAST)).then_inc(past_loaded, 16)
                for k in range(KQ):
                    wait_ready(act, l, FIRST_USE["acq"] + k)
                    t, b, _ = buf(FIRST_USE["acq"] + k)
                    f(two_parts(acq[:, k, :]), halves(t), ACT.Copy).then_inc(free[b], 1)
                act.drain()
                squares(l, FIRST_SQ["qn"], 0, [acq[:, k, :] for k in range(KQ)], None)
                inverse_root(l, FIRST_USE["qn"], NORMS["qn"], Q_RANK)
                round_tiles(l, "q", [(qn_hi[:, k, :], acq[:, k, :]) for k in range(KQ)])
                for k in range(KKV):
                    wait_ready(act, l, FIRST_USE["ckv"] + k)
                    t, b, _ = buf(FIRST_USE["ckv"] + k)
                    f(two_parts(ckv[:, k, 0:T]), halves(t), ACT.Copy).then_inc(free[b], 1)
                act.drain()
                squares(l, FIRST_SQ["kn"], 0, [ckv[:, k, 0:T] for k in range(KKV)], None)
                inverse_root(l, FIRST_USE["kn"], NORMS["kn"], KV_RANK)
                act.wait_ge(past_loaded, l * 64 + 16)
                round_tiles(l, "kv", [(ckv_hi[:, k, :], ckv[:, k, :]) for k in range(KKV)])
                act.dma_start(o_ckv[l], ckv[:, :, 0:CTX]).then_inc(ckv_stored, 16)
                scale = (NOPE + ROPE) ** -0.5
                for m in range(8):
                    use = FIRST_USE["qup"] + m
                    wait_ready(act, l, use)
                    t, b, _ = buf(use)
                    if m < 4:
                        f(two_parts(q_a[0:64, 2 * m, :]), halves(t)[0:64], ACT.Copy, scale=scale)
                        f(two_parts(q_a[0:64, 2 * m + 1, :]), halves(t)[64:128], ACT.Copy, scale=scale)\
                            .then_inc(free[b], 1)
                    else:
                        if m >= 6:
                            act.wait_ge(roped, l * 11 + 1)
                        f(two_parts(stage[:, m % 2, :]), halves(t), ACT.Copy, scale=scale).then_inc(free[b], 1)
                        if m % 2:
                            act.drain().then_inc(raw_kept, 1)
                use = FIRST_USE["kr"]
                act.wait_ge(roped, l * 11 + 2)
                wait_ready(act, l, use)
                t, b, _ = buf(use)
                act.dma_start(k_a[64:96, 0, T:TK], past_d[l, 64:96, PAST_C["kr"][0]:PAST_C["kr"][1]])\
                    .then_inc(past_loaded, 16)
                f(two_parts(stage[64:128, 0, :]), halves(t)[64:128], ACT.Copy).then_inc(free[b], 1)
                act.drain().then_inc(raw_kept, 1)
                act.dma_start(o_kr[l], stage[64:96, 0, 0:CTX]).then_inc(kr_stored, 16)
                for m in range(4):
                    use = FIRST_USE["kvn"] + m
                    wait_ready(act, l, use)
                    t, b, _ = buf(use)
                    f(two_parts(k_a[0:64, 2 * m, :], TK // 2), halves(t, TK // 2)[0:64], ACT.Copy)
                    f(two_parts(k_a[0:64, 2 * m + 1, :], TK // 2), halves(t, TK // 2)[64:128], ACT.Copy)\
                        .then_inc(free[b], 1)
                act.drain().then_inc(kn_copied, 1)
                attend(l, "ma", 1, 0, H_A, prob_a, probT_a, 0)
                act.wait_ge(kr_stored, l * 16 + 16)
                act.wait_ge(ckv_stored, l * 16 + 16)
                round_tiles(l, "oa", [(oa_hi[:, k, :], o_a[:, k, :]) for k in range(4)])
                merge(l, "merge_a", 8)

                act.wait_ge(y_done, l * 24 + 16 + 2)
                act.dma_start(v_d[:, 5, :], past_d[l, :, PAST_C["dv"][0]:PAST_C["dv"][1]]).then_inc(past_loaded, 16)
                act.dma_start(k_d[:, :, T:TK], past_d[l, :, PAST_C["dk"][0]:PAST_C["dk"][1]]
                              .rearrange("p (k t) -> p k t", t=PAST)).then_inc(past_loaded, 16)
                wait_ready(act, l, FIRST_USE["dv"])
                wait_ready(act, l, FIRST_USE["dv"] + 1)
                f(v_d[:, 0:2, :], big[0][:, :, :], ACT.Copy).then_inc(free[0], 1)
                f(v_d[:, 2:4, :], big[1][:, :, :], ACT.Copy).then_inc(free[1], 1)
                f(v_d[:, 4, :], two[:, 0, :], ACT.Copy)
                act.drain().then_inc(v_copied, 1)
                act.dma_start(o_dv[l], v_d[:, 0, :]).then_inc(diff_stored, 16)
                for m in range(8):
                    use = FIRST_USE["dq"] + m
                    wait_ready(act, l, use)
                    act.wait_ge(roped, l * 11 + 3 + max(m - 1, 0))
                    t, b, _ = buf(use)
                    f(two_parts(stage[:, m % 2, :]), halves(t), ACT.Copy, scale=DK_D ** -0.5 if m < 4 else 1.0)\
                        .then_inc(free[b], 1)
                    act.drain().then_inc(raw_kept, 1)
                act.wait_ge(roped, l * 11 + 11)
                act.dma_start(o_dk[l], k_d[:, :, 0:CTX]).then_inc(diff_stored, 16)
                attend(l, "da", 2, 40, H_D, prob_d, probT_d, 40)
                act.wait_ge(diff_stored, l * 32 + 32)
                for h in range(H_D):
                    squares(l, FIRST_SQ["dn"] + h, 0, [q_d[:, h, :]], lambda k: l * 16 + 4 + h + 1)
                    inverse_root(l, FIRST_USE["dn"] + h, NORMS["dn"] + h, DV_D)
                    act.wait_ge(whole, l * SPLITS + FIRST_SPLIT["od"] + h + 1)
                    f(od_hi[:, h, :], q_d[:, h, :], ACT.Copy).then_inc(hi_done, 1)
                merge(l, "merge_d", 16)

                round_tiles(l, "y", [(act_hi[:, k, :], y[:, k, :]) for k in range(KD)], scale=0.5)
                squares(l, FIRST_SQ["norm2"], 0, [x[:, k, :] for k in range(KD)],
                        lambda k: l * 16 + 8 + k + 1)
                inverse_root(l, FIRST_USE["norm2"], NORMS["norm2"], D)
                round_tiles(l, "h2", [(act_hi[:, k, :], stage[:, k % 2, :]) for k in range(KD)])
                with act.Fori(0, FF_CHUNKS) as c:
                    def relu(m):
                        use = FIRST_USE["ff"] + m
                        wait_ready(act, l, use, c * 8)
                        act.wait_ge(relu_used, l * 32 + c * 8 + (m + 1))
                        t, b, _ = buf(use)
                        f(two_parts(sq[:, m % 2, :]), halves(t), ACT.Relu).then_inc(free[b], 1)
                        act.drain().then_inc(relu_ready, 1)

                    def round_ff(m):
                        act.wait_ge(whole, l * SPLITS + c * 8 + (FIRST_SPLIT["ff"] + m + 1))
                        f(ff_hi[:, m, :], stage[:, m % 2, :], ACT.Copy).then_inc(hi_done, 1)
                    relu(0)
                    for m in range(8):
                        if m + 1 < 8:
                            relu(m + 1)
                        round_ff(m)
            act.wait_ge(layer_open, DEPTH + 1)
            squares(DEPTH, 0, 0, [x[:, k, :] for k in range(KD)], None)
            inverse_root(DEPTH, 0, 0, D)

        @block.vector
        def _(dve):
            v = nc.vector

            def remainder(l, name, k, lo, src, hi, more=0):
                dve.wait_ge(hi_done, l * SPLITS + more + (FIRST_SPLIT[name] + k + 1))
                v.tensor_tensor(lo, src, hi.bitcast(f32), ALU.subtract).then_inc(lo_done, 1)

            def norm_apply(l, name, norm, scale, shift):
                for k in range(KD + 1):
                    dve.drain()
                    if k == 0:
                        dve.wait_ge(rs_ready, l * N_NORMS + norm + 1)
                    if k < KD:
                        v.tensor_tensor(t1[:, :], x[:, k, :], rs[:, :], ALU.mult)
                        dve.drain()
                        for g, a, b in GROUPS:
                            last = v.tensor_scalar(stage[:, k % 2, a:b], t1[:, a:b], scale[:, k, g:g + 1],
                                                   shift[:, k, g:g + 1], ALU.mult, ALU.add)
                        last.then_inc(whole, 1)
                    if k:
                        dve.drain()
                        remainder(l, name, k - 1, act_lo[:, k - 1, :], stage[:, (k - 1) % 2, :], act_hi[:, k - 1, :])
                dve.drain().then_inc(rs_used, 1)

            def merge(l, name, first_gate, first):
                for m in range(8):
                    gate, use = first_gate + m, FIRST_USE[name] + 4 * (m // 2) + 2 + m % 2
                    dve.wait_ge(gate_ready, l * 24 + gate + 1)
                    wait_ready(dve, l, use)
                    t, b, _ = buf(use)
                    dst = y[:, m, :] if first else t1[:, :]
                    v.scalar_tensor_tensor(two_parts(dst), two_parts(stage[:, m % 2, :]), 1.0, halves(t), ALU.add,
                                           ALU.mult).then_inc(free[b], 1)
                    dve.drain()
                    if first:
                        dve.drain().then_inc(y_done, 1)
                    else:
                        v.tensor_tensor(y[:, m, :], y[:, m, :], t1[:, :], ALU.add).then_inc(y_done, 1)
                        dve.drain()

            def attend(l, name, maps, unit0, head0, heads, prob, exp0, out_of):
                units = [(h, t) for h in range(heads) for t in range(5)]

                def maxes(i):
                    h, t = units[i]
                    for m in range(maps):
                        use = FIRST_USE[name] + maps * i + m
                        wait_ready(dve, l, use)
                        ps, b, _ = buf(use)
                        col = 2 * (i % 2) + m
                        src = ps[:, 0, 0:CTX] if t == LATE else halves(ps)
                        v.tensor_reduce(neg_max[:, col:col + 1], src, AX.X if t == LATE else AX.XY, ALU.max,
                                        negate=True).then_inc(maxed, 1)

                def normalise(i):
                    h, t = units[i]
                    n = CTX if t == LATE else T
                    c0 = 2 * (i % 2)
                    dve.wait_ge(exped, l * 80 + exp0 + maps * (i + 1))
                    v.reciprocal(row_sum[:, c0:c0 + maps], row_sum[:, c0:c0 + maps])
                    dve.drain()
                    p0 = prob[:, maps * (i % 2), 0:n]
                    if maps == 1:
                        v.tensor_scalar(p0, p0, row_sum[:, c0:c0 + 1], None, ALU.mult).then_inc(p_ready, 1)
                    else:
                        p1 = prob[:, maps * (i % 2) + 1, 0:n]
                        v.tensor_scalar(p1, p1, row_sum[:, c0 + 1:c0 + 2], neg_lam, ALU.mult, ALU.mult)
                        dve.drain()
                        v.scalar_tensor_tensor(p0, p0, row_sum[:, c0:c0 + 1], p1, ALU.mult, ALU.add)\
                            .then_inc(p_ready, 1)
                    dve.drain()

                def outputs(i):
                    h, t = units[i]
                    lat, con, m = out_of(h)
                    if t >= LATE - 1:
                        dve.wait_ge(o_ready, l * 60 + unit0 + i + 1)
                        v.tensor_copy(*((con, one[1][0:m, 0:CTX]) if t == LATE else (lat, one[0][0:m, :])))\
                            .then_inc(o_copied, 1)

                n = len(units)
                for i in range(-1, n + 3):
                    if i + 1 < n:
                        maxes(i + 1)
                    if 0 <= i < n:
                        normalise(i)
                    if i >= 3:
                        outputs(i - 3)
                dve.drain()

            for s, n in ((split_ready, RAW), (block_used, 1), (free[0], 1), (free[1], 1), (row_free, 2), (rs_used, 1), (y_done, 2), (relu_used, 2)):
                v.memset(cols[:, 0:1], 0.0).then_inc(s, n)
                dve.drain()
            v.memset(cols[:, 0:1], 0.0).then_inc(started, 1)
            dve.wait_ge(cst_loaded, 32)
            dve.wait_ge(cond_done, 1)
            v.scalar_tensor_tensor(mod[:, 0:KD, :], mod[:, 0:KD, :], 1.0, cond[:, :, :], ALU.add, ALU.mult)
            dve.drain()
            v.tensor_scalar(cond[:, :, :], mod[:, 0:KD, :], 0.5, None, ALU.mult).then_inc(mod_done, 1)
            dve.wait_ge(x_loaded, 16)
            dve.drain()
            v.memset(cols[:, 0:32], 0.0).then_inc(layer_open, 1)
            with dve.Fori(0, DEPTH) as l:
                dve.wait_ge(small_loaded, l * 16 + 16)
                lam = s_("lam").rearrange("p (a d) -> p a d", d=DK_D)
                v.tensor_tensor(t2[:, 0:64], lam[:, 0, :], lam[:, 1, :], ALU.mult)
                v.tensor_tensor(t2[:, 64:128], lam[:, 2, :], lam[:, 3, :], ALU.mult)
                dve.drain()
                v.tensor_reduce(lam_tmp[:, 0:2], t2[:, 0:128].rearrange("p (a d) -> p a d", d=64), AX.X, ALU.add)\
                    .then_inc(lam_sums, 1)
                dve.wait_ge(lam_exps, l + 1)
                v.tensor_tensor(lam_tmp[:, 2:3], lam_tmp[:, 1:2], lam_tmp[:, 0:1], ALU.subtract)
                dve.drain()
                v.tensor_tensor(neg_lam, lam_tmp[:, 2:3], s_("lam_init")[:, 0:1], ALU.subtract)
                v.tensor_scalar(g_half, s_("ng_m"), 0.5, None, ALU.mult)
                v.tensor_scalar(g_diff, s_("ng_d"), s_("lam_init")[:, 1:2], None, ALU.mult)
                dve.wait_ge(row_free, l * MOD_CHUNKS + MOD_CHUNKS + 2)
                v.tensor_tensor(mod[:, :, :], one[0][:, 0:96].rearrange("p (j g) -> p j g", g=2),
                                s_("bmod").unsqueeze(2).to_broadcast([P, 48, 2]), ALU.add)
                dve.drain()
                for scale, j, g in ((scale1, 1, "n1"), (scale2, 4, "n2")):
                    v.scalar_tensor_tensor(scale[:, :, :], mod[:, 8 * j:8 * j + 8, :], 1.0,
                                           s_(g).unsqueeze(2).to_broadcast([P, KD, 2]), ALU.add, ALU.mult)
                dve.drain()
                norm_apply(l, "h1", NORMS["norm1"], scale1, mod[:, 0:8, :])

                use = FIRST_USE["mg"]
                wait_ready(dve, l, use)
                t, b, _ = buf(use)
                v.tensor_scalar(two_parts(rows[0][:, :]), halves(t)[0:ROWS], s_("gb")[0:ROWS, 0:1], None, ALU.add)
                v.tensor_scalar(two_parts(rows[1][:, :]), halves(t)[64:64 + ROWS], s_("gb")[64:64 + ROWS, 1:2], None,
                                ALU.add).then_inc(free[b], 1)
                v.memset(rows[2][:, :], 0.0)
                v.memset(rows[3][:, :], 1.0)
                dve.drain().then_inc(gate_rows, 1)
                dve.wait_ge(soft_rows, l + 1)
                v.tensor_scalar(rows[1][:, :], rows[1][:, :], 0.0, None, ALU.min)
                dve.drain()
                v.tensor_tensor(rows[1][:, :], rows[1][:, :], rows[5][:, :], ALU.subtract)
                dve.drain()

                def scans(dst, data0, data1, op0, op1, first):
                    for r, a, b_, back in ((0, 0, CTX, 0), (0, CTX, T, 0), (32, 0, CTX, 1), (32, CTX, T, 1)):
                        def w(tile):
                            ap = tile[r:r + H_M, a:b_]
                            return ap[:, ::-1] if back else ap
                        init = 0.0 if first is None or a == 0 else first[r:r + H_M, 0:1]
                        v.tensor_tensor_scan(w(dst), w(data0), w(data1), init, op0, op1)
                    dve.drain()
                scans(rows[2], rows[3], rows[1], ALU.mult, ALU.add, None)
                v.tensor_tensor(rows[0][:, :], rows[0][:, :], rows[2][:, :], ALU.subtract)
                dve.drain()
                scans(rows[3], rows[0], rows[0], ALU.max, ALU.max, s_("m0row"))
                v.tensor_tensor(rows[1][:, :], rows[2][:, :], rows[3][:, :], ALU.add)
                v.tensor_scalar(rows[4][:, :], rows[3][:, :], -1.0, None, ALU.mult)
                dve.drain().then_inc(rows_ready, 1)
                dve.wait_ge(colsT_copied, l + 1)

                def argument(i):
                    u, j = divmod(i, 5)
                    _, h, par, pair, row = unit(u)
                    if i >= 2:
                        dve.wait_ge(e_ready, l * 40 + i - 1)
                    mask = c_("mask_f") if u < H_M else c_("mask_b")
                    if j == 0:
                        dve.wait_ge(bc_copied, l * UNITS + u + 1)
                        dve.wait_ge(w_inter_ready, l * UNITS + u + 1)
                        v.tensor_tensor(qw[par:par + 64, :], qw[par:par + 64, :], qm[par:par + 64, pair, CTX:T],
                                        ALU.mult).then_inc(qw_ready, 1)
                    s = acol[:, 0 if j == LATE else j + 1, row:row + 1]
                    e = ebuf[:, i % 2, :]
                    if j == LATE:
                        v.scalar_tensor_tensor(e[:, 0:P], nMbc[:, 0:CTX], s, mask, ALU.add, ALU.min)
                    else:
                        q0 = CTX + P * j
                        if u < H_M:
                            v.scalar_tensor_tensor(e[:, 0:P], nMbc[:, q0:q0 + P], s, mask, ALU.add, ALU.min)
                            if j < 3:
                                v.tensor_scalar(e[:, P:T - q0], nMbc[:, q0 + P:T], s, 0.0, ALU.add, ALU.min)
                        else:
                            v.scalar_tensor_tensor(e[:, P * j:P * j + P], nMbc[:, q0:q0 + P], s, mask, ALU.add, ALU.min)
                            if j:
                                v.tensor_scalar(e[:, 0:P * j], nMbc[:, CTX:q0], s, 0.0, ALU.add, ALU.min)
                    dve.drain().then_inc(arg_ready, 1)

                def product(i):
                    u, j = divmod(i, 5)
                    _, h, _, _, _ = unit(u)
                    use = FIRST_USE["ms"] + i
                    t, b, _ = buf(use)
                    n = CTX if j == LATE else (LAT - P * j if u < H_M else P * (j + 1))
                    wait_ready(dve, l, use)
                    dve.wait_ge(e_ready, l * 40 + i + 1)
                    if i >= 2:
                        pu, pj = divmod(i - 2, 5)
                        if pj == LATE:
                            dve.wait_ge(num_ready, l * UNITS + pu + 1)
                        else:
                            dve.wait_ge(a_used, l * (4 * UNITS) + 4 * pu + pj + 1)
                    v.tensor_tensor(abuf[:, i % 2, 0:n], ebuf[:, i % 2, 0:n], t[:, 0, 0:n], ALU.mult)\
                        .then_inc(free[b], 1)
                    if j == LATE:
                        last_col = CTX - 1 if u < H_M else 0
                        v.tensor_scalar(kw[:, u, :], ktok[:, DK_M * h:DK_M * h + DK_M],
                                        ebuf[:, i % 2, last_col:last_col + 1], None, ALU.mult).then_inc(kw_ready, 1)
                    dve.drain().then_inc(a_ready, 1)

                argument(0)
                for i in range(40):
                    if i % 5 != 4 and i + 1 < 40:
                        argument(i + 1)
                        product(i)
                    else:
                        product(i)
                        if i + 1 < 40:
                            argument(i + 1)
                dve.wait_ge(num_ready, l * UNITS + UNITS)
                dve.wait_ge(expm_ready, l + 1)
                v.tensor_scalar(rows[2][:, CTX:T], big[0][0:ROWS, 1, :], -1.0, None, ALU.mult)
                v.tensor_scalar(rows[2][:, 0:CTX], big[1][0:ROWS, 1, 0:CTX], -1.0, None, ALU.mult)
                dve.drain()
                v.tensor_tensor(rows[2][:, CTX:T], rows[2][:, CTX:T], big[0][0:ROWS, 1, :], ALU.max)
                v.tensor_tensor(rows[2][:, 0:CTX], rows[2][:, 0:CTX], big[1][0:ROWS, 1, 0:CTX], ALU.max)
                dve.drain()
                v.tensor_tensor(rows[2][:, :], rows[2][:, :], rows[5][:, :], ALU.max)
                dve.drain()
                v.reciprocal(rows[2][:, :], rows[2][:, :]).then_inc(rden_ready, 1)
                dve.wait_ge(num_copied, l * UNITS + UNITS)
                for h in range(H_M):
                    for d in range(2):
                        u, use = h + H_M * d, FIRST_USE["mr"] + 2 * h + d
                        wait_ready(dve, l, use)
                        t, b, _ = buf(use)
                        v.tensor_tensor(two_parts(num_sb[:, u, :]), two_parts(num_sb[:, u, :]), halves(t), ALU.mult)\
                            .then_inc(free[b], 1)
                    dve.drain()
                    v.tensor_tensor(num_sb[:, h, :], num_sb[:, h, :], num_sb[:, h + H_M, :], ALU.add)\
                        .then_inc(src_ready, 1)
                dve.wait_ge(state_ready, l + 1)
                for h in range(H_M):
                    dve.wait_ge(rs_ready, l * N_NORMS + NORMS["mn"] + h + 1)
                    v.scalar_tensor_tensor(t1[:, :], num_sb[:, h, :], g_half[:, h:h + 1], rs[:, :], ALU.mult, ALU.mult)
                    dve.drain().then_inc(rs_used, 1)
                    v.scalar_tensor_tensor(stage[:, h % 2, :], mo_th[:, h, :], 1.0, t1[:, :], ALU.add, ALU.mult)\
                        .then_inc(whole, 1)
                    dve.drain()
                    remainder(l, "om", h, om_lo[:, h, :], stage[:, h % 2, :], om_hi[:, h, :])
                merge(l, "merge_m", 0, True)

                dve.wait_ge(rs_ready, l * N_NORMS + NORMS["qn"] + 1)
                for k in range(KQ):
                    v.scalar_tensor_tensor(acq[:, k, :], acq[:, k, :], s_("ng_q")[:, k:k + 1], rs[:, :], ALU.mult,
                                           ALU.mult).then_inc(whole, 1)
                dve.drain().then_inc(rs_used, 1)
                for k in range(KQ):
                    remainder(l, "q", k, qn_lo[:, k, :], acq[:, k, :], qn_hi[:, k, :])
                dve.wait_ge(rs_ready, l * N_NORMS + NORMS["kn"] + 1)
                dve.wait_ge(past_loaded, l * 64 + 16)
                for k in range(KKV):
                    v.scalar_tensor_tensor(ckv[:, k, 0:T], ckv[:, k, 0:T], s_("ng_kv")[:, k:k + 1], rs[:, :],
                                           ALU.mult, ALU.mult).then_inc(whole, 1)
                dve.drain().then_inc(rs_used, 1)
                for k in range(KKV):
                    remainder(l, "kv", k, ckv_lo[:, k, :], ckv[:, k, :], ckv_hi[:, k, :])
                for j in range(2):
                    dve.wait_ge(raw_kept, l * 11 + j + 1)
                    v.tensor_tensor(t1[:, CTX:T], stage[:, 0, CTX:T], c_("cos_a"), ALU.mult)
                    v.tensor_tensor(t2[:, CTX:T], stage[:, 1, CTX:T], c_("sin_a"), ALU.mult)
                    dve.drain()
                    for g in range(4):
                        r = slice(32 * g, 32 * g + 32)
                        v.tensor_tensor(q_a[64:96, 4 * j + g, CTX:T], t1[r, CTX:T], t2[r, CTX:T], ALU.add)
                        v.tensor_copy(q_a[64:96, 4 * j + g, 0:CTX], stage[r, 0, 0:CTX])
                    dve.drain().then_inc(roped, 1)
                dve.wait_ge(raw_kept, l * 11 + 3)
                v.tensor_tensor(t1[64:96, CTX:T], stage[64:96, 0, CTX:T], c_("cos_a", slice(64, 96)), ALU.mult)
                v.tensor_tensor(t2[64:96, CTX:T], stage[96:128, 0, CTX:T], c_("sin_a", slice(96, 128)), ALU.mult)
                dve.drain()
                v.tensor_tensor(k_a[64:96, 0, CTX:T], t1[64:96, CTX:T], t2[64:96, CTX:T], ALU.add)
                v.tensor_copy(k_a[64:96, 0, 0:CTX], stage[64:96, 0, 0:CTX])
                dve.drain()
                dve.wait_ge(past_loaded, l * 64 + 32)
                for h in range(1, H_A):
                    v.tensor_copy(k_a[64:96, h, :], k_a[64:96, 0, :])
                dve.drain().then_inc(roped, 1)
                dve.wait_ge(ckv_stored, l * 16 + 16)
                for i in range(3):
                    use = FIRST_USE["kvv"] + i
                    wait_ready(dve, l, use)
                    t, b, _ = buf(use)
                    v.tensor_copy(v_a[:, 2 * i:2 * i + 2, :], t[:, :, :]).then_inc(free[b], 1)
                dve.drain().then_inc(v_copied, 1)

                def out_a(h):
                    r = slice(64 * (h % 2), 64 * (h % 2) + 64)
                    return o_a[r, h // 2, CTX:T], o_a[r, h // 2, 0:CTX], V_A
                attend(l, "ma", 1, 0, 0, H_A, prob_a, 0, out_a)
                for k in range(4):
                    dve.drain().then_inc(whole, 1)
                    dve.drain()
                for k in range(4):
                    remainder(l, "oa", k, oa_lo[:, k, :], o_a[:, k, :], oa_hi[:, k, :])
                merge(l, "merge_a", 8, False)

                for m in range(8):
                    dve.wait_ge(raw_kept, l * 11 + 3 + m + 1)
                    dst = q_d[:, m, :] if m < 4 else k_d[:, m - 4, :]
                    src = stage[:, m % 2, :]
                    v.tensor_tensor(t1[:, CTX:T], src[:, CTX:T], c_("cos_d"), ALU.mult)
                    for g in range(4):
                        r, o = slice(32 * g, 32 * g + 32), slice(32 * (g ^ 1), 32 * (g ^ 1) + 32)
                        v.tensor_tensor(t2[o, CTX:T], src[r, CTX:T], c_("sin_d", r), ALU.mult)
                    v.tensor_copy(dst[:, 0:CTX], src[:, 0:CTX])
                    dve.drain()
                    v.tensor_tensor(dst[:, CTX:T], t1[:, CTX:T], t2[:, CTX:T], ALU.add)
                    dve.drain().then_inc(roped, 1)
                def out_d(h):
                    return q_d[:, h, CTX:T], q_d[:, h, 0:CTX], DV_D
                attend(l, "da", 2, 40, 8, H_D, prob_d, 40, out_d)
                for h in range(H_D):
                    dve.drain().then_inc(src_ready, 1)
                    dve.drain()
                for h in range(H_D):
                    dve.wait_ge(rs_ready, l * N_NORMS + NORMS["dn"] + h + 1)
                    v.scalar_tensor_tensor(q_d[:, h, :], q_d[:, h, :], g_diff[:, h:h + 1], rs[:, :], ALU.mult,
                                           ALU.mult).then_inc(whole, 1)
                    dve.drain().then_inc(rs_used, 1)
                    remainder(l, "od", h, od_lo[:, h, :], q_d[:, h, :], od_hi[:, h, :])
                merge(l, "merge_d", 16, False)

                for k in range(KD):
                    dve.drain().then_inc(whole, 1)
                    dve.drain()
                for k in range(KD):
                    dve.wait_ge(hi_done, l * SPLITS + FIRST_SPLIT["y"] + k + 1)
                    v.scalar_tensor_tensor(act_lo[:, k, :], y[:, k, :], 0.5, act_hi[:, k, :].bitcast(f32), ALU.mult,
                                           ALU.subtract).then_inc(lo_done, 1)

                def add_to_x(l, use, m, gate, more=0):
                    wait_ready(dve, l, use, more)
                    t, b, _ = buf(use)
                    for n, (g, h, a, z) in enumerate(PARTS):
                        o = h * HALF
                        last = v.scalar_tensor_tensor(x[:, m, o + a:o + z], t[:, h, a:z],
                                                      mod[:, 8 * gate + m, g:g + 1], x[:, m, o + a:o + z],
                                                      ALU.mult, ALU.add)
                    return last.then_inc(free[b], 1)
                for m in range(KD):
                    add_to_x(l, FIRST_USE["wout"] + m, m, 2)
                    dve.drain().then_inc(src_ready, 1)
                norm_apply(l, "h2", NORMS["norm2"], scale2, mod[:, 24:32, :])

                with dve.Fori(0, FF_CHUNKS) as c:
                    for m in range(9):
                        if m < 8:
                            dve.wait_ge(relu_ready, l * 32 + c * 8 + (m + 1))
                            v.tensor_tensor(stage[:, m % 2, :], sq[:, m % 2, :], sq[:, m % 2, :], ALU.mult)\
                                .then_inc(whole, 1)
                            dve.drain().then_inc(relu_used, 1)
                        if m:
                            remainder(l, "ff", m - 1, ff_lo[:, m - 1, :], stage[:, (m - 1) % 2, :],
                                      ff_hi[:, m - 1, :], c * 8)
                            dve.drain()
                    for m in range(8):
                        add_to_x(l, FIRST_USE["ff"] + 8 + m, m, 5, c * 8)
                dve.drain().then_inc(layer_open, 1)
            dve.wait_ge(rs_ready, DEPTH * N_NORMS + 1)
            for k in range(KD):
                v.scalar_tensor_tensor(x[:, k, :], x[:, k, :], s_("fin")[:, k:k + 1], rs[:, :], ALU.mult, ALU.mult)\
                    .then_inc(y_final, 1)


def _tiles(w, k0=None):
    kk, n = w.shape
    return w.reshape(kk // P, P, n // P, P).transpose(2, 1, 0, 3)


def _wide(w):
    kk, n = w.shape
    return w.reshape(kk // 256, 2, P, n // 512, 512).transpose(3, 0, 2, 1, 4).reshape(-1, P, BLK)


def _pairs(tiles):
    m, _, k, _ = tiles.shape
    s = tiles.transpose(0, 2, 1, 3).reshape(m * k // 8, 8, P, P)
    return s.transpose(0, 2, 1, 3).reshape(-1, P, BLK)


def _swap(w, n):
    s = w.reshape(w.shape[0], -1, 2, n // 2)[:, :, ::-1, :]
    return s.reshape(w.shape)


def _blocks(i, l):
    w = i["w_in"][l]
    cut = np.cumsum([256, 256, 512, 512, 16, 384, 256, 32, 512, 512, 512])
    mq, mk, mv, mo, mg, acq, ckv, kr, dq, dk, dv, gates = np.split(w, cut, axis=1)
    mgp = np.zeros((D, P), w.dtype)
    for n in range(4):
        mgp[:, 32 * n:32 * n + 4] = mg[:, 4 * n:4 * n + 4]
    krp = np.zeros((D, P), w.dtype)
    krp[:, 64:96], krp[:, 96:128] = kr, _swap(kr, ROPE)
    qu = i["mla_w_q_up"][l].reshape(Q_RANK, H_A, NOPE + ROPE)
    qn, qr = qu[:, :, :NOPE].reshape(Q_RANK, -1), qu[:, :, NOPE:].reshape(Q_RANK, -1)
    qs = _swap(qr, ROPE)
    qall = np.concatenate([qn, qr[:, :P], qs[:, :P], qr[:, P:], qs[:, P:]], axis=1)
    ku = i["mla_w_kv_up"][l].reshape(KV_RANK, H_A, NOPE + V_A)
    kn, kv = ku[:, :, :NOPE].reshape(KV_RANK, -1), ku[:, :, NOPE:].reshape(KV_RANK, -1)

    def merge(g, br):
        gt, bt = _pairs(_tiles(gates[:, D * g:D * g + D])), _pairs(_tiles(br))
        return [b for p in range(4) for b in (gt[2 * p], gt[2 * p + 1], bt[p])]
    f1, f2 = _pairs(_tiles(i["w_ff1"][l])), i["w_ff2"][l]
    out = [_wide(i["w_mod"][l]), _wide(mv)]
    out += [_pairs(_tiles(a)) for a in (mq, mk, mo, mgp)]
    out += [merge(0, i["w_br_mlstm"][l])]
    out += [_pairs(_tiles(a)) for a in (acq, ckv, qall, krp, kn)] + [_wide(kv)]
    out += [merge(1, i["w_br_mla"][l]), _wide(dv), _pairs(_tiles(dq)), _pairs(_tiles(dk))]
    out += [merge(2, i["w_br_diff"][l]), _pairs(_tiles(i["w_out"][l]))]
    for c in range(FF_CHUNKS):
        out += [f1[8 * c:8 * c + 8], _pairs(_tiles(f2[D * c:D * c + D]))]
    return np.concatenate([np.stack(o) if isinstance(o, list) else o for o in out])


def _columns_of(a):
    return a.reshape(-1, P).T


def _small(i, l):
    s = np.zeros((P, SMALL_W), np.float32)

    def put(name, a, r=slice(0, P)):
        s[r, SMALL[name][0]:SMALL[name][1]] = a
    for name, key in (("bmod", "b_mod"), ("n1", "norm1_g"), ("n2", "norm2_g"), ("ng_m", "mlstm_norm_g"),
                      ("ng_q", "mla_q_norm_g"), ("ng_kv", "mla_kv_norm_g"), ("ng_d", "diff_norm_g")):
        put(name, _columns_of(i[key][l]))
    put("fin", _columns_of(i["final_norm_g"]))
    gb = i["mlstm_gate_b"][l].reshape(2, 2, H_M)
    m0 = i["state_mlstm_m"][0, l]
    for d in range(2):
        r = slice(32 * d, 32 * d + H_M)
        s[r, SMALL["gb"][0]] = gb[0, d]
        s[64 + 32 * d:64 + 32 * d + H_M, SMALL["gb"][0] + 1] = gb[1, d]
        s[r, SMALL["m0row"][0]] = m0[d]
    put("m0", m0.reshape(1, UNITS))
    put("lam", i["diff_lambda"][l].reshape(1, 256))
    lam_init = 0.8 - 0.6 * math.exp(-0.3 * l)
    put("lam_init", np.array([[lam_init, 1.0 - lam_init]], np.float32))
    n0, c0 = np.zeros((P, 4, ROWS), np.float32), np.zeros((P, 4, DV_M), np.float32)
    for u in range(UNITS):
        d, h, par, pair, row = unit(u)
        n0[par:par + 64, 2 * d + pair, row] = i["state_mlstm_n"][0, l, d, h]
        c0[par:par + 64, 2 * d + pair] = i["state_mlstm_C"][0, l, d, h]
    put("n0", n0.reshape(P, -1))
    put("C0", c0.reshape(P, -1))
    return s


def _past(i, l):
    s = np.zeros((P, PAST_W), np.float32)

    def features(a):
        return a.T.reshape(-1, P, a.shape[0]).transpose(1, 0, 2).reshape(P, -1)
    s[:, PAST_C["ckv"][0]:PAST_C["ckv"][1]] = features(i["cache_mla_ckv"][0, l])
    s[64:96, PAST_C["kr"][0]:PAST_C["kr"][1]] = i["cache_mla_krope"][0, l].T
    s[:, PAST_C["dk"][0]:PAST_C["dk"][1]] = features(i["cache_diff_k"][0, l].reshape(PAST, -1))
    s[:, PAST_C["dv"][0]:PAST_C["dv"][1]] = i["cache_diff_v"][0, l].reshape(PAST, -1)
    return s


def _constants():
    s = np.zeros((P, CONST_W), np.float32)

    def put(name, a, r=slice(0, P)):
        s[r, CONST[name][0]:CONST[name][1]] = a
    t = np.arange(LAT)
    row, col = (t // GRID_W).astype(np.float32), (t % GRID_W).astype(np.float32)
    for name, dim in (("d", DK_D), ("a", ROPE)):
        quarter = dim // 4
        inv = np.float32(ROPE_BASE) ** (-np.arange(quarter, dtype=np.float32) / np.float32(quarter))
        ang = np.concatenate([row[:, None] * inv, col[:, None] * inv], axis=-1).astype(np.float32)
        c, z = np.cos(ang).T, np.sin(ang).T
        put("cos_" + name, np.tile(np.concatenate([c, c]), (P // dim, 1)))
        sign = [z, -z] if name == "d" else [-z, z]
        put("sin_" + name, np.tile(np.concatenate(sign), (P // dim, 1)))
    p, q = np.arange(P)[:, None], np.arange(P)[None, :]
    put("mask_f", np.where(q >= p, 0.0, NEG))
    put("mask_b", np.where(q <= p, 0.0, NEG))
    put("ident", np.eye(P))
    put("ones", 1.0)
    den, rsel = np.zeros((P, UNITS, ROWS)), np.zeros((P, UNITS, P))
    for u in range(UNITS):
        den[:, u, unit(u)[4]] = 1.0
        rsel[unit(u)[4], u, :] = 1.0
    put("den_sel", den.reshape(P, -1))
    put("row_sel", rsel.reshape(P, -1))
    put("eps", EPS)
    return s


def kernel(**inputs):
    import concourse.bacc as bacc
    from concourse.bass_utils import run_bass_kernel_spmd as run

    i = {k: np.asarray(v) for k, v in inputs.items()}
    f32 = mybir.dt.float32
    tokens = np.concatenate([i["x_prompt"][0], i["x_sample"][0]])
    arrays = {
        "in_x": np.ascontiguousarray(tokens.reshape(T, KD, P).transpose(2, 1, 0)),
        "in_cond": np.ascontiguousarray(np.stack([i["c_ctx"], i["c"][0]]).reshape(2, KD, P).transpose(2, 1, 0)),
        "in_const": _constants(),
        "in_small": np.stack([_small(i, l) for l in range(DEPTH)]),
        "in_past": np.stack([_past(i, l) for l in range(DEPTH)]),
        "in_w": np.stack([_blocks(i, l) for l in range(DEPTH)]),
    }
    outs = {"out_y": (P, KD, T), "out_ckv": (DEPTH, P, KKV, CTX), "out_kr": (DEPTH, ROPE, CTX),
            "out_dk": (DEPTH, P, 4, CTX), "out_dv": (DEPTH, CTX, 512), "out_C": (DEPTH, DK_M, UNITS, DV_M),
            "out_n": (DEPTH, DK_M, UNITS), "out_m": (DEPTH, UNITS, 1)}
    nc = bacc.Bacc("TRN2", target_bir_lowering=False, num_devices=1, dynamic_dma_scratch_size=1024)
    args = [nc.dram_tensor(n, a.shape, f32, kind="ExternalInput").ap() for n, a in arrays.items()]
    args += [nc.dram_tensor(n, s, f32, kind="ExternalOutput").ap() for n, s in outs.items()]
    trunk(nc, *args)
    r = run(nc, [arrays], core_ids=[0]).results[0]

    y = r["out_y"].transpose(2, 1, 0).reshape(T, D)
    ckv = r["out_ckv"].transpose(0, 3, 2, 1).reshape(1, DEPTH, CTX, KV_RANK)
    kr = r["out_kr"].transpose(0, 2, 1)[None]
    dk = r["out_dk"].transpose(0, 3, 2, 1).reshape(1, DEPTH, CTX, H_D, 2 * DK_D)
    dv = r["out_dv"].reshape(1, DEPTH, CTX, H_D, DV_D)
    c_new = r["out_C"].transpose(0, 2, 1, 3).reshape(1, DEPTH, 2, H_M, DK_M, DV_M)
    n_new = r["out_n"].transpose(0, 2, 1).reshape(1, DEPTH, 2, H_M, DK_M)
    m_new = r["out_m"].reshape(1, DEPTH, 2, H_M)
    return y[None, :CTX], y[None, CTX:], ckv, kr, dk, dv, c_new, n_new, m_new
```

```python
import math
from contextlib import ExitStack

import numpy as np

import concourse.bass as bass
from concourse import mybir

D = 1024
CTX, LAT, PAST = 128, 512, 128
DEPTH = 2
T = CTX + LAT
TK = T + PAST
HALF = T // 2
P = 128
KD = D // P
H_M, DK_M, DV_M = 4, 64, 128
H_A, NOPE, ROPE, V_A = 8, 64, 32, 64
Q_RANK, KV_RANK = 384, 256
KQ, KKV = Q_RANK // P, KV_RANK // P
H_D, DK_D, DV_D = 4, 64, 128
D_FF = 4 * D
EPS = 1e-6
GRID_W = 64
ROPE_BASE = 10000.0
UNITS = 2 * H_M
ROWS = 32 + H_M
BLK = 1024

MOD_BLOCKS = 6 * D * KD // BLK
MOD_CHUNKS = 6 * D // 512
FF_CHUNKS = 4
STAGES = [("mv", 4), ("mg", 1), ("mq", 2), ("mk", 2), ("mo", 4), ("acq", 3), ("merge_m", 12), ("ckv", 2), ("qup", 3), ("kr", 1), ("kvn", 1), ("kvv", 1), ("merge_a", 12),
          ("dv", 4), ("dq", 4), ("dk", 4), ("merge_d", 12), ("wout", 8), ("ff", 64)]
FIRST_BLOCK, DENSE = {}, 0
for _name, _n in STAGES:
    FIRST_BLOCK[_name] = DENSE
    DENSE += _n
BLOCKS = MOD_BLOCKS + DENSE
RAW, SPLIT = 4, 2
assert BLOCKS % RAW == 0 and DENSE % SPLIT == 0
MOD_A, DENSE_A = 16, FIRST_BLOCK["acq"]
RUNS = [("mod", MOD_A - 4), ("dense", SPLIT), ("mod", 4), ("dense", DENSE_A - SPLIT),
        ("mod", MOD_BLOCKS - MOD_A), ("dense", DENSE - DENSE_A)]
PLACES = {"mod": [], "dense": []}
ORDER = []
for _kind, _n in RUNS:
    for _ in range(_n):
        PLACES[_kind].append(len(ORDER))
        ORDER.append((_kind, len(PLACES[_kind]) - 1))
assert len(ORDER) == BLOCKS

USE_STAGES = [("norm1", 1), ("mv", 2), ("mg", 1), ("mq", 2), ("mk", 2), ("mo", 4),
              ("ms", UNITS * 5), ("acq", KQ), ("mr", UNITS), ("merge_m", 16),
              ("qn", 1), ("ckv", KKV), ("kn", 1), ("qup", 8), ("kr", 1), ("kvn", 4), ("kvv", 3),
              ("ma", H_A * 5), ("merge_a", 16),
              ("dv", 2), ("dq", 4), ("dk", 4), ("da", H_D * 10), ("merge_d", 16),
              ("wout", 8), ("norm2", 1), ("ff", 64)]
FIRST_USE, USES = {}, 0
for _name, _n in USE_STAGES:
    FIRST_USE[_name] = USES
    USES += _n
assert USES % 2 == 0

SPLIT_STAGES = [("h1", 8), ("om", 4), ("q", KQ), ("kv", KKV), ("oa", 4), ("od", 4), ("y", 8), ("h2", 8), ("ff", 32)]
FIRST_SPLIT, SPLITS = {}, 0
for _name, _n in SPLIT_STAGES:
    FIRST_SPLIT[_name] = SPLITS
    SPLITS += _n
SQ_STAGES = [("norm1", 8), ("mn", 4), ("qn", KQ), ("kn", KKV), ("dn", 4), ("norm2", 8)]
FIRST_SQ, SQUARES = {}, 0
for _name, _n in SQ_STAGES:
    FIRST_SQ[_name] = SQUARES
    SQUARES += _n
FIRST_SQ_USED, SQ_USED = {}, 0
for _name, _n in SQ_STAGES:
    FIRST_SQ_USED[FIRST_SQ[_name]] = SQ_USED
    SQ_USED += (_n - 1) * (_n > 1) if _name not in ("mn", "dn") else 0
NORMS = {"norm1": 0, "mn": 1, "qn": 5, "kn": 6, "dn": 7, "norm2": 11}
N_NORMS = 12
HEAD_NORMS = {"mn": 0, "dn": 4}

def _columns(parts):
    at, out = 0, {}
    for name, n in parts:
        out[name] = (at, at + n)
        at += n
    return out, at


SMALL, SMALL_W = _columns([("bmod", 48), ("n1", 8), ("n2", 8), ("ng_m", 4), ("ng_q", KQ), ("ng_kv", KKV),
                           ("ng_d", 4), ("gb", 2), ("m0row", 1), ("m0", UNITS), ("lam", 256), ("lam_init", 2),
                           ("fin", 8), ("n0", 4 * ROWS), ("C0", 4 * DV_M)])
CONST, CONST_W = _columns([("cos_d", LAT), ("sin_d", LAT), ("cos_a", LAT), ("sin_a", LAT), ("mask_f", P),
                           ("mask_b", P), ("ident", P), ("ones", P), ("den_sel", UNITS * ROWS),
                           ("row_sel", UNITS * P), ("fold_sel", 4), ("eps", 1)])
PAST_C, PAST_W = _columns([("ckv", KKV * PAST), ("kr", PAST), ("dk", 4 * PAST), ("dv", H_D * DV_D)])
NEG = -1e30


def unit(u):
    d, h = divmod(u, H_M)
    return d, h, 64 * (h % 2), h // 2, 32 * d + h


def trunk(nc, xT, condT, consts, small_d, past_d, w_d, yT, o_ckv, o_kr, o_dk, o_dv, o_C, o_n, o_m):
    f32, f32r = mybir.dt.float32, mybir.dt.float32r
    ALU, ACT, AX = mybir.AluOpType, mybir.ActivationFunctionType, mybir.AxisListType
    ctx = ExitStack()
    with ctx:
        base = [(nc.sbuf_base + 63) // 64 * 64]

        def at(name, shape, offset, dt=f32):
            return nc.alloc_sbuf_tensor_at(name, shape, dt, offset=offset)

        def sb(name, shape, dt=f32):
            off = base[0]
            base[0] += (int(np.prod(shape[1:])) * 4 + 63) // 64 * 64
            return at(name, shape, off, dt)

        def sem(name):
            return ctx.enter_context(nc.semaphore(name))

        x = sb("x", [P, KD, T])
        act_hi, act_lo = sb("act_hi", [P, KD, T], f32r), sb("act_lo", [P, KD, T], f32r)
        raw = sb("raw", [P, RAW, BLK])
        w_hi, w_lo = sb("w_hi", [P, SPLIT, BLK], f32r), sb("w_lo", [P, SPLIT, BLK], f32r)
        y_at = base[0]
        y = sb("y", [P, KD, T])
        num_sb = at("num_sb", [P, UNITS, T], y_at)
        cst = sb("cst", [P, CONST_W])
        small = sb("small", [P, SMALL_W])
        cond = sb("cond", [P, KD, 32])
        mod = sb("mod", [P, 48, 2])
        scale1, scale2 = sb("scale1", [P, KD, 2]), sb("scale2", [P, KD, 2])
        cols = sb("cols", [P, 32])
        mod_row = sb("mod_row", [P, 2, 256])
        rs = sb("rs", [P, T])
        sq = sb("sq", [P, 2, T])
        t1, t2 = sb("t1", [P, T]), sq[:, 1, :]
        stage = sb("stage", [P, 2, T])
        A0 = base[0]
        qm, km = at("qm", [P, 2, T], A0), at("km", [P, 2, T], A0 + 5120)
        vm = at("vm", [P, 5, 512], A0 + 10240)
        om_hi, om_lo = at("om_hi", [P, 4, T], A0, f32r), at("om_lo", [P, 4, T], A0 + 10240, f32r)
        mo_th = at("mo_th", [P, 4, T], A0 + 20480)
        ebuf, abuf = at("ebuf", [P, 2, 512], A0 + 30720), at("abuf", [P, 2, 512], A0 + 34816)
        nMbc, qw = at("nMbc", [P, T], A0 + 38912), at("qw", [P, 512], A0 + 41472)
        rows = [at(f"row{i}", [ROWS, T], A0 + 43520 + 2560 * i) for i in range(6)]
        acol = at("acol", [P, 5, ROWS], A0 + 58880)
        ktok, kw = at("ktok", [P, 256], A0 + 59648), at("kw", [P, UNITS, DK_M], A0 + 60672)
        c_new, n_new = at("c_new", [DK_M, UNITS, DV_M], A0 + 62720), at("n_new", [DK_M, UNITS], A0 + 66816)
        q_a, o_a = at("q_a", [96, H_A, T], A0), at("o_a", [P, 4, T], A0)
        k_a = at("k_a", [96, H_A, TK], A0 + 20480)
        qn_hi, qn_lo = at("qn_hi", [P, KQ, T], A0 + 20480, f32r), at("qn_lo", [P, KQ, T], A0 + 28160, f32r)
        acq = at("acq", [P, KQ, T], A0 + 35840)
        oa_hi, oa_lo = at("oa_hi", [P, 4, T], A0 + 20480, f32r), at("oa_lo", [P, 4, T], A0 + 30720, f32r)
        v_a, ckv = at("v_a", [P, 6, 512], A0 + 45056), at("ckv", [P, KKV, TK], A0 + 45056)
        ckv_hi, ckv_lo = at("ckv_hi", [P, KKV, TK], A0 + 57344, f32r), at("ckv_lo", [P, KKV, TK], A0 + 63488, f32r)
        prob_a = at("prob_a", [P, 2, T], A0 + 57344)
        probT_a = at("probT_a", [P, 2, 5, P], A0 + 62464)
        q_d, k_d = at("q_d", [P, 4, T], A0), at("k_d", [P, 4, TK], A0 + 10240)
        v_d = at("v_d", [P, 6, 512], A0 + 22528)
        prob_d = at("prob_d", [P, 4, T], A0 + 34816)
        probT_d = at("probT_d", [P, 2, 5, P], A0 + 45056)
        od_hi, od_lo = at("od_hi", [P, 4, T], A0 + 10240, f32r), at("od_lo", [P, 4, T], A0 + 20480, f32r)
        ff_hi, ff_lo = at("ff_hi", [P, 8, T], A0, f32r), at("ff_lo", [P, 8, T], A0 + 20480, f32r)

        big = [ctx.enter_context(nc.psum_tensor(f"big{b}", [P, 2, 512], f32)) for b in range(2)]
        two = ctx.enter_context(nc.psum_tensor("two", [P, 2, 512], f32))
        last_two = ctx.enter_context(nc.psum_tensor("last_two", [P, 2, 512], f32))
        one = [last_two[:, b, :] for b in range(2)]

        def c_(name, rows_=slice(0, P)):
            return cst[rows_, CONST[name][0]:CONST[name][1]]

        def s_(name, rows_=slice(0, P)):
            return small[rows_, SMALL[name][0]:SMALL[name][1]]

        ones, ident = c_("ones"), c_("ident")
        eps, fold_sel = c_("eps"), c_("fold_sel")
        den_sel = c_("den_sel").rearrange("p (u r) -> p u r", r=ROWS)
        row_sel = c_("row_sel", slice(0, ROWS)).rearrange("p (u c) -> p u c", c=P)
        n0 = s_("n0").rearrange("p (a r) -> p a r", r=ROWS)
        C0 = s_("C0").rearrange("p (a e) -> p a e", e=DV_M)
        g_half, g_diff, neg_lam = cols[:, 0:4], cols[:, 4:8], cols[:, 8:9]
        lam_tmp = cols[:, 9:12]
        neg_max, row_sum = cols[:, 12:16], cols[:, 16:20]

        raw_loaded = [sem(f"raw_loaded{i}") for i in range(RAW)]
        mod_block_used = sem("mod_block_used")
        split_ready, block_used = sem("split_ready"), sem("block_used")
        ready, free = [sem("ready_a"), sem("ready_b")], [sem("free_a"), sem("free_b")]
        x_loaded, cst_loaded, small_loaded = sem("x_loaded"), sem("cst_loaded"), sem("small_loaded")
        layer_open, started = sem("layer_open"), sem("started")
        cond_done = sem("cond_done")
        row_ready, row_copied, row_free = sem("row_ready"), sem("row_copied"), sem("row_free")
        silu_done, mod_kept = sem("silu_done"), sem("mod_kept")
        den_read = sem("den_read")
        head_sum, head_sum_free = sem("head_sum"), sem("head_sum_free")
        sq_ready, sq_used = sem("sq_ready"), sem("sq_used")
        rs_ready, rs_used = sem("rs_ready"), sem("rs_used")
        whole, hi_done, lo_done = sem("whole"), sem("hi_done"), sem("lo_done")
        src_ready = sem("src_ready")
        vm_ready, qk_ready, mo_ready = sem("vm_ready"), sem("qk_ready"), sem("mo_ready")
        gate_rows, soft_rows, rows_ready, expm_ready = sem("gate_rows"), sem("soft_rows"), sem("rows_ready"), sem("expm_ready")
        colsT_ready, colsT_copied = sem("colsT_ready"), sem("colsT_copied")
        bc_ready, bc_copied, w_inter_ready, qw_ready = sem("bc_ready"), sem("bc_copied"), sem("w_inter_ready"), sem("qw_ready")
        arg_ready, e_ready, a_ready, a_used = sem("arg_ready"), sem("e_ready"), sem("a_ready"), sem("a_used")
        num_ready, num_copied = sem("num_ready"), sem("num_copied")
        kw_ready, state_ready, state_copied = sem("kw_ready"), sem("state_ready"), sem("state_copied")
        rden_ready = sem("rden_ready")
        gate_ready, y_done = sem("gate_ready"), sem("y_done")
        past_loaded = sem("past_loaded")
        raw_kept, roped = sem("raw_kept"), sem("roped")
        kv_norm_done, k_rope_done, kn_copied = sem("kv_norm_done"), sem("k_rope_done"), sem("kn_copied")
        qnope_copied, v_copied = sem("qnope_copied"), sem("v_copied")
        maxed, exped, p_ready = sem("maxed"), sem("exped"), sem("p_ready")
        pT_ready, pT_copied, o_ready, o_copied = sem("pT_ready"), sem("pT_copied"), sem("o_ready"), sem("o_copied")
        relu_ready, relu_used = sem("relu_ready"), sem("relu_used")
        x_updated, y_final = sem("x_updated"), sem("y_final")
        stored, state_stored, ckv_stored = sem("stored"), sem("state_stored"), sem("ckv_stored")
        kr_stored, diff_stored = sem("kr_stored"), sem("diff_stored")
        lam_sums, lam_exps = sem("lam_sums"), sem("lam_exps")

        def buf(i):
            return big[i % 2], i % 2, i // 2

        def wait_free(pe, l, i, more=0):
            pe.wait_ge(free[i % 2], l * (USES // 2) + more + i // 2 + 1)

        def wait_ready(e, l, i, more=0):
            e.wait_ge(ready[i % 2], l * (USES // 2) + more + i // 2 + 1)

        def halves(t, n=HALF):
            return t[:, :, 0:n]

        def two_parts(ap, n=HALF):
            return ap.rearrange("p (a t) -> p a t", t=n)

        PARTS = [(0, 0, 0, CTX), (1, 0, CTX, HALF), (1, 1, 0, HALF)]
        GROUPS = [(0, 0, CTX), (1, CTX, T)]
        ATT = [(h, t) for h in range(H_A) for t in range(5)]
        LATE = 4

        def keys(t):
            return (0, CTX) if t == LATE else (CTX, TK)

        def queries(t):
            return (0, CTX) if t == LATE else (CTX + P * t, CTX + P * t + P)

        block = ctx.enter_context(nc.Block())

        @block.sync
        def _(sp):
            sp.dma_start(x[:, :, :], xT).then_inc(x_loaded, 16)
            sp.wait_ge(started, 1)
            with sp.Fori(0, DEPTH) as l:
                place = 0
                for kind, n in RUNS:
                    def load(place, i):
                        of_kind, index = ORDER[place - RAW]
                        index -= DENSE if place < RAW else 0
                        if of_kind == "mod":
                            sp.wait_ge(mod_block_used, l * MOD_BLOCKS + i + (index + 1))
                        else:
                            sp.wait_ge(split_ready, l * DENSE + i + (index + 1 + RAW))
                        slot = place % RAW
                        sp.dma_start(raw[:, slot, :], w_d[l, i + place]).then_inc(raw_loaded[slot], 16)
                    head = min(n, RAW)
                    for j in range(head):
                        load(place + j, 0)
                    if n >= 2 * RAW:
                        with sp.Fori(0, n // RAW - 1) as i:
                            for j in range(RAW):
                                load(place + RAW + j, i * RAW)
                        head = n // RAW * RAW
                    for j in range(head, n):
                        load(place + j, 0)
                    place += n
            sp.wait_ge(y_final, KD)
            sp.dma_start(yT, x[:, :, :]).then_inc(stored, 16)
            sp.wait_ge(stored, 16)

        @block.gpsimd
        def _(pool):
            pool.wait_ge(cst_loaded, 32)
            with pool.Fori(0, DEPTH) as l:
                def split(block, i):
                    place, to = PLACES["dense"][block], block % SPLIT
                    slot = place % RAW
                    pool.wait_ge(raw_loaded[slot], l * (16 * BLOCKS // RAW) + i * 16 + 16 * (place // RAW + 1))
                    pool.wait_ge(block_used, l * DENSE + i * RAW + (block + 1))
                    nc.gpsimd.tensor_tensor(w_hi[:, to, :], raw[:, slot, :],
                                            ones[:, 0:1].to_broadcast([P, BLK]), ALU.mult)
                    pool.drain()
                    nc.gpsimd.tensor_tensor(w_lo[:, to, :], raw[:, slot, :], w_hi[:, to, :].bitcast(f32),
                                            ALU.subtract).then_inc(split_ready, 1)
                block = 0
                for n in [n for kind, n in RUNS if kind == "dense"]:
                    looped = n // RAW * RAW
                    if looped:
                        with pool.Fori(0, n // RAW) as i:
                            for j in range(RAW):
                                split(block + j, i)
                    for j in range(looped, n):
                        split(block + j, 0)
                    block += n

        @block.tensor
        def _(pe):
            mm = nc.tensor.matmul

            def block_start(l, b, more=0):
                pe.wait_ge(split_ready, l * DENSE + more + (b + 1 + RAW))

            def project(l, first_use, first_block, tiles, nk, hi, lo, n=HALF, arrived=None, more_b=0, more_u=0):
                for p in range(tiles * nk):
                    m, k = divmod(p, nk)
                    b, q = divmod(p, 8)
                    slot, col = (first_block + b) % SPLIT, P * q
                    if q == 0:
                        block_start(l, first_block + b, more_b)
                    t, _, _ = buf(first_use + m)
                    if k == 0:
                        wait_free(pe, l, first_use + m, more_u)
                    if arrived is not None and m == 0:
                        pe.wait_ge(lo_done, arrived(k))
                    for h in range(2):
                        ps = t[:, h, 0:n]
                        wh, wl = w_hi[:, slot, col:col + P], w_lo[:, slot, col:col + P]
                        ah, al = hi[:, k, h * n:h * n + n], lo[:, k, h * n:h * n + n]
                        first = mm(ps, wh, ah, start=k == 0, stop=False)
                        if q == 0 and h == 0:
                            first.then_inc(block_used, 1)
                        mm(ps, wh, al, start=False, stop=False)
                        last = mm(ps, wl, ah, start=False, stop=k == nk - 1)
                    if k == nk - 1:
                        last.then_inc(ready[(first_use + m) % 2], 1)

            def project_tokens(l, first_use, first_block, arrived=None):
                wait_free(pe, l, first_use)
                wait_free(pe, l, first_use + 1)
                outs = [big[0][:, 0, :], big[0][:, 1, :], big[1][:, 0, :], big[1][:, 1, :], two[:, 0, :]]
                for b in range(4):
                    block_start(l, first_block + b)
                    slot = (first_block + b) % SPLIT
                    if arrived is not None:
                        pe.wait_ge(lo_done, arrived(2 * b + 1))
                    for t in range(5):
                        for kk in range(2):
                            k = 2 * b + kk
                            wh, wl = w_hi[:, slot, 512 * kk:512 * kk + 512], w_lo[:, slot, 512 * kk:512 * kk + 512]
                            ah, al = act_hi[:, k, P * t:P * t + P], act_lo[:, k, P * t:P * t + P]
                            first = mm(outs[t], ah, wh, start=k == 0, stop=False)
                            if t == 0 and kk == 0 and first_block + b:
                                first.then_inc(block_used, 1)
                            mm(outs[t], al, wh, start=False, stop=False)
                            last = mm(outs[t], ah, wl, start=False, stop=k == KD - 1)
                        if b == 3 and t in (1, 4):
                            last.then_inc(ready[t // 4], 1)

            def sums(l, use, first_sq, n, per_layer=SQUARES, off=0):
                wait_free(pe, l, use, off)
                for k in range(n):
                    sum_step(l, use, first_sq, n, k)

            def sum_step(l, use, first_sq, n, k):
                t, b, _ = buf(use)
                pe.wait_ge(sq_ready, l * SQUARES + first_sq + k + 1)
                for h in range(2):
                    last = mm(t[:, h, 0:HALF], ones, sq[:, k % 2, h * HALF:(h + 1) * HALF],
                              start=k == 0, stop=k == n - 1)
                last.then_inc(ready[b] if k == n - 1 else sq_used, 1)

            def head_sums(l, name, heads):
                for h in heads:
                    n = HEAD_NORMS[name] + h
                    pe.wait_ge(sq_ready, l * SQUARES + FIRST_SQ[name] + h + 1)
                    if h >= 2:
                        pe.wait_ge(head_sum_free, l * 8 + n - 1)
                    for a in range(2):
                        last = mm((two, last_two)[h % 2][:, a, 0:HALF], ones, sq[:, h % 2, a * HALF:(a + 1) * HALF],
                                  start=True, stop=True)
                    last.then_inc(head_sum, 1)

            def mod_rows(l, c, out):
                for q in range(4):
                    place = PLACES["mod"][4 * c + q]
                    pe.wait_ge(raw_loaded[place % RAW], l * (16 * BLOCKS // RAW) + 16 * (place // RAW + 1))
                    for kk in range(2):
                        for half in range(2):
                            r = 32 * (2 * half + kk)
                            a = 512 * kk + 256 * half
                            last = mm(out[r:r + 32, :], cond[:, 2 * q + kk, :], raw[:, place % RAW, a:a + 256],
                                      start=q == 0, stop=q == 3)
                            if c + q + kk + half == 0:
                                last.then_inc(block_used, 1)
                    last.then_inc(row_ready if q == 3 else mod_block_used, 1)

            def mod_fold(l, c, out):
                pe.wait_ge(row_copied, l * MOD_CHUNKS + c + 1)
                for j in range(4):
                    half = j // 2
                    last = mm(out[:, 2 * j:2 * j + 2], mod_row[:, c % 2, P * (j % 2):P * (j % 2) + P],
                              fold_sel[:, 2 * half:2 * half + 2], start=True, stop=True)
                    if j == 0:
                        last.then_inc(mod_block_used, 1)
                last.then_inc(row_free, 1)

            def merge(l, name, o_hi, o_lo, split_name, head_norm=None):
                for p in range(4):
                    u, b = FIRST_USE[name] + 4 * p, FIRST_BLOCK[name] + 3 * p
                    for g in range(2):
                        if head_norm and p == 0:
                            head_sums(l, head_norm, (2 * g, 2 * g + 1))
                        project(l, u + g, b + g, 1, KD, act_hi, act_lo)
                    project(l, u + 2, b + 2, 2, 4, o_hi, o_lo,
                            arrived=(lambda k: l * SPLITS + FIRST_SPLIT[split_name] + k + 1) if p == 0 else None)

            def attend(l, name, maps, unit0, head0, q_of, k_of, v_of, heads, prob, probT):
                units = [(h, t) for h in range(heads) for t in range(5)]

                def scores(i):
                    h, t = units[i]
                    q0, q1 = queries(t)
                    k0, k1 = keys(t)
                    for m in range(maps):
                        use = FIRST_USE[name] + maps * i + m
                        wait_free(pe, l, use)
                        ps, b, _ = buf(use)
                        n = (k1 - k0) // (1 if t == LATE else 2)
                        for c in range((k1 - k0) // n):
                            last = mm(ps[:, c, 0:n], q_of(h, m)[:, q0:q1], k_of(h, m)[:, k0 + c * n:k0 + c * n + n],
                                      start=True, stop=True)
                        last.then_inc(ready[b], 1)

                def turn(i):
                    h, t = units[i]
                    pe.wait_ge(p_ready, l * 60 + unit0 + i + 1)
                    if i:
                        pe.wait_ge(pT_copied, l * 60 + unit0 + i)
                    src = prob[:, maps * (i % 2), :]
                    for c in range(1 if t == LATE else 5):
                        out = two[:, 0, P * c:P * c + P] if c < 4 else two[:, 1, 0:P]
                        last = nc.tensor.transpose(out, src[:, P * c:P * c + P], ident)
                    last.then_inc(pT_ready, 1)

                def values(i):
                    h, t = units[i]
                    pe.wait_ge(pT_copied, l * 60 + unit0 + i + 1)
                    if h and t in (0, LATE):
                        pe.wait_ge(o_copied, l * 24 + 2 * (head0 + h) - (t == 0))
                    m = v_of(h, 0).shape[-1]
                    if t == LATE:
                        last = mm(one[1][0:m, 0:CTX], v_of(h, 0), probT[:, i % 2, 0, :], start=True, stop=True)
                    else:
                        for c in range(5):
                            last = mm(one[0][0:m, P * t:P * t + P], v_of(h, c + 1), probT[:, i % 2, c, :],
                                      start=c == 0, stop=c == 4)
                    last.then_inc(o_ready, 1)

                n = len(units)
                for i in range(-1, n + 2):
                    if i + 1 < n:
                        scores(i + 1)
                    if 0 <= i - 1 < n:
                        turn(i - 1)
                    if 0 <= i - 2:
                        values(i - 2)

            pe.wait_ge(cst_loaded, 32)
            pe.wait_ge(started, 1)
            with pe.Fori(0, DEPTH) as l:
                pe.wait_ge(silu_done, 1)
                wait_free(pe, l, FIRST_USE["norm1"])
                for c in range(MOD_A // 4 + 1):
                    if c < MOD_A // 4:
                        mod_rows(l, c, two[:, c % 2, 0:256])
                    if c:
                        mod_fold(l, c - 1, one[0][:, 8 * c - 8:8 * c])
                        for k in (2 * c - 2, 2 * c - 1):
                            sum_step(l, FIRST_USE["norm1"], FIRST_SQ["norm1"], KD, k)

                def h_arrived(k):
                    return l * SPLITS + FIRST_SPLIT["h1"] + k + 1
                project_tokens(l, FIRST_USE["mv"], FIRST_BLOCK["mv"], h_arrived)
                for name, n in (("mg", 1), ("mq", 2), ("mk", 2), ("mo", 4)):
                    project(l, FIRST_USE[name], FIRST_BLOCK[name], n, KD, act_hi, act_lo)

                pe.wait_ge(vm_ready, l + 1)
                mod_rows(l, 4, two[:, 0, 0:256])
                mod_fold(l, 4, one[1][:, 256:264])
                pe.wait_ge(qk_ready, l + 1)
                pe.wait_ge(rows_ready, l + 1)
                for t in range(5):
                    mm(two[:, 1, ROWS * t:ROWS * t + ROWS], rows[0][:, P * t:P * t + P], ident[0:ROWS, 0:ROWS],
                       start=True, stop=True)
                for j in range(2):
                    last = mm(two[:, 0, P * j:P * j + P], km[:, j, 0:CTX], ident, start=True, stop=True)
                last.then_inc(colsT_ready, 1)

                def broadcast(u):
                    if u == 0:
                        pe.wait_ge(colsT_copied, l + 1)
                    else:
                        pe.wait_ge(bc_copied, l * UNITS + u)
                    mm(two[:, 0, :], row_sel[:, u, :], rows[4][:, CTX:T], start=True, stop=True)
                    mm(two[:, 1, 0:CTX], row_sel[:, u, :], rows[4][:, 0:CTX], start=True, stop=True)\
                        .then_inc(bc_ready, 1)

                def span(u, j):
                    if j == LATE:
                        return 0, CTX
                    return (CTX + P * j, T) if u < H_M else (CTX, CTX + P * (j + 1))

                def m_scores(i):
                    u, j = divmod(i, 5)
                    _, h, par, pair, _ = unit(u)
                    s0, _ = queries(j)
                    q0, q1 = span(u, j)
                    use = FIRST_USE["ms"] + i
                    wait_free(pe, l, use)
                    t, b, _ = buf(use)
                    mm(t[:, 0, 0:q1 - q0], km[par:par + 64, pair, s0:s0 + P], qm[par:par + 64, pair, q0:q1],
                       start=True, stop=True).then_inc(ready[b], 1)

                def m_values(i):
                    u, j = divmod(i, 5)
                    d, h, par, pair, row = unit(u)
                    if j == 0:
                        pe.wait_ge(qw_ready, l * UNITS + u + 1)
                        if u:
                            pe.wait_ge(num_copied, l * UNITS + u)
                        mm(one[0][:, :], C0[par:par + 64, 2 * d + pair, :], qw[par:par + 64, :], start=True, stop=False)
                        mm(big[0][0:ROWS, 1, :], n0[par:par + 64, 2 * d + pair, :], qw[par:par + 64, :],
                           start=u == 0, stop=False)
                    q0, q1 = span(u, j)
                    pe.wait_ge(a_ready, l * 40 + i + 1)
                    A = abuf[:, i % 2, 0:q1 - q0]
                    v = vm[:, 0 if j == LATE else j + 1, P * h:P * h + P]
                    if j == LATE:
                        mm(one[1][:, 0:CTX], v, A, start=True, stop=True)
                        mm(big[1][0:ROWS, 1, 0:CTX], den_sel[:, u, :], A, start=u == 0, stop=u == UNITS - 1)\
                            .then_inc(num_ready, 1)
                    else:
                        mm(one[0][:, q0 - CTX:q1 - CTX], v, A, start=False, stop=j == 3)
                        mm(big[0][0:ROWS, 1, q0 - CTX:q1 - CTX], den_sel[:, u, :], A, start=False,
                           stop=u == UNITS - 1 and j == 3).then_inc(a_used, 1)

                broadcast(0)
                m_scores(0)
                for i in range(40):
                    if i + 1 < 40:
                        m_scores(i + 1)
                    u = i // 5
                    if i % 5 == 1 and u + 1 < UNITS:
                        pe.wait_ge(bc_copied, l * UNITS + u + 1)
                        mod_rows(l, 5 + u, two[:, 0, 0:256])
                    if i % 5 == 3 and u + 1 < UNITS:
                        mod_fold(l, 5 + u, one[1][:, 264 + 8 * u:272 + 8 * u])
                        broadcast(u + 1)
                    m_values(i)
                pe.wait_ge(kw_ready, l * UNITS + UNITS)
                pe.wait_ge(num_copied, l * UNITS + UNITS)
                pe.wait_ge(mod_kept, l + 1)
                for u in range(UNITS):
                    _, h, _, _, _ = unit(u)
                    mm(two[0:DK_M, u // 4, P * (u % 4):P * (u % 4) + P], kw[:, u, :], vm[:, 0, P * h:P * h + P],
                       start=True, stop=True)
                    last = mm(one[1][0:DK_M, u:u + 1], kw[:, u, :], ones[:, 0:1], start=True, stop=True)
                last.then_inc(state_ready, 1)
                pe.wait_ge(den_read, l + 1)
                project(l, FIRST_USE["acq"], FIRST_BLOCK["acq"], KQ, KD, act_hi, act_lo)
                pe.wait_ge(rden_ready, l + 1)
                for j in range(UNITS):
                    u = j // 2 + H_M * (j % 2)
                    use = FIRST_USE["mr"] + j
                    wait_free(pe, l, use)
                    t, b, _ = buf(use)
                    for h in range(2):
                        last = mm(t[:, h, 0:HALF], row_sel[:, u, :], rows[2][:, h * HALF:(h + 1) * HALF],
                                  start=True, stop=True)
                    last.then_inc(ready[b], 1)
                pe.wait_ge(state_copied, l + 1)
                merge(l, "merge_m", om_hi, om_lo, "om", "mn")

                sums(l, FIRST_USE["qn"], FIRST_SQ["qn"], KQ)
                project(l, FIRST_USE["ckv"], FIRST_BLOCK["ckv"], KKV, KD, act_hi, act_lo)
                sums(l, FIRST_USE["kn"], FIRST_SQ["kn"], KKV)
                project(l, FIRST_USE["qup"], FIRST_BLOCK["qup"], 8, KQ, qn_hi, qn_lo,
                        arrived=lambda k: l * SPLITS + FIRST_SPLIT["q"] + k + 1)
                project(l, FIRST_USE["kr"], FIRST_BLOCK["kr"], 1, KD, act_hi, act_lo)
                project(l, FIRST_USE["kvn"], FIRST_BLOCK["kvn"], 4, KKV, ckv_hi, ckv_lo, n=TK // 2,
                        arrived=lambda k: l * SPLITS + FIRST_SPLIT["kv"] + k + 1)
                block_start(l, FIRST_BLOCK["kvv"])
                slot = FIRST_BLOCK["kvv"] % SPLIT
                for i in range(3):
                    use = FIRST_USE["kvv"] + i
                    wait_free(pe, l, use)
                    ps, b, _ = buf(use)
                    for tt in range(2):
                        t = 2 * i + tt
                        for kk in range(KKV):
                            wh, wl = w_hi[:, slot, 512 * kk:512 * kk + 512], w_lo[:, slot, 512 * kk:512 * kk + 512]
                            ah, al = ckv_hi[:, kk, P * t:P * t + P], ckv_lo[:, kk, P * t:P * t + P]
                            first = mm(ps[:, tt, :], ah, wh, start=kk == 0, stop=False)
                            if t + kk == 0:
                                first.then_inc(block_used, 1)
                            mm(ps[:, tt, :], al, wh, start=False, stop=False)
                            last = mm(ps[:, tt, :], ah, wl, start=False, stop=kk == KKV - 1)
                    last.then_inc(ready[b], 1)
                pe.wait_ge(roped, l * 11 + 3)
                pe.wait_ge(kn_copied, l + 1)
                pe.wait_ge(v_copied, l * 2 + 1)
                attend(l, "ma", 1, 0, 0, lambda h, m: q_a[:, h, :], lambda h, m: k_a[:, h, :],
                       lambda h, c: v_a[:, c, V_A * h:V_A * h + V_A], H_A, prob_a, probT_a)
                merge(l, "merge_a", oa_hi, oa_lo, "oa")

                project_tokens(l, FIRST_USE["dv"], FIRST_BLOCK["dv"])
                project(l, FIRST_USE["dq"], FIRST_BLOCK["dq"], 4, KD, act_hi, act_lo)
                project(l, FIRST_USE["dk"], FIRST_BLOCK["dk"], 4, KD, act_hi, act_lo)
                pe.wait_ge(roped, l * 11 + 11)
                pe.wait_ge(v_copied, l * 2 + 2)
                pe.wait_ge(past_loaded, l * 64 + 64)
                attend(l, "da", 2, 40, 8, lambda h, m: q_d[64 * m:64 * m + 64, h, :],
                       lambda h, m: k_d[64 * m:64 * m + 64, h, :],
                       lambda h, c: v_d[:, c, P * h:P * h + P], H_D, prob_d, probT_d)
                pe.wait_ge(o_copied, l * 24 + 24)
                merge(l, "merge_d", od_hi, od_lo, "od", "dn")

                project(l, FIRST_USE["wout"], FIRST_BLOCK["wout"], 8, KD, act_hi, act_lo,
                        arrived=lambda k: l * SPLITS + FIRST_SPLIT["y"] + k + 1)
                sums(l, FIRST_USE["norm2"], FIRST_SQ["norm2"], KD)
                with pe.Fori(0, FF_CHUNKS) as c:
                    project(l, FIRST_USE["ff"], FIRST_BLOCK["ff"], 8, KD, act_hi, act_lo,
                            arrived=lambda k: l * SPLITS + (FIRST_SPLIT["h2"] + k + 1), more_b=c * 16, more_u=c * 8)
                    project(l, FIRST_USE["ff"] + 8, FIRST_BLOCK["ff"] + 8, 8, KD, ff_hi, ff_lo,
                            arrived=lambda k: l * SPLITS + c * 8 + (FIRST_SPLIT["ff"] + k + 1),
                            more_b=c * 16, more_u=c * 8)
            pe.wait_ge(layer_open, DEPTH + 1)
            sums(DEPTH, 0, 0, KD)

        @block.scalar
        def _(act):
            f = nc.scalar.activation

            def squares(l, first_sq, first_src, tiles, sources_wait=True, only=None):
                for k, ap in enumerate(tiles):
                    if only is not None and k not in only:
                        continue
                    if sources_wait is not None:
                        act.wait_ge(src_ready, sources_wait(k))
                    if k >= 2:
                        act.wait_ge(sq_used, l * SQ_USED + FIRST_SQ_USED[first_sq] + k - 1)
                    f(sq[:, k % 2, :], ap, ACT.Square).then_inc(sq_ready, 1)

            def inverse_root(l, use, norm, n):
                t, b, _ = buf(use)
                act.wait_ge(rs_used, l * N_NORMS + norm + 1)
                wait_ready(act, l, use)
                f(two_parts(rs[:, :]), halves(t), ACT.Ln, bias=eps, scale=1.0 / n).then_inc(free[b], 1)
                act.drain()
                f(rs[:, :], rs[:, :], ACT.Exp, scale=-0.5).then_inc(rs_ready, 1)

            def head_norms(l, name, tiles, hi, rounded, split_name):
                def square(h):
                    act.wait_ge(src_ready, l * 16 + HEAD_NORMS[name] + h + 1)
                    f(sq[:, h % 2, :], tiles[:, h, :], ACT.Square).then_inc(sq_ready, 1)
                square(0)
                square(1)
                for h in range(4):
                    act.wait_ge(rs_used, l * N_NORMS + NORMS[name] + h + 1)
                    act.wait_ge(head_sum, l * 8 + HEAD_NORMS[name] + h + 1)
                    f(two_parts(rs[:, :]), halves((two, last_two)[h % 2]), ACT.Ln, bias=eps, scale=1.0 / P)\
                        .then_inc(head_sum_free, 1)
                    act.drain()
                    f(rs[:, :], rs[:, :], ACT.Exp, scale=-0.5).then_inc(rs_ready, 1)
                    if h + 2 < 4:
                        square(h + 2)
                    act.wait_ge(whole, l * SPLITS + FIRST_SPLIT[split_name] + h + 1)
                    f(hi[:, h, :], rounded(h), ACT.Copy).then_inc(hi_done, 1)

            def round_tiles(l, name, pairs, scale=None):
                for k, (hi, src) in enumerate(pairs):
                    act.wait_ge(whole, l * SPLITS + FIRST_SPLIT[name] + k + 1)
                    f(hi, src, ACT.Copy, scale=1.0 if scale is None else scale).then_inc(hi_done, 1)

            def merge(l, name, first_gate):
                for m in range(8):
                    use = FIRST_USE[name] + 4 * (m // 2) + m % 2
                    wait_ready(act, l, use)
                    act.wait_ge(y_done, l * 24 + first_gate + m + 1)
                    t, b, _ = buf(use)
                    f(two_parts(stage[:, m % 2, :]), halves(t), ACT.Tanh, scale=0.5).then_inc(free[b], 1)
                    act.drain().then_inc(gate_ready, 1)

            def attend(l, name, maps, unit0, heads, prob, probT, exp0):
                units = [(h, t) for h in range(heads) for t in range(5)]

                def exps(i):
                    h, t = units[i]
                    if i >= 2:
                        act.wait_ge(pT_ready, l * 60 + unit0 + i - 1)
                    for m in range(maps):
                        use = FIRST_USE[name] + maps * i + m
                        ps, b, _ = buf(use)
                        col = 2 * (i % 2) + m
                        act.wait_ge(maxed, l * 80 + exp0 + maps * i + m + 1)
                        dst = prob[:, maps * (i % 2) + m, :]
                        if t == LATE:
                            out, src = dst[:, 0:CTX], ps[:, 0, 0:CTX]
                        else:
                            out, src = two_parts(dst), halves(ps)
                        f(out, src, ACT.Exp, bias=neg_max[:, col:col + 1],
                          accum_out=row_sum[:, col:col + 1]).then_inc(free[b], 1)
                        act.drain().then_inc(exped, 1)

                def copyT(i):
                    h, t = units[i]
                    act.wait_ge(pT_ready, l * 60 + unit0 + i + 1)
                    if i >= 2:
                        act.wait_ge(o_ready, l * 60 + unit0 + i - 1)
                    n = CTX if t == LATE else T
                    f(probT[:, i % 2, :, :].rearrange("p c q -> p (c q)")[:, 0:n],
                      two[:, :, :].rearrange("p a c -> p (a c)")[:, 0:n], ACT.Copy).then_inc(pT_copied, 1)

                n = len(units)
                for i in range(-1, n + 1):
                    if i + 1 < n:
                        exps(i + 1)
                    if i >= 1:
                        copyT(i - 1)

            act.dma_start(cst[:, :], consts).then_inc(cst_loaded, 16)
            act.dma_start(cond[:, :, :], condT).then_inc(cst_loaded, 16)
            act.wait_ge(cst_loaded, 32)
            f(t1[:, 0:32 * KD].rearrange("p (k g) -> p k g", g=32), cond[:, :, :], ACT.Tanh, scale=0.5).then_inc(cond_done, 1)
            act.wait_ge(x_loaded, 16)
            act.wait_ge(started, 1)
            with act.Fori(0, DEPTH) as l:
                act.wait_ge(layer_open, l + 1)
                act.dma_start(small[:, :], small_d[l]).then_inc(small_loaded, 16)
                act.wait_ge(lam_sums, l + 1)
                f(lam_tmp[:, 0:2], lam_tmp[:, 0:2], ACT.Exp).then_inc(lam_exps, 1)
                def keep_row(c, src):
                    act.wait_ge(row_ready, l * MOD_CHUNKS + c + 1)
                    act.wait_ge(row_free, l * MOD_CHUNKS + c + 1)
                    f(mod_row[:, c % 2, :], src, ACT.Copy).then_inc(row_copied, 1)

                for c in range(MOD_A // 4):
                    squares(l, FIRST_SQ["norm1"], 0, [x[:, k, :] for k in range(KD)], None, (2 * c, 2 * c + 1))
                    keep_row(c, two[:, c % 2, 0:256])
                inverse_root(l, FIRST_USE["norm1"], NORMS["norm1"], D)
                round_tiles(l, "h1", [(act_hi[:, k, :], stage[:, k % 2, :]) for k in range(KD)])

                wait_ready(act, l, FIRST_USE["mv"])
                wait_ready(act, l, FIRST_USE["mv"] + 1)
                f(vm[:, 0:2, :], big[0][:, :, :], ACT.Copy).then_inc(free[0], 1)
                f(vm[:, 2:4, :], big[1][:, :, :], ACT.Copy).then_inc(free[1], 1)
                f(vm[:, 4, :], two[:, 0, :], ACT.Copy).then_inc(vm_ready, 1)
                act.wait_ge(gate_rows, l + 1)
                f(rows[5][:, :], rows[1][:, :], ACT.Abs)
                act.drain()
                f(rows[5][:, :], rows[5][:, :], ACT.Exp, scale=-1.0)
                act.drain()
                f(rows[5][:, :], rows[5][:, :], ACT.Ln, bias=ones[0:ROWS, 0:1]).then_inc(soft_rows, 1)
                for name, n, dst, s in (("mq", 2, qm, DK_M ** -0.5), ("mk", 2, km, 1.0)):
                    for m in range(n):
                        wait_ready(act, l, FIRST_USE[name] + m)
                        t, b, _ = buf(FIRST_USE[name] + m)
                        f(two_parts(dst[:, m, :]), halves(t), ACT.Copy, scale=s).then_inc(free[b], 1)
                act.drain().then_inc(qk_ready, 1)
                for m in range(4):
                    wait_ready(act, l, FIRST_USE["mo"] + m)
                    t, b, _ = buf(FIRST_USE["mo"] + m)
                    f(two_parts(mo_th[:, m, :]), halves(t), ACT.Tanh, scale=0.5).then_inc(free[b], 1)
                keep_row(4, two[:, 0, 0:256])
                act.wait_ge(rows_ready, l + 1)
                f(rows[5][:, :], rows[1][:, :], ACT.Exp, scale=-1.0).then_inc(expm_ready, 1)
                act.dma_start(o_m[l, 0:H_M, :], rows[1][0:H_M, CTX - 1:CTX]).then_inc(state_stored, 16)
                act.dma_start(o_m[l, H_M:UNITS, :], rows[1][32:32 + H_M, 0:1]).then_inc(state_stored, 16)
                act.wait_ge(colsT_ready, l + 1)
                f(acol[:, :, :], two[:, 1, 0:5 * ROWS].rearrange("p (t r) -> p t r", r=ROWS), ACT.Copy)
                f(ktok[:, :], two[:, 0, 0:256], ACT.Copy)
                act.drain().then_inc(colsT_copied, 1)

                def unit_start(u):
                    _, h, par, pair, _ = unit(u)
                    act.wait_ge(bc_ready, l * UNITS + u + 1)
                    if u:
                        act.wait_ge(arg_ready, l * 40 + 5 * u)
                    f(nMbc[:, CTX:T], two[:, 0, :], ACT.Copy)
                    f(nMbc[:, 0:CTX], two[:, 1, 0:CTX], ACT.Copy)
                    act.drain().then_inc(bc_copied, 1)
                    if u:
                        act.wait_ge(num_ready, l * UNITS + u)
                    f(qw[par:par + 64, :], nMbc[par:par + 64, CTX:T], ACT.Exp, bias=s_("m0")[par:par + 64, u:u + 1])\
                        .then_inc(w_inter_ready, 1)

                def unit_end(u):
                    act.wait_ge(num_ready, l * UNITS + u + 1)
                    f(num_sb[:, u, CTX:T], one[0][:, :], ACT.Copy)
                    f(num_sb[:, u, 0:CTX], one[1][:, 0:CTX], ACT.Copy).then_inc(num_copied, 1)

                for i in range(40):
                    u, j = divmod(i, 5)
                    if j == 0:
                        if u:
                            unit_end(u - 1)
                        unit_start(u)
                    if j == 2 and u + 1 < UNITS:
                        keep_row(5 + u, two[:, 0, 0:256])
                    act.wait_ge(arg_ready, l * 40 + i + 1)
                    n = CTX if j == LATE else (LAT - P * j if u < H_M else P * (j + 1))
                    f(ebuf[:, i % 2, 0:n], ebuf[:, i % 2, 0:n], ACT.Exp).then_inc(e_ready, 1)
                unit_end(UNITS - 1)
                act.wait_ge(state_ready, l + 1)
                f(c_new[:, 0:4, :], two[0:DK_M, 0, :].rearrange("p (u e) -> p u e", e=DV_M), ACT.Copy)
                f(c_new[:, 4:8, :], two[0:DK_M, 1, :].rearrange("p (u e) -> p u e", e=DV_M), ACT.Copy)
                f(n_new[:, :], one[1][0:DK_M, 0:UNITS], ACT.Copy).then_inc(state_copied, 1)
                act.wait_ge(state_copied, l + 1)
                act.dma_start(o_C[l], c_new[:, :, :]).then_inc(state_stored, 16)
                act.dma_start(o_n[l], n_new[:, :]).then_inc(state_stored, 16)
                for k in range(KQ):
                    wait_ready(act, l, FIRST_USE["acq"] + k)
                    t, b, _ = buf(FIRST_USE["acq"] + k)
                    f(two_parts(acq[:, k, :]), halves(t), ACT.Copy).then_inc(free[b], 1)
                head_norms(l, "mn", num_sb, om_hi, lambda h: stage[:, h % 2, :], "om")
                act.wait_ge(lo_done, l * SPLITS + FIRST_SPLIT["om"] + 4)
                merge(l, "merge_m", 0)

                act.wait_ge(y_done, l * 24 + 8 + 2)
                act.wait_ge(state_stored, l * 64 + 64)
                act.dma_start(ckv[:, :, T:TK], past_d[l, :, PAST_C["ckv"][0]:PAST_C["ckv"][1]]
                              .rearrange("p (k t) -> p k t", t=PAST)).then_inc(past_loaded, 16)
                squares(l, FIRST_SQ["qn"], 0, [acq[:, k, :] for k in range(KQ)], None)
                inverse_root(l, FIRST_USE["qn"], NORMS["qn"], Q_RANK)
                round_tiles(l, "q", [(qn_hi[:, k, :], acq[:, k, :]) for k in range(KQ)])
                for k in range(KKV):
                    wait_ready(act, l, FIRST_USE["ckv"] + k)
                    t, b, _ = buf(FIRST_USE["ckv"] + k)
                    f(two_parts(ckv[:, k, 0:T]), halves(t), ACT.Copy).then_inc(free[b], 1)
                act.drain()
                squares(l, FIRST_SQ["kn"], 0, [ckv[:, k, 0:T] for k in range(KKV)], None)
                inverse_root(l, FIRST_USE["kn"], NORMS["kn"], KV_RANK)
                act.wait_ge(past_loaded, l * 64 + 16)
                round_tiles(l, "kv", [(ckv_hi[:, k, :], ckv[:, k, :]) for k in range(KKV)])
                act.dma_start(o_ckv[l], ckv[:, :, 0:CTX]).then_inc(ckv_stored, 16)
                scale = (NOPE + ROPE) ** -0.5
                for m in range(8):
                    use = FIRST_USE["qup"] + m
                    wait_ready(act, l, use)
                    t, b, _ = buf(use)
                    if m < 4:
                        f(two_parts(q_a[0:64, 2 * m, :]), halves(t)[0:64], ACT.Copy, scale=scale)
                        f(two_parts(q_a[0:64, 2 * m + 1, :]), halves(t)[64:128], ACT.Copy, scale=scale)\
                            .then_inc(free[b], 1)
                    else:
                        if m >= 6:
                            act.wait_ge(roped, l * 11 + 1)
                        f(two_parts(stage[:, m % 2, :]), halves(t), ACT.Copy, scale=scale).then_inc(free[b], 1)
                        if m % 2:
                            act.drain().then_inc(raw_kept, 1)
                use = FIRST_USE["kr"]
                act.wait_ge(roped, l * 11 + 2)
                wait_ready(act, l, use)
                t, b, _ = buf(use)
                act.dma_start(k_a[64:96, 0, T:TK], past_d[l, 64:96, PAST_C["kr"][0]:PAST_C["kr"][1]])\
                    .then_inc(past_loaded, 16)
                f(two_parts(stage[64:128, 0, :]), halves(t)[64:128], ACT.Copy).then_inc(free[b], 1)
                act.drain().then_inc(raw_kept, 1)
                act.dma_start(o_kr[l], stage[64:96, 0, 0:CTX]).then_inc(kr_stored, 16)
                for m in range(4):
                    use = FIRST_USE["kvn"] + m
                    wait_ready(act, l, use)
                    t, b, _ = buf(use)
                    f(two_parts(k_a[0:64, 2 * m, :], TK // 2), halves(t, TK // 2)[0:64], ACT.Copy)
                    f(two_parts(k_a[0:64, 2 * m + 1, :], TK // 2), halves(t, TK // 2)[64:128], ACT.Copy)\
                        .then_inc(free[b], 1)
                act.drain().then_inc(kn_copied, 1)
                attend(l, "ma", 1, 0, H_A, prob_a, probT_a, 0)
                act.wait_ge(kr_stored, l * 16 + 16)
                act.wait_ge(ckv_stored, l * 16 + 16)
                round_tiles(l, "oa", [(oa_hi[:, k, :], o_a[:, k, :]) for k in range(4)])
                merge(l, "merge_a", 8)

                act.wait_ge(y_done, l * 24 + 16 + 2)
                act.dma_start(v_d[:, 5, :], past_d[l, :, PAST_C["dv"][0]:PAST_C["dv"][1]]).then_inc(past_loaded, 16)
                act.dma_start(k_d[:, :, T:TK], past_d[l, :, PAST_C["dk"][0]:PAST_C["dk"][1]]
                              .rearrange("p (k t) -> p k t", t=PAST)).then_inc(past_loaded, 16)
                wait_ready(act, l, FIRST_USE["dv"])
                wait_ready(act, l, FIRST_USE["dv"] + 1)
                f(v_d[:, 0:2, :], big[0][:, :, :], ACT.Copy).then_inc(free[0], 1)
                f(v_d[:, 2:4, :], big[1][:, :, :], ACT.Copy).then_inc(free[1], 1)
                f(v_d[:, 4, :], two[:, 0, :], ACT.Copy)
                act.drain().then_inc(v_copied, 1)
                act.dma_start(o_dv[l], v_d[:, 0, :]).then_inc(diff_stored, 16)
                for m in range(8):
                    use = FIRST_USE["dq"] + m
                    wait_ready(act, l, use)
                    act.wait_ge(roped, l * 11 + 3 + max(m - 1, 0))
                    t, b, _ = buf(use)
                    f(two_parts(stage[:, m % 2, :]), halves(t), ACT.Copy, scale=DK_D ** -0.5 if m < 4 else 1.0)\
                        .then_inc(free[b], 1)
                    act.drain().then_inc(raw_kept, 1)
                act.wait_ge(roped, l * 11 + 11)
                act.dma_start(o_dk[l], k_d[:, :, 0:CTX]).then_inc(diff_stored, 16)
                attend(l, "da", 2, 40, H_D, prob_d, probT_d, 40)
                act.wait_ge(diff_stored, l * 32 + 32)
                head_norms(l, "dn", q_d, od_hi, lambda h: q_d[:, h, :], "od")
                merge(l, "merge_d", 16)

                round_tiles(l, "y", [(act_hi[:, k, :], y[:, k, :]) for k in range(KD)], scale=0.5)
                squares(l, FIRST_SQ["norm2"], 0, [x[:, k, :] for k in range(KD)],
                        lambda k: l * 16 + 8 + k + 1)
                inverse_root(l, FIRST_USE["norm2"], NORMS["norm2"], D)
                for k in range(KD):
                    act.wait_ge(whole, l * SPLITS + FIRST_SPLIT["h2"] + k + 1)
                    for g, a, b in GROUPS:
                        last = f(act_hi[:, k, a:b], y[:, k, a:b], ACT.Identity, bias=mod[:, 24 + k, g:g + 1])
                    last.then_inc(hi_done, 1)
                with act.Fori(0, FF_CHUNKS) as c:
                    def relu(m):
                        use = FIRST_USE["ff"] + m
                        wait_ready(act, l, use, c * 8)
                        act.wait_ge(relu_used, l * 32 + c * 8 + (m + 1))
                        t, b, _ = buf(use)
                        f(two_parts(sq[:, m % 2, :]), halves(t), ACT.Relu).then_inc(free[b], 1)
                        act.drain().then_inc(relu_ready, 1)

                    def round_ff(m):
                        act.wait_ge(whole, l * SPLITS + c * 8 + (FIRST_SPLIT["ff"] + m + 1))
                        f(ff_hi[:, m, :], stage[:, m % 2, :], ACT.Copy).then_inc(hi_done, 1)
                    relu(0)
                    for m in range(8):
                        if m + 1 < 8:
                            relu(m + 1)
                        round_ff(m)
            act.wait_ge(layer_open, DEPTH + 1)
            squares(DEPTH, 0, 0, [x[:, k, :] for k in range(KD)], None)
            inverse_root(DEPTH, 0, 0, D)

        @block.vector
        def _(dve):
            v = nc.vector

            def remainder(l, name, k, lo, src, hi, more=0):
                dve.wait_ge(hi_done, l * SPLITS + more + (FIRST_SPLIT[name] + k + 1))
                v.tensor_tensor(lo, src, hi.bitcast(f32), ALU.subtract).then_inc(lo_done, 1)

            def merge(l, name, first_gate, first):
                for m in range(8):
                    gate, use = first_gate + m, FIRST_USE[name] + 4 * (m // 2) + 2 + m % 2
                    dve.wait_ge(gate_ready, l * 24 + gate + 1)
                    wait_ready(dve, l, use)
                    t, b, _ = buf(use)
                    dst = y[:, m, :] if first else t1[:, :]
                    v.scalar_tensor_tensor(two_parts(dst), two_parts(stage[:, m % 2, :]), 1.0, halves(t), ALU.add,
                                           ALU.mult).then_inc(free[b], 1)
                    dve.drain()
                    if first:
                        dve.drain().then_inc(y_done, 1)
                    else:
                        v.tensor_tensor(y[:, m, :], y[:, m, :], t1[:, :], ALU.add).then_inc(y_done, 1)
                        dve.drain()

            def attend(l, name, maps, unit0, head0, heads, prob, exp0, out_of):
                units = [(h, t) for h in range(heads) for t in range(5)]

                def maxes(i):
                    h, t = units[i]
                    for m in range(maps):
                        use = FIRST_USE[name] + maps * i + m
                        wait_ready(dve, l, use)
                        ps, b, _ = buf(use)
                        col = 2 * (i % 2) + m
                        src = ps[:, 0, 0:CTX] if t == LATE else halves(ps)
                        v.tensor_reduce(neg_max[:, col:col + 1], src, AX.X if t == LATE else AX.XY, ALU.max,
                                        negate=True).then_inc(maxed, 1)

                def normalise(i):
                    h, t = units[i]
                    n = CTX if t == LATE else T
                    c0 = 2 * (i % 2)
                    dve.wait_ge(exped, l * 80 + exp0 + maps * (i + 1))
                    v.reciprocal(row_sum[:, c0:c0 + maps], row_sum[:, c0:c0 + maps])
                    dve.drain()
                    p0 = prob[:, maps * (i % 2), 0:n]
                    if maps == 1:
                        v.tensor_scalar(p0, p0, row_sum[:, c0:c0 + 1], None, ALU.mult).then_inc(p_ready, 1)
                    else:
                        p1 = prob[:, maps * (i % 2) + 1, 0:n]
                        v.tensor_scalar(p1, p1, row_sum[:, c0 + 1:c0 + 2], neg_lam, ALU.mult, ALU.mult)
                        dve.drain()
                        v.scalar_tensor_tensor(p0, p0, row_sum[:, c0:c0 + 1], p1, ALU.mult, ALU.add)\
                            .then_inc(p_ready, 1)
                    dve.drain()

                def outputs(i):
                    h, t = units[i]
                    lat, con, m = out_of(h)
                    if t >= LATE - 1:
                        dve.wait_ge(o_ready, l * 60 + unit0 + i + 1)
                        v.tensor_copy(*((con, one[1][0:m, 0:CTX]) if t == LATE else (lat, one[0][0:m, :])))\
                            .then_inc(o_copied, 1)

                n = len(units)
                for i in range(-1, n + 3):
                    if i + 1 < n:
                        maxes(i + 1)
                    if 0 <= i < n:
                        normalise(i)
                    if i >= 3:
                        outputs(i - 3)
                dve.drain()

            for s, n in ((split_ready, RAW), (block_used, 1), (free[0], 1), (free[1], 1), (row_free, 2), (rs_used, 1), (y_done, 2), (relu_used, 2)):
                v.memset(cols[:, 0:1], 0.0).then_inc(s, n)
                dve.drain()
            v.memset(cols[:, 0:1], 0.0).then_inc(started, 1)
            dve.wait_ge(cst_loaded, 32)
            dve.wait_ge(cond_done, 1)
            silu = t1[:, 0:32 * KD].rearrange("p (k g) -> p k g", g=32)
            v.scalar_tensor_tensor(silu, silu, 1.0, cond[:, :, :], ALU.add, ALU.mult)
            dve.drain()
            v.tensor_scalar(cond[:, :, :], silu, 0.5, None, ALU.mult).then_inc(silu_done, 1)
            dve.wait_ge(x_loaded, 16)
            dve.drain()
            v.memset(cols[:, 0:32], 0.0).then_inc(layer_open, 1)
            with dve.Fori(0, DEPTH) as l:
                dve.wait_ge(small_loaded, l * 16 + 16)
                lam = s_("lam").rearrange("p (a d) -> p a d", d=DK_D)
                v.tensor_tensor(t2[:, 0:64], lam[:, 0, :], lam[:, 1, :], ALU.mult)
                v.tensor_tensor(t2[:, 64:128], lam[:, 2, :], lam[:, 3, :], ALU.mult)
                dve.drain()
                v.tensor_reduce(lam_tmp[:, 0:2], t2[:, 0:128].rearrange("p (a d) -> p a d", d=64), AX.X, ALU.add)\
                    .then_inc(lam_sums, 1)
                dve.wait_ge(lam_exps, l + 1)
                v.tensor_tensor(lam_tmp[:, 2:3], lam_tmp[:, 1:2], lam_tmp[:, 0:1], ALU.subtract)
                dve.drain()
                v.tensor_tensor(neg_lam, lam_tmp[:, 2:3], s_("lam_init")[:, 0:1], ALU.subtract)
                v.tensor_scalar(g_half, s_("ng_m"), 0.5, None, ALU.mult)
                v.tensor_scalar(g_diff, s_("ng_d"), s_("lam_init")[:, 1:2], None, ALU.mult)

                def keep_mod(a, z, src, scale, j, g):
                    v.tensor_tensor(mod[:, a:z, :], src.rearrange("p (j g) -> p j g", g=2),
                                           s_("bmod")[:, a:z].unsqueeze(2).to_broadcast([P, z - a, 2]), ALU.add)
                    dve.drain()
                    v.scalar_tensor_tensor(scale[:, :, :], mod[:, 8 * j:8 * j + 8, :], 1.0,
                                           s_(g).unsqueeze(2).to_broadcast([P, KD, 2]), ALU.add, ALU.mult)
                    dve.drain()
                dve.wait_ge(rs_ready, l * N_NORMS + NORMS["norm1"] + 1)
                for k in range(KD):
                    v.tensor_tensor(y[:, k, :], x[:, k, :], rs[:, :], ALU.mult)
                dve.drain().then_inc(rs_used, 1)
                dve.wait_ge(row_free, l * MOD_CHUNKS + 2 + MOD_A // 4)
                keep_mod(0, 2 * KD, one[0][:, 0:4 * KD], scale1, 1, "n1")
                for k in range(KD + 1):
                    if k < KD:
                        for g, a, b in GROUPS:
                            last = v.tensor_scalar(stage[:, k % 2, a:b], y[:, k, a:b], scale1[:, k, g:g + 1],
                                                   mod[:, k, g:g + 1], ALU.mult, ALU.add)
                        last.then_inc(whole, 1)
                    if k:
                        remainder(l, "h1", k - 1, act_lo[:, k - 1, :], stage[:, (k - 1) % 2, :], act_hi[:, k - 1, :])
                    dve.drain()

                use = FIRST_USE["mg"]
                wait_ready(dve, l, use)
                t, b, _ = buf(use)
                v.tensor_scalar(two_parts(rows[0][:, :]), halves(t)[0:ROWS], s_("gb")[0:ROWS, 0:1], None, ALU.add)
                v.tensor_scalar(two_parts(rows[1][:, :]), halves(t)[64:64 + ROWS], s_("gb")[64:64 + ROWS, 1:2], None,
                                ALU.add).then_inc(free[b], 1)
                v.memset(rows[2][:, :], 0.0)
                v.memset(rows[3][:, :], 1.0)
                dve.drain().then_inc(gate_rows, 1)
                dve.wait_ge(soft_rows, l + 1)
                v.tensor_scalar(rows[1][:, :], rows[1][:, :], 0.0, None, ALU.min)
                dve.drain()
                v.tensor_tensor(rows[1][:, :], rows[1][:, :], rows[5][:, :], ALU.subtract)
                dve.drain()

                def scans(dst, data0, data1, op0, op1, first):
                    for r, a, b_, back in ((0, 0, CTX, 0), (0, CTX, T, 0), (32, 0, CTX, 1), (32, CTX, T, 1)):
                        def w(tile):
                            ap = tile[r:r + H_M, a:b_]
                            return ap[:, ::-1] if back else ap
                        init = 0.0 if first is None or a == 0 else first[r:r + H_M, 0:1]
                        v.tensor_tensor_scan(w(dst), w(data0), w(data1), init, op0, op1)
                    dve.drain()
                scans(rows[2], rows[3], rows[1], ALU.mult, ALU.add, None)
                v.tensor_tensor(rows[0][:, :], rows[0][:, :], rows[2][:, :], ALU.subtract)
                dve.drain()
                scans(rows[3], rows[0], rows[0], ALU.max, ALU.max, s_("m0row"))
                v.tensor_tensor(rows[1][:, :], rows[2][:, :], rows[3][:, :], ALU.add)
                v.tensor_scalar(rows[4][:, :], rows[3][:, :], -1.0, None, ALU.mult)
                dve.drain().then_inc(rows_ready, 1)
                dve.wait_ge(colsT_copied, l + 1)

                def argument(i):
                    u, j = divmod(i, 5)
                    _, h, par, pair, row = unit(u)
                    if i >= 2:
                        dve.wait_ge(e_ready, l * 40 + i - 1)
                    mask = c_("mask_f") if u < H_M else c_("mask_b")
                    if j == 0:
                        dve.wait_ge(bc_copied, l * UNITS + u + 1)
                        dve.wait_ge(w_inter_ready, l * UNITS + u + 1)
                        v.tensor_tensor(qw[par:par + 64, :], qw[par:par + 64, :], qm[par:par + 64, pair, CTX:T],
                                        ALU.mult).then_inc(qw_ready, 1)
                    s = acol[:, 0 if j == LATE else j + 1, row:row + 1]
                    e = ebuf[:, i % 2, :]
                    if j == LATE:
                        v.scalar_tensor_tensor(e[:, 0:P], nMbc[:, 0:CTX], s, mask, ALU.add, ALU.min)
                    else:
                        q0 = CTX + P * j
                        if u < H_M:
                            v.scalar_tensor_tensor(e[:, 0:P], nMbc[:, q0:q0 + P], s, mask, ALU.add, ALU.min)
                            if j < 3:
                                v.tensor_scalar(e[:, P:T - q0], nMbc[:, q0 + P:T], s, 0.0, ALU.add, ALU.min)
                        else:
                            v.scalar_tensor_tensor(e[:, P * j:P * j + P], nMbc[:, q0:q0 + P], s, mask, ALU.add, ALU.min)
                            if j:
                                v.tensor_scalar(e[:, 0:P * j], nMbc[:, CTX:q0], s, 0.0, ALU.add, ALU.min)
                    dve.drain().then_inc(arg_ready, 1)

                def product(i):
                    u, j = divmod(i, 5)
                    _, h, _, _, _ = unit(u)
                    use = FIRST_USE["ms"] + i
                    t, b, _ = buf(use)
                    n = CTX if j == LATE else (LAT - P * j if u < H_M else P * (j + 1))
                    wait_ready(dve, l, use)
                    dve.wait_ge(e_ready, l * 40 + i + 1)
                    if i >= 2:
                        pu, pj = divmod(i - 2, 5)
                        if pj == LATE:
                            dve.wait_ge(num_ready, l * UNITS + pu + 1)
                        else:
                            dve.wait_ge(a_used, l * (4 * UNITS) + 4 * pu + pj + 1)
                    v.tensor_tensor(abuf[:, i % 2, 0:n], ebuf[:, i % 2, 0:n], t[:, 0, 0:n], ALU.mult)\
                        .then_inc(free[b], 1)
                    if j == LATE:
                        last_col = CTX - 1 if u < H_M else 0
                        v.tensor_scalar(kw[:, u, :], ktok[:, DK_M * h:DK_M * h + DK_M],
                                        ebuf[:, i % 2, last_col:last_col + 1], None, ALU.mult).then_inc(kw_ready, 1)
                    dve.drain().then_inc(a_ready, 1)

                argument(0)
                for i in range(40):
                    if i == 36:
                        dve.wait_ge(row_free, l * MOD_CHUNKS + 2 + MOD_CHUNKS)
                        keep_mod(2 * KD, 6 * KD, one[1][:, 256:256 + 8 * KD], scale2, 4, "n2")
                        dve.drain().then_inc(mod_kept, 1)
                    if i % 5 != 4 and i + 1 < 40:
                        argument(i + 1)
                        product(i)
                    else:
                        product(i)
                        if i + 1 < 40:
                            argument(i + 1)
                dve.wait_ge(num_ready, l * UNITS + UNITS)
                dve.wait_ge(expm_ready, l + 1)
                v.tensor_scalar(rows[2][:, CTX:T], big[0][0:ROWS, 1, :], -1.0, None, ALU.mult)
                v.tensor_scalar(rows[2][:, 0:CTX], big[1][0:ROWS, 1, 0:CTX], -1.0, None, ALU.mult)
                dve.drain()
                v.tensor_tensor(rows[2][:, CTX:T], rows[2][:, CTX:T], big[0][0:ROWS, 1, :], ALU.max)
                v.tensor_tensor(rows[2][:, 0:CTX], rows[2][:, 0:CTX], big[1][0:ROWS, 1, 0:CTX], ALU.max)
                dve.drain().then_inc(den_read, 1)
                v.tensor_tensor(rows[2][:, :], rows[2][:, :], rows[5][:, :], ALU.max)
                dve.drain()
                v.reciprocal(rows[2][:, :], rows[2][:, :]).then_inc(rden_ready, 1)
                dve.wait_ge(num_copied, l * UNITS + UNITS)
                for h in range(H_M):
                    for d in range(2):
                        u, use = h + H_M * d, FIRST_USE["mr"] + 2 * h + d
                        wait_ready(dve, l, use)
                        t, b, _ = buf(use)
                        v.tensor_tensor(two_parts(num_sb[:, u, :]), two_parts(num_sb[:, u, :]), halves(t), ALU.mult)\
                            .then_inc(free[b], 1)
                    dve.drain()
                    v.tensor_tensor(num_sb[:, h, :], num_sb[:, h, :], num_sb[:, h + H_M, :], ALU.add)\
                        .then_inc(src_ready, 1)
                dve.wait_ge(state_ready, l + 1)
                for h in range(H_M):
                    dve.wait_ge(rs_ready, l * N_NORMS + NORMS["mn"] + h + 1)
                    v.scalar_tensor_tensor(t1[:, :], num_sb[:, h, :], g_half[:, h:h + 1], rs[:, :], ALU.mult, ALU.mult)
                    dve.drain().then_inc(rs_used, 1)
                    v.scalar_tensor_tensor(stage[:, h % 2, :], mo_th[:, h, :], 1.0, t1[:, :], ALU.add, ALU.mult)\
                        .then_inc(whole, 1)
                    dve.drain()
                    remainder(l, "om", h, om_lo[:, h, :], stage[:, h % 2, :], om_hi[:, h, :])
                merge(l, "merge_m", 0, True)

                dve.wait_ge(rs_ready, l * N_NORMS + NORMS["qn"] + 1)
                for k in range(KQ):
                    v.scalar_tensor_tensor(acq[:, k, :], acq[:, k, :], s_("ng_q")[:, k:k + 1], rs[:, :], ALU.mult,
                                           ALU.mult).then_inc(whole, 1)
                dve.drain().then_inc(rs_used, 1)
                for k in range(KQ):
                    remainder(l, "q", k, qn_lo[:, k, :], acq[:, k, :], qn_hi[:, k, :])
                dve.wait_ge(rs_ready, l * N_NORMS + NORMS["kn"] + 1)
                dve.wait_ge(past_loaded, l * 64 + 16)
                for k in range(KKV):
                    v.scalar_tensor_tensor(ckv[:, k, 0:T], ckv[:, k, 0:T], s_("ng_kv")[:, k:k + 1], rs[:, :],
                                           ALU.mult, ALU.mult).then_inc(whole, 1)
                dve.drain().then_inc(rs_used, 1)
                for k in range(KKV):
                    remainder(l, "kv", k, ckv_lo[:, k, :], ckv[:, k, :], ckv_hi[:, k, :])
                for j in range(2):
                    dve.wait_ge(raw_kept, l * 11 + j + 1)
                    v.tensor_tensor(t1[:, CTX:T], stage[:, 0, CTX:T], c_("cos_a"), ALU.mult)
                    v.tensor_tensor(t2[:, CTX:T], stage[:, 1, CTX:T], c_("sin_a"), ALU.mult)
                    dve.drain()
                    for g in range(4):
                        r = slice(32 * g, 32 * g + 32)
                        v.tensor_tensor(q_a[64:96, 4 * j + g, CTX:T], t1[r, CTX:T], t2[r, CTX:T], ALU.add)
                        v.tensor_copy(q_a[64:96, 4 * j + g, 0:CTX], stage[r, 0, 0:CTX])
                    dve.drain().then_inc(roped, 1)
                dve.wait_ge(raw_kept, l * 11 + 3)
                v.tensor_tensor(t1[64:96, CTX:T], stage[64:96, 0, CTX:T], c_("cos_a", slice(64, 96)), ALU.mult)
                v.tensor_tensor(t2[64:96, CTX:T], stage[96:128, 0, CTX:T], c_("sin_a", slice(96, 128)), ALU.mult)
                dve.drain()
                v.tensor_tensor(k_a[64:96, 0, CTX:T], t1[64:96, CTX:T], t2[64:96, CTX:T], ALU.add)
                v.tensor_copy(k_a[64:96, 0, 0:CTX], stage[64:96, 0, 0:CTX])
                dve.drain()
                dve.wait_ge(past_loaded, l * 64 + 32)
                for h in range(1, H_A):
                    v.tensor_copy(k_a[64:96, h, :], k_a[64:96, 0, :])
                dve.drain().then_inc(roped, 1)
                dve.wait_ge(ckv_stored, l * 16 + 16)
                for i in range(3):
                    use = FIRST_USE["kvv"] + i
                    wait_ready(dve, l, use)
                    t, b, _ = buf(use)
                    v.tensor_copy(v_a[:, 2 * i:2 * i + 2, :], t[:, :, :]).then_inc(free[b], 1)
                dve.drain().then_inc(v_copied, 1)

                def out_a(h):
                    r = slice(64 * (h % 2), 64 * (h % 2) + 64)
                    return o_a[r, h // 2, CTX:T], o_a[r, h // 2, 0:CTX], V_A
                attend(l, "ma", 1, 0, 0, H_A, prob_a, 0, out_a)
                for k in range(4):
                    dve.drain().then_inc(whole, 1)
                    dve.drain()
                for k in range(4):
                    remainder(l, "oa", k, oa_lo[:, k, :], o_a[:, k, :], oa_hi[:, k, :])
                merge(l, "merge_a", 8, False)

                for m in range(8):
                    dve.wait_ge(raw_kept, l * 11 + 3 + m + 1)
                    dst = q_d[:, m, :] if m < 4 else k_d[:, m - 4, :]
                    src = stage[:, m % 2, :]
                    v.tensor_tensor(t1[:, CTX:T], src[:, CTX:T], c_("cos_d"), ALU.mult)
                    for g in range(4):
                        r, o = slice(32 * g, 32 * g + 32), slice(32 * (g ^ 1), 32 * (g ^ 1) + 32)
                        v.tensor_tensor(t2[o, CTX:T], src[r, CTX:T], c_("sin_d", r), ALU.mult)
                    v.tensor_copy(dst[:, 0:CTX], src[:, 0:CTX])
                    dve.drain()
                    v.tensor_tensor(dst[:, CTX:T], t1[:, CTX:T], t2[:, CTX:T], ALU.add)
                    dve.drain().then_inc(roped, 1)
                def out_d(h):
                    return q_d[:, h, CTX:T], q_d[:, h, 0:CTX], DV_D
                attend(l, "da", 2, 40, 8, H_D, prob_d, 40, out_d)
                for h in range(H_D):
                    dve.drain().then_inc(src_ready, 1)
                    dve.drain()
                for h in range(H_D):
                    dve.wait_ge(rs_ready, l * N_NORMS + NORMS["dn"] + h + 1)
                    v.scalar_tensor_tensor(q_d[:, h, :], q_d[:, h, :], g_diff[:, h:h + 1], rs[:, :], ALU.mult,
                                           ALU.mult).then_inc(whole, 1)
                    dve.drain().then_inc(rs_used, 1)
                    remainder(l, "od", h, od_lo[:, h, :], q_d[:, h, :], od_hi[:, h, :])
                merge(l, "merge_d", 16, False)

                for k in range(KD):
                    dve.drain().then_inc(whole, 1)
                    dve.drain()
                for k in range(KD):
                    dve.wait_ge(hi_done, l * SPLITS + FIRST_SPLIT["y"] + k + 1)
                    v.scalar_tensor_tensor(act_lo[:, k, :], y[:, k, :], 0.5, act_hi[:, k, :].bitcast(f32), ALU.mult,
                                           ALU.subtract).then_inc(lo_done, 1)

                def add_to_x(l, use, m, gate, more=0):
                    wait_ready(dve, l, use, more)
                    t, b, _ = buf(use)
                    for n, (g, h, a, z) in enumerate(PARTS):
                        o = h * HALF
                        last = v.scalar_tensor_tensor(x[:, m, o + a:o + z], t[:, h, a:z],
                                                      mod[:, 8 * gate + m, g:g + 1], x[:, m, o + a:o + z],
                                                      ALU.mult, ALU.add)
                    return last.then_inc(free[b], 1)
                for m in range(KD):
                    add_to_x(l, FIRST_USE["wout"] + m, m, 2)
                    dve.drain().then_inc(src_ready, 1)
                    for g, a, b in GROUPS:
                        v.tensor_scalar(y[:, m, a:b], x[:, m, a:b], scale2[:, m, g:g + 1], None, ALU.mult)
                    dve.drain()
                dve.wait_ge(rs_ready, l * N_NORMS + NORMS["norm2"] + 1)
                for k in range(KD + 1):
                    if k < KD:
                        v.tensor_tensor(y[:, k, :], y[:, k, :], rs[:, :], ALU.mult).then_inc(whole, 1)
                    if k:
                        dve.wait_ge(hi_done, l * SPLITS + FIRST_SPLIT["h2"] + k)
                        for g, a, b in GROUPS:
                            last = v.scalar_tensor_tensor(act_lo[:, k - 1, a:b], y[:, k - 1, a:b],
                                                          mod[:, 23 + k, g:g + 1],
                                                          act_hi[:, k - 1, a:b].bitcast(f32), ALU.add, ALU.subtract)
                        last.then_inc(lo_done, 1)
                    dve.drain()
                v.memset(cols[:, 31:32], 0.0).then_inc(rs_used, 1)

                with dve.Fori(0, FF_CHUNKS) as c:
                    for m in range(9):
                        if m < 8:
                            dve.wait_ge(relu_ready, l * 32 + c * 8 + (m + 1))
                            v.tensor_tensor(stage[:, m % 2, :], sq[:, m % 2, :], sq[:, m % 2, :], ALU.mult)\
                                .then_inc(whole, 1)
                            dve.drain().then_inc(relu_used, 1)
                        if m:
                            remainder(l, "ff", m - 1, ff_lo[:, m - 1, :], stage[:, (m - 1) % 2, :],
                                      ff_hi[:, m - 1, :], c * 8)
                            dve.drain()
                    for m in range(8):
                        add_to_x(l, FIRST_USE["ff"] + 8 + m, m, 5, c * 8)
                dve.drain().then_inc(layer_open, 1)
            dve.wait_ge(rs_ready, DEPTH * N_NORMS + 1)
            for k in range(KD):
                v.scalar_tensor_tensor(x[:, k, :], x[:, k, :], s_("fin")[:, k:k + 1], rs[:, :], ALU.mult, ALU.mult)\
                    .then_inc(y_final, 1)


def _tiles(w, k0=None):
    kk, n = w.shape
    return w.reshape(kk // P, P, n // P, P).transpose(2, 1, 0, 3)


def _wide(w):
    kk, n = w.shape
    return w.reshape(kk // 256, 2, P, n // 512, 512).transpose(3, 0, 2, 1, 4).reshape(-1, P, BLK)


def _pairs(tiles):
    m, _, k, _ = tiles.shape
    s = tiles.transpose(0, 2, 1, 3).reshape(m * k // 8, 8, P, P)
    return s.transpose(0, 2, 1, 3).reshape(-1, P, BLK)


def _swap(w, n):
    s = w.reshape(w.shape[0], -1, 2, n // 2)[:, :, ::-1, :]
    return s.reshape(w.shape)


def _blocks(i, l):
    w = i["w_in"][l]
    cut = np.cumsum([256, 256, 512, 512, 16, 384, 256, 32, 512, 512, 512])
    mq, mk, mv, mo, mg, acq, ckv, kr, dq, dk, dv, gates = np.split(w, cut, axis=1)
    mgp = np.zeros((D, P), w.dtype)
    for n in range(4):
        mgp[:, 32 * n:32 * n + 4] = mg[:, 4 * n:4 * n + 4]
    krp = np.zeros((D, P), w.dtype)
    krp[:, 64:96], krp[:, 96:128] = kr, _swap(kr, ROPE)
    qu = i["mla_w_q_up"][l].reshape(Q_RANK, H_A, NOPE + ROPE)
    qn, qr = qu[:, :, :NOPE].reshape(Q_RANK, -1), qu[:, :, NOPE:].reshape(Q_RANK, -1)
    qs = _swap(qr, ROPE)
    qall = np.concatenate([qn, qr[:, :P], qs[:, :P], qr[:, P:], qs[:, P:]], axis=1)
    ku = i["mla_w_kv_up"][l].reshape(KV_RANK, H_A, NOPE + V_A)
    kn, kv = ku[:, :, :NOPE].reshape(KV_RANK, -1), ku[:, :, NOPE:].reshape(KV_RANK, -1)

    def merge(g, br):
        gt, bt = _pairs(_tiles(gates[:, D * g:D * g + D])), _pairs(_tiles(br))
        return [b for p in range(4) for b in (gt[2 * p], gt[2 * p + 1], bt[p])]
    f1, f2 = _pairs(_tiles(i["w_ff1"][l])), i["w_ff2"][l]
    out = [_wide(mv)] + [_pairs(_tiles(a)) for a in (mgp, mq, mk, mo, acq)] + [merge(0, i["w_br_mlstm"][l])]
    out += [_pairs(_tiles(a)) for a in (ckv, qall, krp, kn)] + [_wide(kv)]
    out += [merge(1, i["w_br_mla"][l]), _wide(dv), _pairs(_tiles(dq)), _pairs(_tiles(dk))]
    out += [merge(2, i["w_br_diff"][l]), _pairs(_tiles(i["w_out"][l]))]
    for c in range(FF_CHUNKS):
        out += [f1[8 * c:8 * c + 8], _pairs(_tiles(f2[D * c:D * c + D]))]
    kinds = {"mod": _wide(i["w_mod"][l]),
             "dense": np.concatenate([np.stack(o) if isinstance(o, list) else o for o in out])}
    return np.stack([kinds[kind][index] for kind, index in ORDER])


def _columns_of(a):
    return a.reshape(-1, P).T


def _small(i, l):
    s = np.zeros((P, SMALL_W), np.float32)

    def put(name, a, r=slice(0, P)):
        s[r, SMALL[name][0]:SMALL[name][1]] = a
    for name, key in (("bmod", "b_mod"), ("n1", "norm1_g"), ("n2", "norm2_g"), ("ng_m", "mlstm_norm_g"),
                      ("ng_q", "mla_q_norm_g"), ("ng_kv", "mla_kv_norm_g"), ("ng_d", "diff_norm_g")):
        put(name, _columns_of(i[key][l]))
    put("fin", _columns_of(i["final_norm_g"]))
    gb = i["mlstm_gate_b"][l].reshape(2, 2, H_M)
    m0 = i["state_mlstm_m"][0, l]
    for d in range(2):
        r = slice(32 * d, 32 * d + H_M)
        s[r, SMALL["gb"][0]] = gb[0, d]
        s[64 + 32 * d:64 + 32 * d + H_M, SMALL["gb"][0] + 1] = gb[1, d]
        s[r, SMALL["m0row"][0]] = m0[d]
    put("m0", m0.reshape(1, UNITS))
    put("lam", i["diff_lambda"][l].reshape(1, 256))
    lam_init = 0.8 - 0.6 * math.exp(-0.3 * l)
    put("lam_init", np.array([[lam_init, 1.0 - lam_init]], np.float32))
    n0, c0 = np.zeros((P, 4, ROWS), np.float32), np.zeros((P, 4, DV_M), np.float32)
    for u in range(UNITS):
        d, h, par, pair, row = unit(u)
        n0[par:par + 64, 2 * d + pair, row] = i["state_mlstm_n"][0, l, d, h]
        c0[par:par + 64, 2 * d + pair] = i["state_mlstm_C"][0, l, d, h]
    put("n0", n0.reshape(P, -1))
    put("C0", c0.reshape(P, -1))
    return s


def _past(i, l):
    s = np.zeros((P, PAST_W), np.float32)

    def features(a):
        return a.T.reshape(-1, P, a.shape[0]).transpose(1, 0, 2).reshape(P, -1)
    s[:, PAST_C["ckv"][0]:PAST_C["ckv"][1]] = features(i["cache_mla_ckv"][0, l])
    s[64:96, PAST_C["kr"][0]:PAST_C["kr"][1]] = i["cache_mla_krope"][0, l].T
    s[:, PAST_C["dk"][0]:PAST_C["dk"][1]] = features(i["cache_diff_k"][0, l].reshape(PAST, -1))
    s[:, PAST_C["dv"][0]:PAST_C["dv"][1]] = i["cache_diff_v"][0, l].reshape(PAST, -1)
    return s


def _constants():
    s = np.zeros((P, CONST_W), np.float32)

    def put(name, a, r=slice(0, P)):
        s[r, CONST[name][0]:CONST[name][1]] = a
    t = np.arange(LAT)
    row, col = (t // GRID_W).astype(np.float32), (t % GRID_W).astype(np.float32)
    for name, dim in (("d", DK_D), ("a", ROPE)):
        quarter = dim // 4
        inv = np.float32(ROPE_BASE) ** (-np.arange(quarter, dtype=np.float32) / np.float32(quarter))
        ang = np.concatenate([row[:, None] * inv, col[:, None] * inv], axis=-1).astype(np.float32)
        c, z = np.cos(ang).T, np.sin(ang).T
        put("cos_" + name, np.tile(np.concatenate([c, c]), (P // dim, 1)))
        sign = [z, -z] if name == "d" else [-z, z]
        put("sin_" + name, np.tile(np.concatenate(sign), (P // dim, 1)))
    p, q = np.arange(P)[:, None], np.arange(P)[None, :]
    put("mask_f", np.where(q >= p, 0.0, NEG))
    put("mask_b", np.where(q <= p, 0.0, NEG))
    put("ident", np.eye(P))
    put("ones", 1.0)
    den, rsel = np.zeros((P, UNITS, ROWS)), np.zeros((P, UNITS, P))
    for u in range(UNITS):
        den[:, u, unit(u)[4]] = 1.0
        rsel[unit(u)[4], u, :] = 1.0
    put("den_sel", den.reshape(P, -1))
    put("row_sel", rsel.reshape(P, -1))
    put("fold_sel", np.concatenate([(p % 32 == np.arange(2)) & (p // 64 == half) for half in range(2)], axis=1))
    put("eps", EPS)
    return s


def kernel(**inputs):
    import concourse.bacc as bacc
    from concourse.bass_utils import run_bass_kernel_spmd as run

    i = {k: np.asarray(v) for k, v in inputs.items()}
    f32 = mybir.dt.float32
    tokens = np.concatenate([i["x_prompt"][0], i["x_sample"][0]])
    arrays = {
        "in_x": np.ascontiguousarray(tokens.reshape(T, KD, P).transpose(2, 1, 0)),
        "in_cond": np.ascontiguousarray(np.pad(np.stack([i["c_ctx"], i["c"][0]]), ((0, 30), (0, 0)))
                                        .reshape(32, KD, P).transpose(2, 1, 0)),
        "in_const": _constants(),
        "in_small": np.stack([_small(i, l) for l in range(DEPTH)]),
        "in_past": np.stack([_past(i, l) for l in range(DEPTH)]),
        "in_w": np.stack([_blocks(i, l) for l in range(DEPTH)]),
    }
    outs = {"out_y": (P, KD, T), "out_ckv": (DEPTH, P, KKV, CTX), "out_kr": (DEPTH, ROPE, CTX),
            "out_dk": (DEPTH, P, 4, CTX), "out_dv": (DEPTH, CTX, 512), "out_C": (DEPTH, DK_M, UNITS, DV_M),
            "out_n": (DEPTH, DK_M, UNITS), "out_m": (DEPTH, UNITS, 1)}
    nc = bacc.Bacc("TRN2", target_bir_lowering=False, num_devices=1, dynamic_dma_scratch_size=1024)
    args = [nc.dram_tensor(n, a.shape, f32, kind="ExternalInput").ap() for n, a in arrays.items()]
    args += [nc.dram_tensor(n, s, f32, kind="ExternalOutput").ap() for n, s in outs.items()]
    trunk(nc, *args)
    r = run(nc, [arrays], core_ids=[0]).results[0]

    y = r["out_y"].transpose(2, 1, 0).reshape(T, D)
    ckv = r["out_ckv"].transpose(0, 3, 2, 1).reshape(1, DEPTH, CTX, KV_RANK)
    kr = r["out_kr"].transpose(0, 2, 1)[None]
    dk = r["out_dk"].transpose(0, 3, 2, 1).reshape(1, DEPTH, CTX, H_D, 2 * DK_D)
    dv = r["out_dv"].reshape(1, DEPTH, CTX, H_D, DV_D)
    c_new = r["out_C"].transpose(0, 2, 1, 3).reshape(1, DEPTH, 2, H_M, DK_M, DV_M)
    n_new = r["out_n"].transpose(0, 2, 1).reshape(1, DEPTH, 2, H_M, DK_M)
    m_new = r["out_m"].reshape(1, DEPTH, 2, H_M)
    return y[None, :CTX], y[None, CTX:], ckv, kr, dk, dv, c_new, n_new, m_new
```

```python
import math
from contextlib import ExitStack

import numpy as np

import concourse.bass as bass
from concourse import mybir

D = 1024
CTX, LAT, PAST = 128, 512, 128
DEPTH = 2
T = CTX + LAT
TK = T + PAST
HALF = T // 2
P = 128
KD = D // P
H_M, DK_M, DV_M = 4, 64, 128
H_A, NOPE, ROPE, V_A = 8, 64, 32, 64
Q_RANK, KV_RANK = 384, 256
KQ, KKV = Q_RANK // P, KV_RANK // P
H_D, DK_D, DV_D = 4, 64, 128
D_FF = 4 * D
EPS = 1e-6
GRID_W = 64
ROPE_BASE = 10000.0
UNITS = 2 * H_M
ROWS = 32 + H_M
BLK = 1024

MOD_BLOCKS = 6 * D * KD // BLK
MOD_CHUNKS = 6 * D // 512
FF_CHUNKS = 4
STAGES = [("mv", 4), ("mg", 1), ("mq", 2), ("mk", 2), ("mo", 4), ("acq", 3), ("merge_m", 2), ("ckv", 2),
          ("merge_m rest", 10), ("qup", 3), ("kr", 1), ("kvn", 1), ("kvv", 1),
          ("dq", 4), ("dk", 4), ("dv", 4), ("merge_a", 12), ("merge_d", 12), ("wout", 8), ("ff", 64)]
FIRST_BLOCK, DENSE = {}, 0
for _name, _n in STAGES:
    FIRST_BLOCK[_name] = DENSE
    DENSE += _n
BLOCKS = MOD_BLOCKS + DENSE
RAW, SPLIT = 4, 2
assert BLOCKS % RAW == 0 and DENSE % SPLIT == 0
MOD_A, DENSE_A = 16, FIRST_BLOCK["acq"]
RUNS = [("mod", MOD_A - 4), ("dense", SPLIT), ("mod", 8), ("dense", DENSE_A - SPLIT),
        ("mod", MOD_BLOCKS - MOD_A - 12), ("dense", FIRST_BLOCK["ff"] + 1 - DENSE_A), ("mod", 8),
        ("dense", DENSE - FIRST_BLOCK["ff"] - 1)]
PLACES = {"mod": [], "dense": []}
ORDER = []
for _kind, _n in RUNS:
    for _ in range(_n):
        PLACES[_kind].append(len(ORDER))
        ORDER.append((_kind, len(PLACES[_kind]) - 1))
assert len(ORDER) == BLOCKS

USE_STAGES = [("norm1", 1), ("mv", 2), ("mg", 1), ("mq", 2), ("mk", 2), ("mo", 4),
              ("ms", UNITS * 5), ("acq", KQ), ("mr", UNITS), ("merge_m", 2),
              ("ckv", KKV), ("merge_m rest", 14), ("qup", 8), ("kr", 1), ("kvn", 4), ("kvv", 3),
              ("ma", H_A * 5),
              ("dq", 4), ("dk", 4), ("dv", 2), ("da", H_D * 10), ("merge_a", 16), ("merge_d", 16),
              ("wout", 8), ("norm2", 1), ("ff", 64)]
FIRST_USE, USES = {}, 0
for _name, _n in USE_STAGES:
    FIRST_USE[_name] = USES
    USES += _n
assert USES % 2 == 0


def place_in(table, name, i):
    return table[name] + i if i < 2 or name + " rest" not in table else table[name + " rest"] + i - 2



SPLIT_STAGES = [("h1", 8), ("om", 4), ("kv", KKV), ("q", KQ), ("oa", 4), ("od", 4), ("y", 8), ("h2", 8), ("ff", 32)]
FIRST_SPLIT, SPLITS = {}, 0
for _name, _n in SPLIT_STAGES:
    FIRST_SPLIT[_name] = SPLITS
    SPLITS += _n
SQ_STAGES = [("norm1", 8), ("mn", 4), ("kn", KKV), ("qn", KQ), ("dn", 4), ("norm2", 8)]
FIRST_SQ, SQUARES = {}, 0
for _name, _n in SQ_STAGES:
    FIRST_SQ[_name] = SQUARES
    SQUARES += _n
FIRST_SQ_USED, SQ_USED = {}, 0
for _name, _n in SQ_STAGES:
    FIRST_SQ_USED[FIRST_SQ[_name]] = SQ_USED
    SQ_USED += _n - 1 if _name not in ("mn", "dn") else 0
NORMS = {"norm1": 0, "mn": 1, "kn": 5, "qn": 6, "dn": 7, "norm2": 11}
N_NORMS = 12
HEAD_NORMS = {"mn": 0, "dn": 4}

def _columns(parts):
    at, out = 0, {}
    for name, n in parts:
        out[name] = (at, at + n)
        at += n
    return out, at


SMALL, SMALL_W = _columns([("bmod", 48), ("n1", 8), ("n2", 8), ("ng_m", 4), ("ng_q", KQ), ("ng_kv", KKV),
                           ("ng_d", 4), ("gb", 2), ("m0row", 1), ("m0", UNITS), ("lam", 256), ("lam_init", 2),
                           ("fin", 8), ("n0", 4 * ROWS), ("C0", 4 * DV_M)])
CONST, CONST_W = _columns([("cos_d", LAT), ("sin_d", LAT), ("cos_a", LAT), ("sin_a", LAT), ("mask_f", P),
                           ("mask_b", P), ("ident", P), ("ones", P), ("den_sel", UNITS * ROWS),
                           ("row_sel", UNITS * P), ("fold_sel", 4), ("eps", 1)])
PAST_C, PAST_W = _columns([("ckv", KKV * PAST), ("kr", PAST), ("dk", 4 * PAST), ("dv", H_D * DV_D)])
NEG = -1e30


def unit(u):
    d, h = divmod(u, H_M)
    return d, h, 64 * (h % 2), h // 2, 32 * d + h


def trunk(nc, xT, condT, consts, small_d, past_d, w_d, yT, o_ckv, o_kr, o_dk, o_dv, o_C, o_n, o_m):
    f32, f32r = mybir.dt.float32, mybir.dt.float32r
    ALU, ACT, AX = mybir.AluOpType, mybir.ActivationFunctionType, mybir.AxisListType
    ctx = ExitStack()
    with ctx:
        base = [(nc.sbuf_base + 63) // 64 * 64]

        def at(name, shape, offset, dt=f32):
            return nc.alloc_sbuf_tensor_at(name, shape, dt, offset=offset)

        def sb(name, shape, dt=f32):
            off = base[0]
            base[0] += (int(np.prod(shape[1:])) * 4 + 63) // 64 * 64
            return at(name, shape, off, dt)

        def sem(name):
            return ctx.enter_context(nc.semaphore(name))

        x = sb("x", [P, KD, T])
        act_hi, act_lo = sb("act_hi", [P, KD, T], f32r), sb("act_lo", [P, KD, T], f32r)
        raw = sb("raw", [P, RAW, BLK])
        w_hi, w_lo = sb("w_hi", [P, SPLIT, BLK], f32r), sb("w_lo", [P, SPLIT, BLK], f32r)
        y_at = base[0]
        y = sb("y", [P, KD, T])
        num_sb = at("num_sb", [P, UNITS, T], y_at)
        cst = sb("cst", [P, CONST_W])
        small = sb("small", [P, SMALL_W])
        cond = sb("cond", [P, KD, 32])
        mod = sb("mod", [P, 48, 2])
        scale1, scale2 = sb("scale1", [P, KD, 2]), sb("scale2", [P, KD, 2])
        cols = sb("cols", [P, 32])
        mod_row = sb("mod_row", [P, 2, 256])
        rs = sb("rs", [P, T])
        sq = sb("sq", [P, 2, T])
        t1, t2 = sb("t1", [P, T]), sq[:, 1, :]
        stage = sb("stage", [P, 2, T])
        A0 = base[0]
        qm, km = at("qm", [P, 2, T], A0), at("km", [P, 2, T], A0 + 5120)
        q_head = [qm[:, 0, :], qm[:, 1, :], stage[:, 0, :], stage[:, 1, :]]
        q_map = [stage, sq]
        vm = at("vm", [P, 5, 512], A0 + 10240)
        om_hi, om_lo = at("om_hi", [P, 4, T], A0, f32r), at("om_lo", [P, 4, T], A0 + 10240, f32r)
        mo_th = at("mo_th", [P, 4, T], A0 + 20480)
        ebuf, abuf = at("ebuf", [P, 2, 512], A0 + 30720), at("abuf", [P, 2, 512], A0 + 34816)
        nMbc = [at("nMbc0", [P, T], A0 + 38912), at("nMbc1", [P, T], A0 + 69632)]
        qw = at("qw", [P, 512], A0 + 41472)
        rows_full = {i: at(f"row{i}", [P, T], A0 + 43520 + 2560 * i) for i in (2, 4)}
        rows = [rows_full[i][0:ROWS, :] if i in rows_full else at(f"row{i}", [ROWS, T], A0 + 43520 + 2560 * i)
                for i in range(6)]
        acol = at("acol", [P, 5, ROWS], A0 + 58880)
        ktok, kw = at("ktok", [P, 256], A0 + 59648), at("kw", [P, UNITS, DK_M], A0 + 60672)
        c_new, n_new = at("c_new", [DK_M, UNITS, DV_M], A0 + 62720), at("n_new", [DK_M, UNITS], A0 + 66816)
        q_a, o_a = at("q_a", [96, H_A, T], A0), at("o_a", [P, 4, T], A0)
        k_a = at("k_a", [96, H_A, TK], A0 + 20480)
        qn_hi, qn_lo = at("qn_hi", [P, KQ, T], A0 + 20480, f32r), at("qn_lo", [P, KQ, T], A0 + 28160, f32r)
        acq = at("acq", [P, KQ, T], A0 + 35840)
        oa_hi, oa_lo = at("oa_hi", [P, 4, T], A0 + 50176, f32r), at("oa_lo", [P, 4, T], A0 + 60416, f32r)
        v_a, ckv = at("v_a", [P, 6, 512], A0 + 45056), at("ckv", [P, KKV, TK], A0 + 45056)
        ckv_hi, ckv_lo = at("ckv_hi", [P, KKV, TK], A0 + 57344, f32r), at("ckv_lo", [P, KKV, TK], A0 + 63488, f32r)
        prob_a = at("prob_a", [P, 2, T], A0 + 57344)
        probT_a = at("probT_a", [P, 4, 5, P], A0 + 62464)
        q_d, k_d = at("q_d", [P, 4, T], A0), at("k_d", [P, 4, TK], A0 + 10240)
        v_d = at("v_d", [P, 6, 512], A0 + 22528)
        prob_d = at("prob_d", [P, 4, T], A0 + 34816)
        probT_d = at("probT_d", [P, 2, 5, P], A0 + 45056)
        od_hi, od_lo = at("od_hi", [P, 4, T], A0 + 10240, f32r), at("od_lo", [P, 4, T], A0 + 20480, f32r)
        ff_hi, ff_lo = at("ff_hi", [P, 8, T], A0, f32r), at("ff_lo", [P, 8, T], A0 + 20480, f32r)

        big = [ctx.enter_context(nc.psum_tensor(f"big{b}", [P, 2, 512], f32)) for b in range(2)]
        two = ctx.enter_context(nc.psum_tensor("two", [P, 2, 512], f32))
        last_two = ctx.enter_context(nc.psum_tensor("last_two", [P, 2, 512], f32))
        one = [last_two[:, b, :] for b in range(2)]

        def c_(name, rows_=slice(0, P)):
            return cst[rows_, CONST[name][0]:CONST[name][1]]

        def s_(name, rows_=slice(0, P)):
            return small[rows_, SMALL[name][0]:SMALL[name][1]]

        ones, ident = c_("ones"), c_("ident")
        eps, fold_sel = c_("eps"), c_("fold_sel")
        den_sel = c_("den_sel").rearrange("p (u r) -> p u r", r=ROWS)
        row_sel = c_("row_sel").rearrange("p (u c) -> p u c", c=P)
        n0 = s_("n0").rearrange("p (a r) -> p a r", r=ROWS)
        C0 = s_("C0").rearrange("p (a e) -> p a e", e=DV_M)
        g_half, g_diff, neg_lam = cols[:, 0:4], cols[:, 4:8], cols[:, 8:9]
        lam_tmp = cols[:, 9:12]
        neg_max, row_sum = cols[:, 12:16], cols[:, 16:20]

        raw_loaded = [sem(f"raw_loaded{i}") for i in range(RAW)]
        mod_block_used = sem("mod_block_used")
        split_ready, block_used = sem("split_ready"), sem("block_used")
        ready, free = [sem("ready_a"), sem("ready_b")], [sem("free_a"), sem("free_b")]
        cond_loaded = sem("cond_loaded")
        x_loaded, cst_loaded, small_loaded = sem("x_loaded"), sem("cst_loaded"), sem("small_loaded")
        layer_open, started = sem("layer_open"), sem("started")
        cond_done = sem("cond_done")
        q_map_ready = sem("q_map_ready")
        gather_done, small_sum = sem("gather_done"), sem("small_sum")
        row_ready, row_copied, row_free = sem("row_ready"), sem("row_copied"), sem("row_free")
        silu_done, mod_kept = sem("silu_done"), sem("mod_kept")
        den_read = sem("den_read")
        head_sum, head_sum_free = sem("head_sum"), sem("head_sum_free")
        sq_ready, sq_used = sem("sq_ready"), sem("sq_used")
        rs_ready, rs_used = sem("rs_ready"), sem("rs_used")
        whole, hi_done, lo_done = sem("whole"), sem("hi_done"), sem("lo_done")
        src_ready = sem("src_ready")
        vm_ready, qk_ready, mo_ready = sem("vm_ready"), sem("qk_ready"), sem("mo_ready")
        gate_rows, soft_rows, rows_ready, expm_ready = sem("gate_rows"), sem("soft_rows"), sem("rows_ready"), sem("expm_ready")
        colsT_ready, colsT_copied = sem("colsT_ready"), sem("colsT_copied")
        bc_ready, bc_copied, w_inter_ready, qw_ready = sem("bc_ready"), sem("bc_copied"), sem("w_inter_ready"), sem("qw_ready")
        arg_ready, e_ready, a_ready, a_used = sem("arg_ready"), sem("e_ready"), sem("a_ready"), sem("a_used")
        num_ready, num_copied = sem("num_ready"), sem("num_copied")
        kw_ready, state_ready, state_copied = sem("kw_ready"), sem("state_ready"), sem("state_copied")
        rden_ready = sem("rden_ready")
        gate_ready, y_done = sem("gate_ready"), sem("y_done")
        past_loaded = sem("past_loaded")
        raw_kept, roped = sem("raw_kept"), sem("roped")
        kv_norm_done, k_rope_done, kn_copied = sem("kv_norm_done"), sem("k_rope_done"), sem("kn_copied")
        qnope_copied, v_copied = sem("qnope_copied"), sem("v_copied")
        maxed, exped, p_ready = sem("maxed"), sem("exped"), sem("p_ready")
        pT_ready, pT_copied, o_ready, o_copied = sem("pT_ready"), sem("pT_copied"), sem("o_ready"), sem("o_copied")
        relu_ready, relu_used = sem("relu_ready"), sem("relu_used")
        x_updated, y_final = sem("x_updated"), sem("y_final")
        stored, state_stored, ckv_stored = sem("stored"), sem("state_stored"), sem("ckv_stored")
        kr_stored, diff_stored = sem("kr_stored"), sem("diff_stored")
        lam_sums, lam_exps = sem("lam_sums"), sem("lam_exps")

        def buf(i):
            return big[i % 2], i % 2, i // 2

        def wait_free(pe, l, i, more=0):
            pe.wait_ge(free[i % 2], l * (USES // 2) + more + i // 2 + 1)

        def wait_ready(e, l, i, more=0):
            e.wait_ge(ready[i % 2], l * (USES // 2) + more + i // 2 + 1)

        def halves(t, n=HALF):
            return t[:, :, 0:n]

        def two_parts(ap, n=HALF):
            return ap.rearrange("p (a t) -> p a t", t=n)

        PARTS = [(0, 0, 0, CTX), (1, 0, CTX, HALF), (1, 1, 0, HALF)]
        GROUPS = [(0, 0, CTX), (1, CTX, T)]
        LATE = 4

        def prob_tile(prob, maps, i, m):
            return prob[:, maps * (i % 3) + m, :] if i % 3 < 2 else (t1, rs)[m]

        def attention_units(heads, side):
            return [(side * p + g, t) for p in range(heads // side) for t in range(5) for g in range(side)]

        def keys(t):
            return (0, CTX) if t == LATE else (CTX, TK)

        def queries(t):
            return (0, CTX) if t == LATE else (CTX + P * t, CTX + P * t + P)

        block = ctx.enter_context(nc.Block())

        @block.sync
        def _(sp):
            sp.wait_ge(started, 1)
            with sp.Fori(0, DEPTH) as l:
                place = 0
                for kind, n in RUNS:
                    def load(place, i):
                        of_kind, index = ORDER[place - RAW]
                        index -= DENSE if place < RAW else 0
                        if of_kind == "mod":
                            sp.wait_ge(mod_block_used, l * MOD_BLOCKS + i + (index + 1))
                        else:
                            sp.wait_ge(split_ready, l * DENSE + i + (index + 1 + RAW))
                        slot = place % RAW
                        sp.dma_start(raw[:, slot, :], w_d[l, i + place]).then_inc(raw_loaded[slot], 16)
                    head = min(n, RAW)
                    for j in range(head):
                        load(place + j, 0)
                    if n >= 2 * RAW:
                        with sp.Fori(0, n // RAW - 1) as i:
                            for j in range(RAW):
                                load(place + RAW + j, i * RAW)
                        head = n // RAW * RAW
                    for j in range(head, n):
                        load(place + j, 0)
                    place += n
            for k in range(KD):
                sp.wait_ge(y_final, k + 1)
                sp.dma_start(yT[:, k, :], x[:, k, :]).then_inc(stored, 16)
            sp.wait_ge(stored, 16 * KD)

        @block.gpsimd
        def _(pool):
            pool.wait_ge(cst_loaded, 16)
            with pool.Fori(0, DEPTH) as l:
                def split(block, i):
                    place, to = PLACES["dense"][block], block % SPLIT
                    slot = place % RAW
                    pool.wait_ge(raw_loaded[slot], l * (16 * BLOCKS // RAW) + i * 16 + 16 * (place // RAW + 1))
                    pool.wait_ge(block_used, l * DENSE + i * RAW + (block + 1))
                    nc.gpsimd.tensor_tensor(w_hi[:, to, :], raw[:, slot, :],
                                            ones[:, 0:1].to_broadcast([P, BLK]), ALU.mult)
                    pool.drain()
                    nc.gpsimd.tensor_tensor(w_lo[:, to, :], raw[:, slot, :], w_hi[:, to, :].bitcast(f32),
                                            ALU.subtract).then_inc(split_ready, 1)
                block = 0
                for n in [n for kind, n in RUNS if kind == "dense"]:
                    looped = n // RAW * RAW
                    if looped:
                        with pool.Fori(0, n // RAW) as i:
                            for j in range(RAW):
                                split(block + j, i)
                    for j in range(looped, n):
                        split(block + j, 0)
                    block += n

        @block.tensor
        def _(pe):
            mm = nc.tensor.matmul

            def block_start(l, b, more=0):
                pe.wait_ge(split_ready, l * DENSE + more + (b + 1 + RAW))

            def project(l, first_use, first_block, tiles, nk, hi, lo, n=HALF, arrived=None, more_b=0, more_u=0):
                for p in range(tiles * nk):
                    m, k = divmod(p, nk)
                    b, q = divmod(p, 8)
                    slot, col = (first_block + b) % SPLIT, P * q
                    if q == 0:
                        block_start(l, first_block + b, more_b)
                    t, _, _ = buf(first_use + m)
                    if k == 0:
                        wait_free(pe, l, first_use + m, more_u)
                    if arrived is not None and m == 0:
                        pe.wait_ge(lo_done, arrived(k))
                    for h in range(2):
                        ps = t[:, h, 0:n]
                        wh, wl = w_hi[:, slot, col:col + P], w_lo[:, slot, col:col + P]
                        ah, al = hi[:, k, h * n:h * n + n], lo[:, k, h * n:h * n + n]
                        first = mm(ps, wh, ah, start=k == 0, stop=False)
                        if q == 0 and h == 0:
                            first.then_inc(block_used, 1)
                        mm(ps, wh, al, start=False, stop=False)
                        last = mm(ps, wl, ah, start=False, stop=k == nk - 1)
                    if k == nk - 1:
                        last.then_inc(ready[(first_use + m) % 2], 1)

            def project_tokens(l, first_use, first_block, arrived=None):
                wait_free(pe, l, first_use)
                wait_free(pe, l, first_use + 1)
                outs = [big[0][:, 0, :], big[0][:, 1, :], big[1][:, 0, :], big[1][:, 1, :], two[:, 0, :]]
                for b in range(4):
                    block_start(l, first_block + b)
                    slot = (first_block + b) % SPLIT
                    if arrived is not None:
                        pe.wait_ge(lo_done, arrived(2 * b + 1))
                    for t in range(5):
                        for kk in range(2):
                            k = 2 * b + kk
                            wh, wl = w_hi[:, slot, 512 * kk:512 * kk + 512], w_lo[:, slot, 512 * kk:512 * kk + 512]
                            ah, al = act_hi[:, k, P * t:P * t + P], act_lo[:, k, P * t:P * t + P]
                            first = mm(outs[t], ah, wh, start=k == 0, stop=False)
                            if t == 0 and kk == 0 and first_block + b:
                                first.then_inc(block_used, 1)
                            mm(outs[t], al, wh, start=False, stop=False)
                            last = mm(outs[t], ah, wl, start=False, stop=k == KD - 1)
                        if b == 3 and t in (1, 4):
                            last.then_inc(ready[t // 4], 1)

            def sums(l, use, first_sq, n, gathered=None, off=0):
                wait_free(pe, l, use, off)
                t, b, _ = buf(use)
                for k in range(n) if gathered is None else (0, n - 1):
                    src = sq[:, k % 2, :]
                    if gathered is not None and k == 0:
                        src = t1
                        pe.wait_ge(gather_done, l * 2 + gathered)
                    else:
                        pe.wait_ge(sq_ready, l * SQUARES + first_sq + k + 1)
                    for h in range(2):
                        last = mm(t[:, h, 0:HALF], ones, src[:, h * HALF:(h + 1) * HALF], start=k == 0, stop=k == n - 1)
                    if k == n - 1:
                        last.then_inc(ready[b], 1)
                    elif gathered is None:
                        last.then_inc(sq_used, 1)

            def head_sums(l, name, heads):
                for h in heads:
                    n = HEAD_NORMS[name] + h
                    pe.wait_ge(sq_ready, l * SQUARES + FIRST_SQ[name] + h + 1)
                    if h >= 2:
                        pe.wait_ge(head_sum_free, l * 8 + n - 1)
                    for a in range(2):
                        last = mm((two, last_two)[h % 2][:, a, 0:HALF], ones, sq[:, h % 2, a * HALF:(a + 1) * HALF],
                                  start=True, stop=True)
                    last.then_inc(head_sum, 1)

            def small_sums(l, t, first_sq, n):
                for k in range(n):
                    pe.wait_ge(sq_ready, l * SQUARES + first_sq + k + 1)
                    for h in range(2):
                        last = mm(t[:, h, 0:HALF], ones, sq[:, k % 2, h * HALF:(h + 1) * HALF],
                                  start=k == 0, stop=k == n - 1)
                    last.then_inc(small_sum if k == n - 1 else sq_used, 1)

            def mod_rows(l, c, out):
                for q in range(4):
                    place = PLACES["mod"][4 * c + q]
                    pe.wait_ge(raw_loaded[place % RAW], l * (16 * BLOCKS // RAW) + 16 * (place // RAW + 1))
                    for kk in range(2):
                        for half in range(2):
                            r = 32 * (2 * half + kk)
                            a = 512 * kk + 256 * half
                            last = mm(out[r:r + 32, :], cond[:, 2 * q + kk, :], raw[:, place % RAW, a:a + 256],
                                      start=q == 0, stop=q == 3)
                            if c + q + kk + half == 0:
                                last.then_inc(block_used, 1)
                            if 0 < c < MOD_A // 4 and q + kk + half == 0:
                                last.then_inc(mod_block_used, 1)
                    last.then_inc(row_ready if q == 3 else mod_block_used, 1)

            def mod_fold(l, c, out):
                pe.wait_ge(row_copied, l * MOD_CHUNKS + c + 1)
                for j in range(4):
                    half = j // 2
                    last = mm(out[:, 2 * j:2 * j + 2], mod_row[:, c % 2, P * (j % 2):P * (j % 2) + P],
                              fold_sel[:, 2 * half:2 * half + 2], start=True, stop=True)
                    if j == 0 and c >= MOD_A // 4 - 1:
                        last.then_inc(mod_block_used, 1)
                last.then_inc(row_free, 1)

            def merge(l, name, o_hi, o_lo, split_name, gate_hook=None, pair_hook=None):
                for p in range(4):
                    for g in range(2):
                        if gate_hook and p == 0:
                            gate_hook(g)
                        project(l, place_in(FIRST_USE, name, 4 * p + g), place_in(FIRST_BLOCK, name, 3 * p + g),
                                1, KD, act_hi, act_lo)
                    if gate_hook and p == 0:
                        gate_hook(2)
                    project(l, place_in(FIRST_USE, name, 4 * p + 2), place_in(FIRST_BLOCK, name, 3 * p + 2),
                            2, 4, o_hi, o_lo,
                            arrived=(lambda k: l * SPLITS + FIRST_SPLIT[split_name] + k + 1) if p == 0 else None)
                    if pair_hook:
                        pair_hook(p)

            def attend(l, name, maps, side, unit0, set0, q_of, k_of, v_of, heads, prob, probT):
                units = attention_units(heads, side)

                def scores(i):
                    h, t = units[i]
                    q0, q1 = queries(t)
                    k0, k1 = keys(t)
                    if maps == 2 and t == 0:
                        pe.wait_ge(q_map_ready, l * H_D + h + 1)
                    for m in range(maps):
                        use = FIRST_USE[name] + maps * i + m
                        wait_free(pe, l, use)
                        ps, b, _ = buf(use)
                        n = (k1 - k0) // (1 if t == LATE else 2)
                        for c in range((k1 - k0) // n):
                            last = mm(ps[:, c, 0:n], q_of(h, m)[:, q0:q1], k_of(h, m)[:, k0 + c * n:k0 + c * n + n],
                                      start=True, stop=True)
                        last.then_inc(ready[b], 1)

                def turn(i):
                    h, t = units[i]
                    if maps == 2 and i == 0:
                        pe.wait_ge(v_copied, l * 2 + 2)
                    pe.wait_ge(p_ready, l * 60 + unit0 + i + 1)
                    if i:
                        pe.wait_ge(pT_copied, l * 60 + unit0 + i)
                    src = prob_tile(prob, maps, i, 0)
                    for c in range(1 if t == LATE else 5):
                        out = two[:, 0, P * c:P * c + P] if c < 4 else two[:, 1, 0:P]
                        last = nc.tensor.transpose(out, src[:, P * c:P * c + P], ident)
                    last.then_inc(pT_ready, 1)

                def values(j):
                    p, t = divmod(j, 5)
                    pe.wait_ge(pT_copied, l * 60 + unit0 + side * (j + 1))
                    if p and t in (0, LATE):
                        pe.wait_ge(o_copied, l * 16 + 2 * (set0 + p) - (t == 0))
                    m = P // side
                    for c in range(1 if t == LATE else 5):
                        for g in range(side):
                            turned = probT[:, (side * j + g) % (2 * side), c, :]
                            r = slice(m * g, m * g + m)
                            if t == LATE:
                                last = mm(one[1][r, 0:CTX], v_of(side * p + g, 0), turned, start=True, stop=True)
                            else:
                                last = mm(one[0][r, P * t:P * t + P], v_of(side * p + g, c + 1), turned,
                                          start=c == 0, stop=c == 4)
                    last.then_inc(o_ready, side)

                n = len(units)
                for i in range(-1, n + 2):
                    if i + 1 < n:
                        scores(i + 1)
                    if 0 <= i - 1 < n:
                        turn(i - 1)
                    if 0 <= i - 2 and (i - 2) % side == side - 1:
                        values((i - 2) // side)

            pe.wait_ge(started, 1)
            with pe.Fori(0, DEPTH) as l:
                pe.wait_ge(cond_loaded, 16)
                pe.wait_ge(silu_done, 1)
                for c in range(MOD_A // 4 + 1):
                    if c < MOD_A // 4:
                        mod_rows(l, c, two[:, c % 2, 0:256])
                    if c:
                        pe.wait_ge(cst_loaded, 16)
                        mod_fold(l, c - 1, one[0][:, 8 * c - 8:8 * c])
                    if c == 2:
                        sums(l, FIRST_USE["norm1"], FIRST_SQ["norm1"], KD, 1)

                mod_rows(l, 4, two[:, 1, 0:256])

                def h_arrived(k):
                    return l * SPLITS + FIRST_SPLIT["h1"] + k + 1
                project_tokens(l, FIRST_USE["mv"], FIRST_BLOCK["mv"], h_arrived)
                mod_fold(l, 4, one[1][:, 256:264])
                for name, n in (("mg", 1), ("mq", 2), ("mk", 2), ("mo", 4)):
                    project(l, FIRST_USE[name], FIRST_BLOCK[name], n, KD, act_hi, act_lo)

                pe.wait_ge(vm_ready, l + 1)
                pe.wait_ge(qk_ready, l + 1)
                pe.wait_ge(rows_ready, l + 1)
                for t in range(5):
                    mm(two[:, 1, ROWS * t:ROWS * t + ROWS], rows[0][:, P * t:P * t + P], ident[0:ROWS, 0:ROWS],
                       start=True, stop=True)
                for j in range(2):
                    last = mm(two[:, 0, P * j:P * j + P], km[:, j, 0:CTX], ident, start=True, stop=True)
                last.then_inc(colsT_ready, 1)

                def broadcast(u):
                    if u == 0:
                        pe.wait_ge(colsT_copied, l + 1)
                    else:
                        pe.wait_ge(bc_copied, l * UNITS + u)
                    mm(two[:, 0, :], row_sel[:, u, :], rows_full[4][:, CTX:T], start=True, stop=True)
                    mm(two[:, 1, 0:CTX], row_sel[:, u, :], rows_full[4][:, 0:CTX], start=True, stop=True)\
                        .then_inc(bc_ready, 1)

                def span(u, j):
                    if j == LATE:
                        return 0, CTX
                    return (CTX + P * j, T) if u < H_M else (CTX, CTX + P * (j + 1))

                def m_scores(i):
                    u, j = divmod(i, 5)
                    _, h, par, pair, _ = unit(u)
                    s0, _ = queries(j)
                    q0, q1 = span(u, j)
                    use = FIRST_USE["ms"] + i
                    wait_free(pe, l, use)
                    t, b, _ = buf(use)
                    mm(t[:, 0, 0:q1 - q0], km[:, pair, s0:s0 + P], q_head[h][:, q0:q1],
                       start=True, stop=True).then_inc(ready[b], 1)

                def m_values(i):
                    u, j = divmod(i, 5)
                    d, h, par, pair, row = unit(u)
                    if j == 0:
                        pe.wait_ge(qw_ready, l * UNITS + u + 1)
                        if u:
                            pe.wait_ge(num_copied, l * 2 * UNITS + 2 * u - 1)
                        mm(one[0][:, :], C0[:, 2 * d + pair, :], qw[:, :], start=True, stop=False)
                        mm(big[0][0:ROWS, 1, :], n0[:, 2 * d + pair, :], qw[:, :],
                           start=u == 0, stop=False)
                    q0, q1 = span(u, j)
                    pe.wait_ge(a_ready, l * 40 + i + 1)
                    A = abuf[:, i % 2, 0:q1 - q0]
                    v = vm[:, 0 if j == LATE else j + 1, P * h:P * h + P]
                    if j == LATE:
                        if u:
                            pe.wait_ge(num_copied, l * 2 * UNITS + 2 * u)
                        mm(one[1][:, 0:CTX], v, A, start=True, stop=True)
                        mm(big[1][0:ROWS, 1, 0:CTX], den_sel[:, u, :], A, start=u == 0, stop=u == UNITS - 1)\
                            .then_inc(num_ready, 1)
                    else:
                        mm(one[0][:, q0 - CTX:q1 - CTX], v, A, start=False, stop=j == 3)
                        mm(big[0][0:ROWS, 1, q0 - CTX:q1 - CTX], den_sel[:, u, :], A, start=False,
                           stop=u == UNITS - 1 and j == 3).then_inc(a_used, 1)

                broadcast(0)
                m_scores(0)
                for i in range(40):
                    if i + 1 < 40:
                        m_scores(i + 1)
                    u = i // 5
                    if i % 5 == 1 and 1 <= u <= 5:
                        pe.wait_ge(num_copied, l * 2 * UNITS + 2 * u)
                        mod_fold(l, 4 + u, one[1][:, 256 + 8 * u:264 + 8 * u])
                    if i % 5 == 1 and u + 1 < UNITS:
                        broadcast(u + 1)
                    if i % 5 == 3 and u < 5:
                        pe.wait_ge(bc_copied, l * UNITS + u + 2)
                        mod_rows(l, 5 + u, two[:, 0, 0:256])
                    m_values(i)
                pe.wait_ge(kw_ready, l * UNITS + UNITS)
                pe.wait_ge(num_copied, l * 2 * UNITS + 2 * UNITS)
                pe.wait_ge(mod_kept, l + 1)
                for u in range(UNITS):
                    _, h, _, _, _ = unit(u)
                    mm(two[0:DK_M, u // 4, P * (u % 4):P * (u % 4) + P], kw[:, u, :], vm[:, 0, P * h:P * h + P],
                       start=True, stop=True)
                    last = mm(one[1][0:DK_M, u:u + 1], kw[:, u, :], ones[:, 0:1], start=True, stop=True)
                last.then_inc(state_ready, 1)
                pe.wait_ge(den_read, l + 1)
                project(l, FIRST_USE["acq"], FIRST_BLOCK["acq"], KQ, KD, act_hi, act_lo)
                pe.wait_ge(rden_ready, l + 1)
                for j in range(UNITS):
                    u = j // 2 + H_M * (j % 2)
                    use = FIRST_USE["mr"] + j
                    wait_free(pe, l, use)
                    t, b, _ = buf(use)
                    for h in range(2):
                        last = mm(t[:, h, 0:HALF], row_sel[:, u, :], rows_full[2][:, h * HALF:(h + 1) * HALF],
                                  start=True, stop=True)
                    last.then_inc(ready[b], 1)
                pe.wait_ge(state_copied, l + 1)

                def beside_gates_m(g):
                    if g < 2:
                        head_sums(l, "mn", (2 * g, 2 * g + 1))
                    else:
                        project(l, FIRST_USE["ckv"], FIRST_BLOCK["ckv"], KKV, KD, act_hi, act_lo)

                def behind_pair_m(p):
                    if p == 1:
                        pe.wait_ge(head_sum_free, l * 8 + 4)
                        small_sums(l, two, FIRST_SQ["kn"], KKV)
                    if p == 2:
                        small_sums(l, last_two, FIRST_SQ["qn"], KQ)
                merge(l, "merge_m", om_hi, om_lo, "om", beside_gates_m, behind_pair_m)

                project(l, FIRST_USE["qup"], FIRST_BLOCK["qup"], 8, KQ, qn_hi, qn_lo,
                        arrived=lambda k: l * SPLITS + FIRST_SPLIT["q"] + k + 1)
                project(l, FIRST_USE["kr"], FIRST_BLOCK["kr"], 1, KD, act_hi, act_lo)
                project(l, FIRST_USE["kvn"], FIRST_BLOCK["kvn"], 4, KKV, ckv_hi, ckv_lo, n=TK // 2,
                        arrived=lambda k: l * SPLITS + FIRST_SPLIT["kv"] + k + 1)
                block_start(l, FIRST_BLOCK["kvv"])
                slot = FIRST_BLOCK["kvv"] % SPLIT
                for i in range(3):
                    use = FIRST_USE["kvv"] + i
                    wait_free(pe, l, use)
                    ps, b, _ = buf(use)
                    for tt in range(2):
                        t = 2 * i + tt
                        for kk in range(KKV):
                            wh, wl = w_hi[:, slot, 512 * kk:512 * kk + 512], w_lo[:, slot, 512 * kk:512 * kk + 512]
                            ah, al = ckv_hi[:, kk, P * t:P * t + P], ckv_lo[:, kk, P * t:P * t + P]
                            first = mm(ps[:, tt, :], ah, wh, start=kk == 0, stop=False)
                            if t + kk == 0:
                                first.then_inc(block_used, 1)
                            mm(ps[:, tt, :], al, wh, start=False, stop=False)
                            last = mm(ps[:, tt, :], ah, wl, start=False, stop=kk == KKV - 1)
                    last.then_inc(ready[b], 1)
                pe.wait_ge(roped, l * 11 + 3)
                pe.wait_ge(kn_copied, l + 1)
                pe.wait_ge(v_copied, l * 2 + 1)
                attend(l, "ma", 1, 2, 0, 0, lambda h, m: q_a[:, h, :], lambda h, m: k_a[:, h, :],
                       lambda h, c: v_a[:, c, V_A * h:V_A * h + V_A], H_A, prob_a, probT_a)
                project(l, FIRST_USE["dq"], FIRST_BLOCK["dq"], 4, KD, act_hi, act_lo)
                project(l, FIRST_USE["dk"], FIRST_BLOCK["dk"], 4, KD, act_hi, act_lo)
                project_tokens(l, FIRST_USE["dv"], FIRST_BLOCK["dv"])
                pe.wait_ge(roped, l * 11 + 11)
                pe.wait_ge(past_loaded, l * 64 + 64)
                attend(l, "da", 2, 1, 40, 4, lambda h, m: q_map[h % 2][:, m, :], lambda h, m: k_d[:, h, :],
                       lambda h, c: v_d[:, c, P * h:P * h + P], H_D, prob_d, probT_d)

                def behind_pair_a(p):
                    if p == 0:
                        pe.wait_ge(o_copied, l * 16 + 16)
                    head_sums(l, "dn", (p,))
                merge(l, "merge_a", oa_hi, oa_lo, "oa", None, behind_pair_a)
                merge(l, "merge_d", od_hi, od_lo, "od")

                project(l, FIRST_USE["wout"], FIRST_BLOCK["wout"], 8, KD, act_hi, act_lo,
                        arrived=lambda k: l * SPLITS + FIRST_SPLIT["y"] + k + 1)
                mod_rows(l, MOD_CHUNKS - 2, two[:, 0, 0:256])
                sums(l, FIRST_USE["norm2"], FIRST_SQ["norm2"], KD, 2)
                mod_fold(l, MOD_CHUNKS - 2, one[0][:, 0:8])
                mod_rows(l, MOD_CHUNKS - 1, two[:, 1, 0:256])
                mod_fold(l, MOD_CHUNKS - 1, one[0][:, 8:16])
                with pe.Fori(0, FF_CHUNKS) as c:
                    project(l, FIRST_USE["ff"], FIRST_BLOCK["ff"], 8, KD, act_hi, act_lo,
                            arrived=lambda k: l * SPLITS + (FIRST_SPLIT["h2"] + k + 1), more_b=c * 16, more_u=c * 8)
                    project(l, FIRST_USE["ff"] + 8, FIRST_BLOCK["ff"] + 8, 8, KD, ff_hi, ff_lo,
                            arrived=lambda k: l * SPLITS + c * 8 + (FIRST_SPLIT["ff"] + k + 1),
                            more_b=c * 16, more_u=c * 8)
            pe.wait_ge(layer_open, DEPTH + 1)
            sums(DEPTH, 0, 0, KD, 1)

        @block.scalar
        def _(act):
            f = nc.scalar.activation

            def squares(l, first_sq, tiles, sources_wait=True, only=None):
                for k, ap in enumerate(tiles):
                    if only is not None and k not in only:
                        continue
                    if sources_wait is not None:
                        act.wait_ge(src_ready, sources_wait(k))
                    if k >= 2:
                        act.wait_ge(sq_used, l * SQ_USED + FIRST_SQ_USED[first_sq] + k - 1)
                    f(sq[:, k % 2, :], ap, ACT.Square).then_inc(sq_ready, 1)

            def inverse_root(l, use, norm, n):
                t, b, _ = buf(use)
                act.wait_ge(rs_used, l * N_NORMS + norm + 1)
                wait_ready(act, l, use)
                f(two_parts(rs[:, :]), halves(t), ACT.Ln, bias=eps, scale=1.0 / n).then_inc(free[b], 1)
                act.drain()
                f(rs[:, :], rs[:, :], ACT.Exp, scale=-0.5).then_inc(rs_ready, 1)

            def small_root(l, t, norm, n):
                act.wait_ge(rs_used, l * N_NORMS + norm + 1)
                act.wait_ge(small_sum, l * 2 + norm - NORMS["kn"] + 1)
                f(two_parts(rs[:, :]), halves(t), ACT.Ln, bias=eps, scale=1.0 / n)
                act.drain()
                f(rs[:, :], rs[:, :], ACT.Exp, scale=-0.5).then_inc(rs_ready, 1)

            def head_square(l, name, tiles, h):
                act.wait_ge(src_ready, l * 16 + HEAD_NORMS[name] + h + 1)
                f(sq[:, h % 2, :], tiles[:, h, :], ACT.Square).then_inc(sq_ready, 1)

            def head_root(l, name, h):
                act.wait_ge(rs_used, l * N_NORMS + NORMS[name] + h + 1)
                act.wait_ge(head_sum, l * 8 + HEAD_NORMS[name] + h + 1)
                f(two_parts(rs[:, :]), halves((two, last_two)[h % 2]), ACT.Ln, bias=eps, scale=1.0 / P)\
                    .then_inc(head_sum_free, 1)
                act.drain()
                f(rs[:, :], rs[:, :], ACT.Exp, scale=-0.5).then_inc(rs_ready, 1)

            def head_hi(l, split_name, tiles, hi, h):
                act.wait_ge(whole, l * SPLITS + FIRST_SPLIT[split_name] + h + 1)
                f(hi[:, h, :], tiles[:, h, :], ACT.Copy).then_inc(hi_done, 1)

            def round_tiles(l, name, pairs, scale=None):
                for k, (hi, src) in enumerate(pairs):
                    act.wait_ge(whole, l * SPLITS + FIRST_SPLIT[name] + k + 1)
                    f(hi, src, ACT.Copy, scale=1.0 if scale is None else scale).then_inc(hi_done, 1)

            def gate(l, name, first_gate, m):
                use = place_in(FIRST_USE, name, 4 * (m // 2) + m % 2)
                wait_ready(act, l, use)
                act.wait_ge(y_done, l * 24 + first_gate + m + 1)
                t, b, _ = buf(use)
                f(two_parts(stage[:, m % 2, :]), halves(t), ACT.Tanh, scale=0.5).then_inc(free[b], 1)
                act.drain().then_inc(gate_ready, 1)

            def merge(l, name, first_gate, start=0, behind=None):
                for m in range(start, 8):
                    gate(l, name, first_gate, m)
                    if behind:
                        behind(m)

            def attend(l, name, maps, side, unit0, set0, heads, prob, probT, exp0):
                units = attention_units(heads, side)

                def exps(i):
                    h, t = units[i]
                    if i >= 3:
                        act.wait_ge(pT_ready, l * 60 + unit0 + i - 2)
                    for m in range(maps):
                        use = FIRST_USE[name] + maps * i + m
                        ps, b, _ = buf(use)
                        col = 2 * (i % 2) + m
                        act.wait_ge(maxed, l * 80 + exp0 + maps * i + m + 1)
                        dst = prob_tile(prob, maps, i, m)
                        if t == LATE:
                            out, src = dst[:, 0:CTX], ps[:, 0, 0:CTX]
                        else:
                            out, src = two_parts(dst), halves(ps)
                        f(out, src, ACT.Exp, bias=neg_max[:, col:col + 1],
                          accum_out=row_sum[:, col:col + 1]).then_inc(free[b], 1)
                        act.drain().then_inc(exped, 1)

                def copyT(i):
                    h, t = units[i]
                    act.wait_ge(pT_ready, l * 60 + unit0 + i + 1)
                    if i >= 2 * side:
                        act.wait_ge(o_ready, l * 60 + unit0 + side * (i // side - 1))
                    n = CTX if t == LATE else T
                    f(probT[:, i % (2 * side), :, :].rearrange("p c q -> p (c q)")[:, 0:n],
                      two[:, :, :].rearrange("p a c -> p (a c)")[:, 0:n], ACT.Copy).then_inc(pT_copied, 1)

                n = len(units)
                for i in range(-1, n + 1):
                    if i >= 1 and maps == 1:
                        copyT(i - 1)
                    if i + 1 < n:
                        exps(i + 1)
                    if i >= 1 and maps == 2:
                        copyT(i - 1)

            act.dma_start(cond[:, :, :], condT).then_inc(cond_loaded, 16)
            act.dma_start(x[:, :, :], xT).then_inc(x_loaded, 16)
            act.dma_start(cst[:, :], consts).then_inc(cst_loaded, 16)
            act.wait_ge(cond_loaded, 16)
            f(t1[:, 0:32 * KD].rearrange("p (k g) -> p k g", g=32), cond[:, :, :], ACT.Tanh, scale=0.5).then_inc(cond_done, 1)
            act.wait_ge(x_loaded, 16)
            act.wait_ge(cst_loaded, 16)
            act.wait_ge(started, 1)
            with act.Fori(0, DEPTH) as l:
                act.wait_ge(layer_open, l + 1)
                act.dma_start(small[:, :], small_d[l]).then_inc(small_loaded, 16)
                act.wait_ge(lam_sums, l + 1)
                f(lam_tmp[:, 0:2], lam_tmp[:, 0:2], ACT.Exp).then_inc(lam_exps, 1)
                def keep_row(c, src):
                    act.wait_ge(row_ready, l * MOD_CHUNKS + c + 1)
                    act.wait_ge(row_free, l * MOD_CHUNKS + c + 1)
                    f(mod_row[:, c % 2, :], src, ACT.Copy).then_inc(row_copied, 1)

                x_tiles = [x[:, k, :] for k in range(KD)]
                squares(l, FIRST_SQ["norm1"], x_tiles, None, range(0, 5))
                keep_row(0, two[:, 0, 0:256])
                squares(l, FIRST_SQ["norm1"], x_tiles, None, range(5, KD))
                keep_row(1, two[:, 1, 0:256])
                inverse_root(l, FIRST_USE["norm1"], NORMS["norm1"], D)
                for c in (2, 3):
                    keep_row(c, two[:, c % 2, 0:256])
                round_tiles(l, "h1", [(act_hi[:, k, :], stage[:, k % 2, :]) for k in range(KD)])

                keep_row(4, two[:, 1, 0:256])

                wait_ready(act, l, FIRST_USE["mv"])
                wait_ready(act, l, FIRST_USE["mv"] + 1)
                f(vm[:, 0:2, :], big[0][:, :, :], ACT.Copy).then_inc(free[0], 1)
                f(vm[:, 2:4, :], big[1][:, :, :], ACT.Copy).then_inc(free[1], 1)
                f(vm[:, 4, :], two[:, 0, :], ACT.Copy).then_inc(vm_ready, 1)
                act.wait_ge(gate_rows, l + 1)
                f(rows[5][:, :], rows[1][:, :], ACT.Abs)
                act.drain()
                f(rows[5][:, :], rows[5][:, :], ACT.Exp, scale=-1.0)
                act.drain()
                f(rows[5][:, :], rows[5][:, :], ACT.Ln, bias=ones[0:ROWS, 0:1]).then_inc(soft_rows, 1)
                for m in range(2):
                    wait_ready(act, l, FIRST_USE["mq"] + m)
                    t, b, _ = buf(FIRST_USE["mq"] + m)
                    for g in range(2):
                        r = slice(64 * g, 64 * g + 64)
                        last = f(two_parts(q_head[2 * m + g][r, :]), halves(t)[r], ACT.Copy, scale=DK_M ** -0.5)
                    last.then_inc(free[b], 1)
                for m in range(2):
                    wait_ready(act, l, FIRST_USE["mk"] + m)
                    t, b, _ = buf(FIRST_USE["mk"] + m)
                    f(two_parts(km[:, m, :]), halves(t), ACT.Copy).then_inc(free[b], 1)
                act.drain().then_inc(qk_ready, 1)
                for m in range(4):
                    wait_ready(act, l, FIRST_USE["mo"] + m)
                    t, b, _ = buf(FIRST_USE["mo"] + m)
                    f(two_parts(mo_th[:, m, :]), halves(t), ACT.Tanh, scale=0.5).then_inc(free[b], 1)
                act.wait_ge(rows_ready, l + 1)
                f(rows[5][:, :], rows[1][:, :], ACT.Exp, scale=-1.0).then_inc(expm_ready, 1)
                act.dma_start(o_m[l, 0:H_M, :], rows[1][0:H_M, CTX - 1:CTX]).then_inc(state_stored, 16)
                act.dma_start(o_m[l, H_M:UNITS, :], rows[1][32:32 + H_M, 0:1]).then_inc(state_stored, 16)
                act.wait_ge(colsT_ready, l + 1)
                f(acol[:, :, :], two[:, 1, 0:5 * ROWS].rearrange("p (t r) -> p t r", r=ROWS), ACT.Copy)
                f(ktok[:, :], two[:, 0, 0:256], ACT.Copy)
                act.drain().then_inc(colsT_copied, 1)

                def unit_start(u):
                    _, h, par, pair, _ = unit(u)
                    bc = nMbc[u % 2]
                    act.wait_ge(bc_ready, l * UNITS + u + 1)
                    if u >= 2:
                        act.wait_ge(arg_ready, l * 40 + 5 * (u - 1))
                    f(bc[:, CTX:T], two[:, 0, :], ACT.Copy)
                    f(bc[:, 0:CTX], two[:, 1, 0:CTX], ACT.Copy)
                    act.drain().then_inc(bc_copied, 1)
                    if u:
                        act.wait_ge(a_used, l * (4 * UNITS) + 4 * (u - 1) + 1)
                    f(qw[:, :], bc[:, CTX:T], ACT.Exp, bias=s_("m0")[:, u:u + 1])\
                        .then_inc(w_inter_ready, 1)

                def keep_latent(u):
                    act.wait_ge(a_used, l * (4 * UNITS) + 4 * u + 4)
                    f(num_sb[:, u, CTX:T], one[0][:, :], ACT.Copy).then_inc(num_copied, 1)

                def keep_context(u):
                    act.wait_ge(num_ready, l * UNITS + u + 1)
                    f(num_sb[:, u, 0:CTX], one[1][:, 0:CTX], ACT.Copy).then_inc(num_copied, 1)

                unit_start(0)
                for i in range(40):
                    u, j = divmod(i, 5)
                    if j == 2 and u + 1 < UNITS:
                        unit_start(u + 1)
                    act.wait_ge(arg_ready, l * 40 + i + 1)
                    n = CTX if j == LATE else (LAT - P * j if u < H_M else P * (j + 1))
                    f(ebuf[:, i % 2, 0:n], ebuf[:, i % 2, 0:n], ACT.Exp).then_inc(e_ready, 1)
                    if j == 0 and u:
                        keep_context(u - 1)
                    if j == LATE:
                        keep_latent(u)
                        if u < 5:
                            keep_row(5 + u, two[:, 0, 0:256])
                keep_context(UNITS - 1)
                act.wait_ge(state_ready, l + 1)
                f(c_new[:, 0:4, :], two[0:DK_M, 0, :].rearrange("p (u e) -> p u e", e=DV_M), ACT.Copy)
                f(c_new[:, 4:8, :], two[0:DK_M, 1, :].rearrange("p (u e) -> p u e", e=DV_M), ACT.Copy)
                f(n_new[:, :], one[1][0:DK_M, 0:UNITS], ACT.Copy).then_inc(state_copied, 1)
                act.wait_ge(state_copied, l + 1)
                act.dma_start(o_C[l], c_new[:, :, :]).then_inc(state_stored, 16)
                act.dma_start(o_n[l], n_new[:, :]).then_inc(state_stored, 16)
                for k in range(KQ):
                    wait_ready(act, l, FIRST_USE["acq"] + k)
                    t, b, _ = buf(FIRST_USE["acq"] + k)
                    f(two_parts(acq[:, k, :]), halves(t), ACT.Copy).then_inc(free[b], 1)
                head_square(l, "mn", num_sb, 0)
                head_square(l, "mn", num_sb, 1)
                for h in range(H_M):
                    head_root(l, "mn", h)
                    if h + 2 < H_M:
                        head_square(l, "mn", num_sb, h + 2)
                    head_hi(l, "om", num_sb, om_hi, h)
                    if h == 1:
                        gate(l, "merge_m", 0, 0)

                def behind_gate_m(m):
                    if m == 1:
                        act.wait_ge(state_stored, l * 64 + 64)
                        act.dma_start(ckv[:, :, T:TK], past_d[l, :, PAST_C["ckv"][0]:PAST_C["ckv"][1]]
                                      .rearrange("p (k t) -> p k t", t=PAST)).then_inc(past_loaded, 16)
                        for k in range(KKV):
                            wait_ready(act, l, FIRST_USE["ckv"] + k)
                            t, b, _ = buf(FIRST_USE["ckv"] + k)
                            f(two_parts(ckv[:, k, 0:T]), halves(t), ACT.Copy).then_inc(free[b], 1)
                        act.drain()
                    if m == 3:
                        squares(l, FIRST_SQ["kn"], [ckv[:, k, 0:T] for k in range(KKV)], None)
                        small_root(l, two, NORMS["kn"], KV_RANK)
                        act.wait_ge(past_loaded, l * 64 + 16)
                        round_tiles(l, "kv", [(ckv_hi[:, k, :], ckv[:, k, :]) for k in range(KKV)])
                    if m == 5:
                        squares(l, FIRST_SQ["qn"], [acq[:, k, :] for k in range(KQ)], None)
                        small_root(l, last_two, NORMS["qn"], Q_RANK)
                        round_tiles(l, "q", [(qn_hi[:, k, :], acq[:, k, :]) for k in range(KQ)])
                merge(l, "merge_m", 0, 1, behind_gate_m)
                act.dma_start(o_ckv[l], ckv[:, :, 0:CTX]).then_inc(ckv_stored, 16)

                scale = (NOPE + ROPE) ** -0.5
                for m in range(8):
                    use = FIRST_USE["qup"] + m
                    wait_ready(act, l, use)
                    t, b, _ = buf(use)
                    if m < 4:
                        f(two_parts(q_a[0:64, 2 * m, :]), halves(t)[0:64], ACT.Copy, scale=scale)
                        f(two_parts(q_a[0:64, 2 * m + 1, :]), halves(t)[64:128], ACT.Copy, scale=scale)\
                            .then_inc(free[b], 1)
                    else:
                        if m >= 6:
                            act.wait_ge(roped, l * 11 + 1)
                        f(two_parts(stage[:, m % 2, :]), halves(t), ACT.Copy, scale=scale).then_inc(free[b], 1)
                        if m % 2:
                            act.drain().then_inc(raw_kept, 1)
                use = FIRST_USE["kr"]
                act.wait_ge(roped, l * 11 + 2)
                wait_ready(act, l, use)
                t, b, _ = buf(use)
                act.dma_start(k_a[64:96, 0, T:TK], past_d[l, 64:96, PAST_C["kr"][0]:PAST_C["kr"][1]])\
                    .then_inc(past_loaded, 16)
                f(two_parts(stage[64:128, 0, :]), halves(t)[64:128], ACT.Copy).then_inc(free[b], 1)
                act.drain().then_inc(raw_kept, 1)
                act.dma_start(o_kr[l], stage[64:96, 0, 0:CTX]).then_inc(kr_stored, 16)
                for m in range(4):
                    use = FIRST_USE["kvn"] + m
                    wait_ready(act, l, use)
                    t, b, _ = buf(use)
                    f(two_parts(k_a[0:64, 2 * m, :], TK // 2), halves(t, TK // 2)[0:64], ACT.Copy)
                    f(two_parts(k_a[0:64, 2 * m + 1, :], TK // 2), halves(t, TK // 2)[64:128], ACT.Copy)\
                        .then_inc(free[b], 1)
                act.drain().then_inc(kn_copied, 1)
                attend(l, "ma", 1, 2, 0, 0, H_A, prob_a, probT_a, 0)
                act.wait_ge(kr_stored, l * 16 + 16)
                act.wait_ge(ckv_stored, l * 16 + 16)
                round_tiles(l, "oa", [(oa_hi[:, k, :], o_a[:, k, :]) for k in range(4)])
                act.wait_ge(lo_done, l * SPLITS + FIRST_SPLIT["oa"] + 4)

                act.dma_start(v_d[:, 5, :], past_d[l, :, PAST_C["dv"][0]:PAST_C["dv"][1]]).then_inc(past_loaded, 16)
                act.dma_start(k_d[:, :, T:TK], past_d[l, :, PAST_C["dk"][0]:PAST_C["dk"][1]]
                              .rearrange("p (k t) -> p k t", t=PAST)).then_inc(past_loaded, 16)
                for m in range(8):
                    use = FIRST_USE["dq"] + m
                    wait_ready(act, l, use)
                    act.wait_ge(roped, l * 11 + 3 + max(m - 1, 0))
                    t, b, _ = buf(use)
                    f(two_parts(stage[:, m % 2, :]), halves(t), ACT.Copy, scale=DK_D ** -0.5 if m < 4 else 1.0)\
                        .then_inc(free[b], 1)
                    act.drain().then_inc(raw_kept, 1)
                act.wait_ge(roped, l * 11 + 11)
                act.dma_start(o_dk[l], k_d[:, :, 0:CTX]).then_inc(diff_stored, 16)
                wait_ready(act, l, FIRST_USE["dv"])
                wait_ready(act, l, FIRST_USE["dv"] + 1)
                f(v_d[:, 0:2, :], big[0][:, :, :], ACT.Copy).then_inc(free[0], 1)
                f(v_d[:, 2:4, :], big[1][:, :, :], ACT.Copy).then_inc(free[1], 1)
                f(v_d[:, 4, :], two[:, 0, :], ACT.Copy)
                act.drain().then_inc(v_copied, 1)
                act.dma_start(o_dv[l], v_d[:, 0, :]).then_inc(diff_stored, 16)
                attend(l, "da", 2, 1, 40, 4, H_D, prob_d, probT_d, 40)
                act.wait_ge(diff_stored, l * 32 + 32)

                def behind_gate_a(m):
                    if m % 2:
                        h = m // 2
                        head_square(l, "dn", q_d, h)
                        head_root(l, "dn", h)
                        head_hi(l, "od", q_d, od_hi, h)
                merge(l, "merge_a", 8, 0, behind_gate_a)
                merge(l, "merge_d", 16)

                round_tiles(l, "y", [(act_hi[:, k, :], y[:, k, :]) for k in range(KD)], scale=0.5)
                squares(l, FIRST_SQ["norm2"], [x[:, k, :] for k in range(KD)],
                        lambda k: l * 16 + 8 + k + 1)
                keep_row(MOD_CHUNKS - 2, two[:, 0, 0:256])
                inverse_root(l, FIRST_USE["norm2"], NORMS["norm2"], D)
                keep_row(MOD_CHUNKS - 1, two[:, 1, 0:256])
                for k in range(KD):
                    act.wait_ge(whole, l * SPLITS + FIRST_SPLIT["h2"] + k + 1)
                    for g, a, b in GROUPS:
                        last = f(act_hi[:, k, a:b], y[:, k, a:b], ACT.Identity, bias=mod[:, 24 + k, g:g + 1])
                    last.then_inc(hi_done, 1)
                with act.Fori(0, FF_CHUNKS) as c:
                    def relu(m):
                        use = FIRST_USE["ff"] + m
                        wait_ready(act, l, use, c * 8)
                        act.wait_ge(relu_used, l * 32 + c * 8 + (m + 1))
                        t, b, _ = buf(use)
                        f(two_parts(sq[:, m % 2, :]), halves(t), ACT.Relu).then_inc(free[b], 1)
                        act.drain().then_inc(relu_ready, 1)

                    def round_ff(m):
                        act.wait_ge(whole, l * SPLITS + c * 8 + (FIRST_SPLIT["ff"] + m + 1))
                        f(ff_hi[:, m, :], stage[:, m % 2, :], ACT.Copy).then_inc(hi_done, 1)
                    relu(0)
                    for m in range(8):
                        if m + 1 < 8:
                            relu(m + 1)
                        round_ff(m)
            act.wait_ge(layer_open, DEPTH + 1)
            squares(DEPTH, 0, [x[:, k, :] for k in range(KD)], None)
            inverse_root(DEPTH, 0, 0, D)

        @block.vector
        def _(dve):
            v = nc.vector

            def remainder(l, name, k, lo, src, hi, more=0):
                dve.wait_ge(hi_done, l * SPLITS + more + (FIRST_SPLIT[name] + k + 1))
                v.tensor_tensor(lo, src, hi.bitcast(f32), ALU.subtract).then_inc(lo_done, 1)

            def gather(l, first_sq, k):
                if 0 < k < KD - 1:
                    dve.wait_ge(sq_ready, l * SQUARES + first_sq + k + 1)
                    v.tensor_tensor(t1[:, :], sq[:, 0, :] if k == 1 else t1[:, :], sq[:, k % 2, :], ALU.add)\
                        .then_inc(sq_used, 2 if k == 1 else 1)
                    dve.drain()
                    if k == KD - 2:
                        dve.drain().then_inc(gather_done, 1)

            def merge(l, name, first_gate, behind=None):
                for m in range(8):
                    gate, use = first_gate + m, place_in(FIRST_USE, name, 4 * (m // 2) + 2 + m % 2)
                    dve.wait_ge(gate_ready, l * 24 + gate + 1)
                    wait_ready(dve, l, use)
                    t, b, _ = buf(use)
                    dst = y[:, m, :] if first_gate == 0 else t1[:, :]
                    v.scalar_tensor_tensor(two_parts(dst), two_parts(stage[:, m % 2, :]), 1.0, halves(t), ALU.add,
                                           ALU.mult).then_inc(free[b], 1)
                    dve.drain()
                    if first_gate == 0:
                        dve.drain().then_inc(y_done, 1)
                    else:
                        v.tensor_tensor(y[:, m, :], y[:, m, :], t1[:, :], ALU.add).then_inc(y_done, 1)
                        dve.drain()
                    if first_gate == 16:
                        dve.drain().then_inc(whole, 1)
                    if behind:
                        behind(m)

            def attend(l, name, maps, side, unit0, set0, heads, prob, exp0, out, lay_out=None):
                units = attention_units(heads, side)

                def maxes(i):
                    h, t = units[i]
                    for m in range(maps):
                        use = FIRST_USE[name] + maps * i + m
                        wait_ready(dve, l, use)
                        ps, b, _ = buf(use)
                        col = 2 * (i % 2) + m
                        src = ps[:, 0, 0:CTX] if t == LATE else halves(ps)
                        v.tensor_reduce(neg_max[:, col:col + 1], src, AX.X if t == LATE else AX.XY, ALU.max,
                                        negate=True).then_inc(maxed, 1)

                def normalise(i):
                    h, t = units[i]
                    n = CTX if t == LATE else T
                    c0 = 2 * (i % 2)
                    dve.wait_ge(exped, l * 80 + exp0 + maps * (i + 1))
                    v.reciprocal(row_sum[:, c0:c0 + maps], row_sum[:, c0:c0 + maps])
                    dve.drain()
                    p0 = prob_tile(prob, maps, i, 0)[:, 0:n]
                    if maps == 1:
                        v.tensor_scalar(p0, p0, row_sum[:, c0:c0 + 1], None, ALU.mult).then_inc(p_ready, 1)
                    else:
                        p1 = prob_tile(prob, maps, i, 1)[:, 0:n]
                        v.tensor_scalar(p1, p1, row_sum[:, c0 + 1:c0 + 2], neg_lam, ALU.mult, ALU.mult)
                        dve.drain()
                        v.scalar_tensor_tensor(p0, p0, row_sum[:, c0:c0 + 1], p1, ALU.mult, ALU.add)\
                            .then_inc(p_ready, 1)
                    dve.drain()

                def outputs(j):
                    p, t = divmod(j, 5)
                    if t >= LATE - 1:
                        dve.wait_ge(o_ready, l * 60 + unit0 + side * (j + 1))
                        v.tensor_copy(*((out[:, p, 0:CTX], one[1][:, 0:CTX]) if t == LATE else
                                        (out[:, p, CTX:T], one[0][:, :]))).then_inc(o_copied, 1)

                n = len(units)
                for i in range(-1, n + 3):
                    if i + 1 < n:
                        maxes(i + 1)
                        h, t = units[i + 1]
                        if maps == 2 and t == LATE and h + 2 < heads:
                            lay_out(h + 2)
                    if 0 <= i < n:
                        normalise(i)
                    if i >= side + 2 and i % side == 0:
                        outputs((i - side - 2) // side)
                dve.drain()

            for s, n in ((split_ready, RAW), (block_used, 1), (free[0], 1), (free[1], 1), (row_free, 2), (rs_used, 1),
                         (y_done, 2), (relu_used, 2)):
                v.memset(cols[:, 0:1], 0.0).then_inc(s, n)
                dve.drain()
            v.memset(cols[:, 0:1], 0.0).then_inc(started, 1)
            dve.wait_ge(cond_done, 1)
            silu = t1[:, 0:32 * KD].rearrange("p (k g) -> p k g", g=32)
            v.scalar_tensor_tensor(silu, silu, 1.0, cond[:, :, :], ALU.add, ALU.mult)
            dve.drain()
            v.tensor_scalar(cond[:, :, :], silu, 0.5, None, ALU.mult).then_inc(silu_done, 1)
            dve.wait_ge(cst_loaded, 16)
            dve.wait_ge(x_loaded, 16)
            dve.drain()
            v.memset(cols[:, 0:32], 0.0).then_inc(layer_open, 1)
            with dve.Fori(0, DEPTH) as l:
                dve.wait_ge(small_loaded, l * 16 + 16)
                lam = s_("lam").rearrange("p (a d) -> p a d", d=DK_D)
                v.tensor_tensor(t2[:, 0:64], lam[:, 0, :], lam[:, 1, :], ALU.mult)
                v.tensor_tensor(t2[:, 64:128], lam[:, 2, :], lam[:, 3, :], ALU.mult)
                dve.drain()
                v.tensor_reduce(lam_tmp[:, 0:2], t2[:, 0:128].rearrange("p (a d) -> p a d", d=64), AX.X, ALU.add)\
                    .then_inc(lam_sums, 1)
                dve.wait_ge(lam_exps, l + 1)
                v.tensor_tensor(lam_tmp[:, 2:3], lam_tmp[:, 1:2], lam_tmp[:, 0:1], ALU.subtract)
                dve.drain()
                v.tensor_tensor(neg_lam, lam_tmp[:, 2:3], s_("lam_init")[:, 0:1], ALU.subtract)
                v.tensor_scalar(g_half, s_("ng_m"), 0.5, None, ALU.mult)
                v.tensor_scalar(g_diff, s_("ng_d"), s_("lam_init")[:, 1:2], None, ALU.mult)

                def keep_mod(a, z, src, scale, j, g):
                    v.tensor_tensor(mod[:, a:z, :], src.rearrange("p (j g) -> p j g", g=2),
                                           s_("bmod")[:, a:z].unsqueeze(2).to_broadcast([P, z - a, 2]), ALU.add)
                    dve.drain()
                    if scale is None:
                        return
                    v.scalar_tensor_tensor(scale[:, :, :], mod[:, 8 * j:8 * j + 8, :], 1.0,
                                           s_(g).unsqueeze(2).to_broadcast([P, KD, 2]), ALU.add, ALU.mult)
                    dve.drain()
                for k in range(KD):
                    gather(l, FIRST_SQ["norm1"], k)
                dve.wait_ge(rs_ready, l * N_NORMS + NORMS["norm1"] + 1)
                for k in range(KD):
                    v.tensor_tensor(y[:, k, :], x[:, k, :], rs[:, :], ALU.mult)
                dve.drain().then_inc(rs_used, 1)
                dve.wait_ge(row_free, l * MOD_CHUNKS + 2 + MOD_A // 4)
                keep_mod(0, 2 * KD, one[0][:, 0:4 * KD], scale1, 1, "n1")
                for k in range(KD + 1):
                    if k < KD:
                        for g, a, b in GROUPS:
                            last = v.tensor_scalar(stage[:, k % 2, a:b], y[:, k, a:b], scale1[:, k, g:g + 1],
                                                   mod[:, k, g:g + 1], ALU.mult, ALU.add)
                        last.then_inc(whole, 1)
                    if k:
                        remainder(l, "h1", k - 1, act_lo[:, k - 1, :], stage[:, (k - 1) % 2, :], act_hi[:, k - 1, :])
                    dve.drain()

                for h in range(H_M):
                    other = 64 * (1 - h % 2)
                    v.memset(q_head[h][other:other + 64, :], 0.0)

                use = FIRST_USE["mg"]
                wait_ready(dve, l, use)
                t, b, _ = buf(use)
                v.tensor_scalar(two_parts(rows[0][:, :]), halves(t)[0:ROWS], s_("gb")[0:ROWS, 0:1], None, ALU.add)
                v.tensor_scalar(two_parts(rows[1][:, :]), halves(t)[64:64 + ROWS], s_("gb")[64:64 + ROWS, 1:2], None,
                                ALU.add).then_inc(free[b], 1)
                v.memset(rows_full[2][:, :], 0.0)
                v.memset(rows_full[4][:, :], 0.0)
                v.memset(rows[3][:, :], 1.0)
                dve.drain().then_inc(gate_rows, 1)
                dve.wait_ge(soft_rows, l + 1)
                v.tensor_scalar(rows[1][:, :], rows[1][:, :], 0.0, None, ALU.min)
                dve.drain()
                v.tensor_tensor(rows[1][:, :], rows[1][:, :], rows[5][:, :], ALU.subtract)
                dve.drain()

                def scans(dst, data0, data1, op0, op1, first):
                    for r, a, b_, back in ((0, 0, CTX, 0), (0, CTX, T, 0), (32, 0, CTX, 1), (32, CTX, T, 1)):
                        def w(tile):
                            ap = tile[r:r + H_M, a:b_]
                            return ap[:, ::-1] if back else ap
                        init = 0.0 if first is None or a == 0 else first[r:r + H_M, 0:1]
                        v.tensor_tensor_scan(w(dst), w(data0), w(data1), init, op0, op1)
                    dve.drain()
                scans(rows[2], rows[3], rows[1], ALU.mult, ALU.add, None)
                v.tensor_tensor(rows[0][:, :], rows[0][:, :], rows[2][:, :], ALU.subtract)
                dve.drain()
                scans(rows[3], rows[0], rows[0], ALU.max, ALU.max, s_("m0row"))
                v.tensor_tensor(rows[1][:, :], rows[2][:, :], rows[3][:, :], ALU.add)
                v.tensor_scalar(rows[4][:, :], rows[3][:, :], -1.0, None, ALU.mult)
                dve.drain().then_inc(rows_ready, 1)
                dve.wait_ge(colsT_copied, l + 1)

                def argument(i):
                    u, j = divmod(i, 5)
                    _, h, par, pair, row = unit(u)
                    bc = nMbc[u % 2]
                    if i >= 2:
                        dve.wait_ge(e_ready, l * 40 + i - 1)
                    mask = c_("mask_f") if u < H_M else c_("mask_b")
                    if j == 0:
                        dve.wait_ge(bc_copied, l * UNITS + u + 1)
                        dve.wait_ge(w_inter_ready, l * UNITS + u + 1)
                        v.tensor_tensor(qw[:, :], qw[:, :], q_head[h][:, CTX:T], ALU.mult).then_inc(qw_ready, 1)
                    s = acol[:, 0 if j == LATE else j + 1, row:row + 1]
                    e = ebuf[:, i % 2, :]
                    if j == LATE:
                        v.scalar_tensor_tensor(e[:, 0:P], bc[:, 0:CTX], s, mask, ALU.add, ALU.min)
                    else:
                        q0 = CTX + P * j
                        if u < H_M:
                            v.scalar_tensor_tensor(e[:, 0:P], bc[:, q0:q0 + P], s, mask, ALU.add, ALU.min)
                            if j < 3:
                                v.tensor_scalar(e[:, P:T - q0], bc[:, q0 + P:T], s, 0.0, ALU.add, ALU.min)
                        else:
                            v.scalar_tensor_tensor(e[:, P * j:P * j + P], bc[:, q0:q0 + P], s, mask, ALU.add, ALU.min)
                            if j:
                                v.tensor_scalar(e[:, 0:P * j], bc[:, CTX:q0], s, 0.0, ALU.add, ALU.min)
                    dve.drain().then_inc(arg_ready, 1)

                def product(i):
                    u, j = divmod(i, 5)
                    _, h, _, _, _ = unit(u)
                    use = FIRST_USE["ms"] + i
                    t, b, _ = buf(use)
                    n = CTX if j == LATE else (LAT - P * j if u < H_M else P * (j + 1))
                    wait_ready(dve, l, use)
                    dve.wait_ge(e_ready, l * 40 + i + 1)
                    if i >= 2:
                        pu, pj = divmod(i - 2, 5)
                        if pj == LATE:
                            dve.wait_ge(num_ready, l * UNITS + pu + 1)
                        else:
                            dve.wait_ge(a_used, l * (4 * UNITS) + 4 * pu + pj + 1)
                    v.tensor_tensor(abuf[:, i % 2, 0:n], ebuf[:, i % 2, 0:n], t[:, 0, 0:n], ALU.mult)\
                        .then_inc(free[b], 1)
                    if j == LATE:
                        last_col = CTX - 1 if u < H_M else 0
                        v.tensor_scalar(kw[:, u, :], ktok[:, DK_M * h:DK_M * h + DK_M],
                                        ebuf[:, i % 2, last_col:last_col + 1], None, ALU.mult).then_inc(kw_ready, 1)
                    dve.drain().then_inc(a_ready, 1)

                argument(0)
                for i in range(40):
                    if i == 36:
                        dve.wait_ge(row_free, l * MOD_CHUNKS + MOD_CHUNKS)
                        dve.wait_ge(num_copied, l * 2 * UNITS + 2 * UNITS - 2)
                        keep_mod(2 * KD, 5 * KD, one[1][:, 256:256 + 6 * KD], scale2, 4, "n2")
                        dve.drain().then_inc(mod_kept, 1)
                    if i + 1 < 40:
                        argument(i + 1)
                    product(i)
                dve.wait_ge(num_ready, l * UNITS + UNITS)
                dve.wait_ge(expm_ready, l + 1)
                v.tensor_scalar(rows[2][:, CTX:T], big[0][0:ROWS, 1, :], -1.0, None, ALU.mult)
                v.tensor_scalar(rows[2][:, 0:CTX], big[1][0:ROWS, 1, 0:CTX], -1.0, None, ALU.mult)
                dve.drain()
                v.tensor_tensor(rows[2][:, CTX:T], rows[2][:, CTX:T], big[0][0:ROWS, 1, :], ALU.max)
                v.tensor_tensor(rows[2][:, 0:CTX], rows[2][:, 0:CTX], big[1][0:ROWS, 1, 0:CTX], ALU.max)
                dve.drain().then_inc(den_read, 1)
                v.tensor_tensor(rows[2][:, :], rows[2][:, :], rows[5][:, :], ALU.max)
                dve.drain()
                v.reciprocal(rows[2][:, :], rows[2][:, :]).then_inc(rden_ready, 1)
                dve.wait_ge(num_copied, l * 2 * UNITS + 2 * UNITS)
                for h in range(H_M):
                    for d in range(2):
                        u, use = h + H_M * d, FIRST_USE["mr"] + 2 * h + d
                        wait_ready(dve, l, use)
                        t, b, _ = buf(use)
                        v.tensor_tensor(two_parts(num_sb[:, u, :]), two_parts(num_sb[:, u, :]), halves(t), ALU.mult)\
                            .then_inc(free[b], 1)
                    dve.drain()
                    v.tensor_tensor(num_sb[:, h, :], num_sb[:, h, :], num_sb[:, h + H_M, :], ALU.add)\
                        .then_inc(src_ready, 1)
                dve.wait_ge(state_ready, l + 1)
                for h in range(H_M):
                    dve.wait_ge(rs_ready, l * N_NORMS + NORMS["mn"] + h + 1)
                    v.scalar_tensor_tensor(t1[:, :], num_sb[:, h, :], g_half[:, h:h + 1], rs[:, :], ALU.mult, ALU.mult)
                    dve.drain().then_inc(rs_used, 1)
                    v.scalar_tensor_tensor(num_sb[:, h, :], mo_th[:, h, :], 1.0, t1[:, :], ALU.add, ALU.mult)\
                        .then_inc(whole, 1)
                    dve.drain()
                    remainder(l, "om", h, om_lo[:, h, :], num_sb[:, h, :], om_hi[:, h, :])
                dve.drain()

                def norm_behind(m):
                    if m == 3:
                        dve.wait_ge(rs_ready, l * N_NORMS + NORMS["kn"] + 1)
                        dve.wait_ge(past_loaded, l * 64 + 16)
                        for k in range(KKV):
                            v.scalar_tensor_tensor(ckv[:, k, 0:T], ckv[:, k, 0:T], s_("ng_kv")[:, k:k + 1], rs[:, :],
                                                   ALU.mult, ALU.mult).then_inc(whole, 1)
                        dve.drain().then_inc(rs_used, 1)
                        for k in range(KKV):
                            remainder(l, "kv", k, ckv_lo[:, k, :], ckv[:, k, :], ckv_hi[:, k, :])
                    if m == 5:
                        dve.wait_ge(rs_ready, l * N_NORMS + NORMS["qn"] + 1)
                        for k in range(KQ):
                            v.scalar_tensor_tensor(acq[:, k, :], acq[:, k, :], s_("ng_q")[:, k:k + 1], rs[:, :], ALU.mult,
                                                   ALU.mult).then_inc(whole, 1)
                        dve.drain().then_inc(rs_used, 1)
                        for k in range(KQ):
                            remainder(l, "q", k, qn_lo[:, k, :], acq[:, k, :], qn_hi[:, k, :])
                    dve.drain()
                merge(l, "merge_m", 0, norm_behind)

                for j in range(2):
                    dve.wait_ge(raw_kept, l * 11 + j + 1)
                    v.tensor_tensor(t1[:, CTX:T], stage[:, 0, CTX:T], c_("cos_a"), ALU.mult)
                    v.tensor_tensor(t2[:, CTX:T], stage[:, 1, CTX:T], c_("sin_a"), ALU.mult)
                    dve.drain()
                    for g in range(4):
                        r = slice(32 * g, 32 * g + 32)
                        v.tensor_tensor(q_a[64:96, 4 * j + g, CTX:T], t1[r, CTX:T], t2[r, CTX:T], ALU.add)
                        v.tensor_copy(q_a[64:96, 4 * j + g, 0:CTX], stage[r, 0, 0:CTX])
                    dve.drain().then_inc(roped, 1)
                dve.wait_ge(raw_kept, l * 11 + 3)
                v.tensor_tensor(t1[64:96, CTX:T], stage[64:96, 0, CTX:T], c_("cos_a", slice(64, 96)), ALU.mult)
                v.tensor_tensor(t2[64:96, CTX:T], stage[96:128, 0, CTX:T], c_("sin_a", slice(96, 128)), ALU.mult)
                dve.drain()
                v.tensor_tensor(k_a[64:96, 0, CTX:T], t1[64:96, CTX:T], t2[64:96, CTX:T], ALU.add)
                v.tensor_copy(k_a[64:96, 0, 0:CTX], stage[64:96, 0, 0:CTX])
                dve.drain()
                dve.wait_ge(past_loaded, l * 64 + 32)
                for h in range(1, H_A):
                    v.tensor_copy(k_a[64:96, h, :], k_a[64:96, 0, :])
                dve.drain().then_inc(roped, 1)
                dve.wait_ge(ckv_stored, l * 16 + 16)
                for i in range(3):
                    use = FIRST_USE["kvv"] + i
                    wait_ready(dve, l, use)
                    t, b, _ = buf(use)
                    v.tensor_copy(v_a[:, 2 * i:2 * i + 2, :], t[:, :, :]).then_inc(free[b], 1)
                dve.drain().then_inc(v_copied, 1)

                attend(l, "ma", 1, 2, 0, 0, H_A, prob_a, 0, o_a)
                for k in range(4):
                    dve.drain().then_inc(whole, 1)
                    dve.drain()
                for k in range(4):
                    remainder(l, "oa", k, oa_lo[:, k, :], o_a[:, k, :], oa_hi[:, k, :])
                for m in range(8):
                    dve.wait_ge(raw_kept, l * 11 + 3 + m + 1)
                    dst = q_d[:, m, :] if m < 4 else k_d[:, m - 4, :]
                    src = stage[:, m % 2, :]
                    v.tensor_tensor(t1[:, CTX:T], src[:, CTX:T], c_("cos_d"), ALU.mult)
                    for g in range(4):
                        r, o = slice(32 * g, 32 * g + 32), slice(32 * (g ^ 1), 32 * (g ^ 1) + 32)
                        v.tensor_tensor(t2[o, CTX:T], src[r, CTX:T], c_("sin_d", r), ALU.mult)
                    v.tensor_copy(dst[:, 0:CTX], src[:, 0:CTX])
                    dve.drain()
                    v.tensor_tensor(dst[:, CTX:T], t1[:, CTX:T], t2[:, CTX:T], ALU.add)
                    dve.drain().then_inc(roped, 1)
                for tile in q_map:
                    for m in range(2):
                        other = 64 * (1 - m)
                        v.memset(tile[other:other + 64, m, :], 0.0)

                def lay_out(h):
                    for m in range(2):
                        r = slice(64 * m, 64 * m + 64)
                        v.tensor_copy(q_map[h % 2][r, m, :], q_d[r, h, :])
                    dve.drain().then_inc(q_map_ready, 1)
                lay_out(0)
                lay_out(1)

                attend(l, "da", 2, 1, 40, 4, H_D, prob_d, 40, q_d, lay_out)
                for h in range(H_D):
                    dve.drain().then_inc(src_ready, 1)
                    dve.drain()
                def norm_head(m):
                    if m % 2:
                        h = m // 2
                        dve.wait_ge(rs_ready, l * N_NORMS + NORMS["dn"] + h + 1)
                        v.scalar_tensor_tensor(q_d[:, h, :], q_d[:, h, :], g_diff[:, h:h + 1], rs[:, :], ALU.mult,
                                               ALU.mult).then_inc(whole, 1)
                        dve.drain().then_inc(rs_used, 1)
                        remainder(l, "od", h, od_lo[:, h, :], q_d[:, h, :], od_hi[:, h, :])
                        dve.drain()
                merge(l, "merge_a", 8, norm_head)

                def split_y(m):
                    for k in range(0, 6) if m == 5 else ([m] if m > 5 else []):
                        dve.wait_ge(hi_done, l * SPLITS + FIRST_SPLIT["y"] + k + 1)
                        v.scalar_tensor_tensor(act_lo[:, k, :], y[:, k, :], 0.5, act_hi[:, k, :].bitcast(f32),
                                               ALU.mult, ALU.subtract).then_inc(lo_done, 1)
                    dve.drain()
                merge(l, "merge_d", 16, split_y)


                def add_to_x(l, use, m, gate, more=0):
                    wait_ready(dve, l, use, more)
                    t, b, _ = buf(use)
                    for n, (g, h, a, z) in enumerate(PARTS):
                        o = h * HALF
                        last = v.scalar_tensor_tensor(x[:, m, o + a:o + z], t[:, h, a:z],
                                                      mod[:, 8 * gate + m, g:g + 1], x[:, m, o + a:o + z],
                                                      ALU.mult, ALU.add)
                    return last.then_inc(free[b], 1)
                for m in range(KD):
                    add_to_x(l, FIRST_USE["wout"] + m, m, 2)
                    dve.drain().then_inc(src_ready, 1)
                    for g, a, b in GROUPS:
                        v.tensor_scalar(y[:, m, a:b], x[:, m, a:b], scale2[:, m, g:g + 1], None, ALU.mult)
                    dve.drain()
                    gather(l, FIRST_SQ["norm2"], m - 1)
                dve.wait_ge(rs_ready, l * N_NORMS + NORMS["norm2"] + 1)
                for k in range(KD + 1):
                    if k < KD:
                        v.tensor_tensor(y[:, k, :], y[:, k, :], rs[:, :], ALU.mult).then_inc(whole, 1)
                    if k:
                        dve.wait_ge(hi_done, l * SPLITS + FIRST_SPLIT["h2"] + k)
                        for g, a, b in GROUPS:
                            last = v.scalar_tensor_tensor(act_lo[:, k - 1, a:b], y[:, k - 1, a:b],
                                                          mod[:, 23 + k, g:g + 1],
                                                          act_hi[:, k - 1, a:b].bitcast(f32), ALU.add, ALU.subtract)
                        last.then_inc(lo_done, 1)
                    dve.drain()
                v.memset(cols[:, 31:32], 0.0).then_inc(rs_used, 1)
                dve.wait_ge(row_free, l * MOD_CHUNKS + 2 + MOD_CHUNKS)
                keep_mod(5 * KD, 6 * KD, one[0][:, 0:16], None, 0, None)

                with dve.Fori(0, FF_CHUNKS) as c:
                    for m in range(9):
                        if m < 8:
                            dve.wait_ge(relu_ready, l * 32 + c * 8 + (m + 1))
                            v.tensor_tensor(stage[:, m % 2, :], sq[:, m % 2, :], sq[:, m % 2, :], ALU.mult)\
                                .then_inc(whole, 1)
                            dve.drain().then_inc(relu_used, 1)
                        if m:
                            remainder(l, "ff", m - 1, ff_lo[:, m - 1, :], stage[:, (m - 1) % 2, :],
                                      ff_hi[:, m - 1, :], c * 8)
                            dve.drain()
                    for m in range(8):
                        add_to_x(l, FIRST_USE["ff"] + 8 + m, m, 5, c * 8)
                dve.drain().then_inc(layer_open, 1)
            for k in range(KD):
                gather(DEPTH, 0, k)
            dve.wait_ge(rs_ready, DEPTH * N_NORMS + 1)
            for k in range(KD):
                v.scalar_tensor_tensor(x[:, k, :], x[:, k, :], s_("fin")[:, k:k + 1], rs[:, :], ALU.mult, ALU.mult)\
                    .then_inc(y_final, 1)


def _tiles(w, k0=None):
    kk, n = w.shape
    return w.reshape(kk // P, P, n // P, P).transpose(2, 1, 0, 3)


def _wide(w):
    kk, n = w.shape
    return w.reshape(kk // 256, 2, P, n // 512, 512).transpose(3, 0, 2, 1, 4).reshape(-1, P, BLK)


def _pairs(tiles):
    m, _, k, _ = tiles.shape
    s = tiles.transpose(0, 2, 1, 3).reshape(m * k // 8, 8, P, P)
    return s.transpose(0, 2, 1, 3).reshape(-1, P, BLK)


def _swap(w, n):
    s = w.reshape(w.shape[0], -1, 2, n // 2)[:, :, ::-1, :]
    return s.reshape(w.shape)


def _blocks(i, l):
    w = i["w_in"][l]
    cut = np.cumsum([256, 256, 512, 512, 16, 384, 256, 32, 512, 512, 512])
    mq, mk, mv, mo, mg, acq, ckv, kr, dq, dk, dv, gates = np.split(w, cut, axis=1)
    mgp = np.zeros((D, P), w.dtype)
    for n in range(4):
        mgp[:, 32 * n:32 * n + 4] = mg[:, 4 * n:4 * n + 4]
    krp = np.zeros((D, P), w.dtype)
    krp[:, 64:96], krp[:, 96:128] = kr, _swap(kr, ROPE)
    qu = i["mla_w_q_up"][l].reshape(Q_RANK, H_A, NOPE + ROPE)
    qn, qr = qu[:, :, :NOPE].reshape(Q_RANK, -1), qu[:, :, NOPE:].reshape(Q_RANK, -1)
    qs = _swap(qr, ROPE)
    qall = np.concatenate([qn, qr[:, :P], qs[:, :P], qr[:, P:], qs[:, P:]], axis=1)
    ku = i["mla_w_kv_up"][l].reshape(KV_RANK, H_A, NOPE + V_A)
    kn, kv = ku[:, :, :NOPE].reshape(KV_RANK, -1), ku[:, :, NOPE:].reshape(KV_RANK, -1)

    def merge(g, br):
        gt, bt = _pairs(_tiles(gates[:, D * g:D * g + D])), _pairs(_tiles(br))
        return [b for p in range(4) for b in (gt[2 * p], gt[2 * p + 1], bt[p])]
    f1, f2 = _pairs(_tiles(i["w_ff1"][l])), i["w_ff2"][l]
    merge_m = merge(0, i["w_br_mlstm"][l])
    out = [_wide(mv)] + [_pairs(_tiles(a)) for a in (mgp, mq, mk, mo, acq)] + [merge_m[:2]]
    out += [_pairs(_tiles(ckv)), merge_m[2:]]
    out += [_pairs(_tiles(a)) for a in (qall, krp, kn)] + [_wide(kv)]
    out += [_pairs(_tiles(dq)), _pairs(_tiles(dk)), _wide(dv), merge(1, i["w_br_mla"][l])]
    out += [merge(2, i["w_br_diff"][l]), _pairs(_tiles(i["w_out"][l]))]
    for c in range(FF_CHUNKS):
        out += [f1[8 * c:8 * c + 8], _pairs(_tiles(f2[D * c:D * c + D]))]
    kinds = {"mod": _wide(i["w_mod"][l]),
             "dense": np.concatenate([np.stack(o) if isinstance(o, list) else o for o in out])}
    return np.stack([kinds[kind][index] for kind, index in ORDER])


def _columns_of(a):
    return a.reshape(-1, P).T


def _small(i, l):
    s = np.zeros((P, SMALL_W), np.float32)

    def put(name, a, r=slice(0, P)):
        s[r, SMALL[name][0]:SMALL[name][1]] = a
    for name, key in (("bmod", "b_mod"), ("n1", "norm1_g"), ("n2", "norm2_g"), ("ng_m", "mlstm_norm_g"),
                      ("ng_q", "mla_q_norm_g"), ("ng_kv", "mla_kv_norm_g"), ("ng_d", "diff_norm_g")):
        put(name, _columns_of(i[key][l]))
    put("fin", _columns_of(i["final_norm_g"]))
    gb = i["mlstm_gate_b"][l].reshape(2, 2, H_M)
    m0 = i["state_mlstm_m"][0, l]
    for d in range(2):
        r = slice(32 * d, 32 * d + H_M)
        s[r, SMALL["gb"][0]] = gb[0, d]
        s[64 + 32 * d:64 + 32 * d + H_M, SMALL["gb"][0] + 1] = gb[1, d]
        s[r, SMALL["m0row"][0]] = m0[d]
    put("m0", m0.reshape(1, UNITS))
    put("lam", i["diff_lambda"][l].reshape(1, 256))
    lam_init = 0.8 - 0.6 * math.exp(-0.3 * l)
    put("lam_init", np.array([[lam_init, 1.0 - lam_init]], np.float32))
    n0, c0 = np.zeros((P, 4, ROWS), np.float32), np.zeros((P, 4, DV_M), np.float32)
    for u in range(UNITS):
        d, h, par, pair, row = unit(u)
        n0[par:par + 64, 2 * d + pair, row] = i["state_mlstm_n"][0, l, d, h]
        c0[par:par + 64, 2 * d + pair] = i["state_mlstm_C"][0, l, d, h]
    put("n0", n0.reshape(P, -1))
    put("C0", c0.reshape(P, -1))
    return s


def _past(i, l):
    s = np.zeros((P, PAST_W), np.float32)

    def features(a):
        return a.T.reshape(-1, P, a.shape[0]).transpose(1, 0, 2).reshape(P, -1)
    s[:, PAST_C["ckv"][0]:PAST_C["ckv"][1]] = features(i["cache_mla_ckv"][0, l])
    s[64:96, PAST_C["kr"][0]:PAST_C["kr"][1]] = i["cache_mla_krope"][0, l].T
    s[:, PAST_C["dk"][0]:PAST_C["dk"][1]] = features(i["cache_diff_k"][0, l].reshape(PAST, -1))
    s[:, PAST_C["dv"][0]:PAST_C["dv"][1]] = i["cache_diff_v"][0, l].reshape(PAST, -1)
    return s


def _constants():
    s = np.zeros((P, CONST_W), np.float32)

    def put(name, a, r=slice(0, P)):
        s[r, CONST[name][0]:CONST[name][1]] = a
    t = np.arange(LAT)
    row, col = (t // GRID_W).astype(np.float32), (t % GRID_W).astype(np.float32)
    for name, dim in (("d", DK_D), ("a", ROPE)):
        quarter = dim // 4
        inv = np.float32(ROPE_BASE) ** (-np.arange(quarter, dtype=np.float32) / np.float32(quarter))
        ang = np.concatenate([row[:, None] * inv, col[:, None] * inv], axis=-1).astype(np.float32)
        c, z = np.cos(ang).T, np.sin(ang).T
        put("cos_" + name, np.tile(np.concatenate([c, c]), (P // dim, 1)))
        sign = [z, -z] if name == "d" else [-z, z]
        put("sin_" + name, np.tile(np.concatenate(sign), (P // dim, 1)))
    p, q = np.arange(P)[:, None], np.arange(P)[None, :]
    put("mask_f", np.where(q >= p, 0.0, NEG))
    put("mask_b", np.where(q <= p, 0.0, NEG))
    put("ident", np.eye(P))
    put("ones", 1.0)
    den, rsel = np.zeros((P, UNITS, ROWS)), np.zeros((P, UNITS, P))
    for u in range(UNITS):
        den[:, u, unit(u)[4]] = 1.0
        rsel[unit(u)[4], u, :] = 1.0
    put("den_sel", den.reshape(P, -1))
    put("row_sel", rsel.reshape(P, -1))
    put("fold_sel", np.concatenate([(p % 32 == np.arange(2)) & (p // 64 == half) for half in range(2)], axis=1))
    put("eps", EPS)
    return s


def kernel(**inputs):
    import concourse.bacc as bacc
    from concourse.bass_utils import run_bass_kernel_spmd as run

    i = {k: np.asarray(v) for k, v in inputs.items()}
    f32 = mybir.dt.float32
    tokens = np.concatenate([i["x_prompt"][0], i["x_sample"][0]])
    arrays = {
        "in_x": np.ascontiguousarray(tokens.reshape(T, KD, P).transpose(2, 1, 0)),
        "in_cond": np.ascontiguousarray(np.pad(np.stack([i["c_ctx"], i["c"][0]]), ((0, 30), (0, 0)))
                                        .reshape(32, KD, P).transpose(2, 1, 0)),
        "in_const": _constants(),
        "in_small": np.stack([_small(i, l) for l in range(DEPTH)]),
        "in_past": np.stack([_past(i, l) for l in range(DEPTH)]),
        "in_w": np.stack([_blocks(i, l) for l in range(DEPTH)]),
    }
    outs = {"out_y": (P, KD, T), "out_ckv": (DEPTH, P, KKV, CTX), "out_kr": (DEPTH, ROPE, CTX),
            "out_dk": (DEPTH, P, 4, CTX), "out_dv": (DEPTH, CTX, 512), "out_C": (DEPTH, DK_M, UNITS, DV_M),
            "out_n": (DEPTH, DK_M, UNITS), "out_m": (DEPTH, UNITS, 1)}
    nc = bacc.Bacc("TRN2", target_bir_lowering=False, num_devices=1, dynamic_dma_scratch_size=1024)
    args = [nc.dram_tensor(n, a.shape, f32, kind="ExternalInput").ap() for n, a in arrays.items()]
    args += [nc.dram_tensor(n, s, f32, kind="ExternalOutput").ap() for n, s in outs.items()]
    trunk(nc, *args)
    r = run(nc, [arrays], core_ids=[0]).results[0]

    y = r["out_y"].transpose(2, 1, 0).reshape(T, D)
    ckv = r["out_ckv"].transpose(0, 3, 2, 1).reshape(1, DEPTH, CTX, KV_RANK)
    kr = r["out_kr"].transpose(0, 2, 1)[None]
    dk = r["out_dk"].transpose(0, 3, 2, 1).reshape(1, DEPTH, CTX, H_D, 2 * DK_D)
    dv = r["out_dv"].reshape(1, DEPTH, CTX, H_D, DV_D)
    c_new = r["out_C"].transpose(0, 2, 1, 3).reshape(1, DEPTH, 2, H_M, DK_M, DV_M)
    n_new = r["out_n"].transpose(0, 2, 1).reshape(1, DEPTH, 2, H_M, DK_M)
    m_new = r["out_m"].reshape(1, DEPTH, 2, H_M)
    return y[None, :CTX], y[None, CTX:], ckv, kr, dk, dv, c_new, n_new, m_new
```
